# Optimizing a Trainium2 kernel written in Bass

```python
import jax, jax.numpy as jnp
from jax import lax
import numpy as np
import math

D_MODEL = 2048
BATCH = 1
SEQ = 256
DEPTH = 2

N_MIXERS = 2
CHUNK = 128
GMLP_EXPAND = 2
GMLP_WIDTH = GMLP_EXPAND * D_MODEL
GMLP_GROUPS = 16
GMLP_GROUP_DIM = GMLP_WIDTH // GMLP_GROUPS
SB_HEAD_DIM = 128
SB_HEADS = D_MODEL // SB_HEAD_DIM
SB_WIDTH = SB_HEADS * SB_HEAD_DIM
Q_BLOCK = 128
N_A = (DEPTH + 1) // 2
N_B = DEPTH // 2
EPS = 1e-6


def rms_norm(x, g):
    xf = x.astype(jnp.float32)
    y = xf * lax.rsqrt(jnp.mean(xf * xf, axis=-1, keepdims=True) + EPS)
    return (y * g.astype(jnp.float32)).astype(x.dtype)

def gmlp_branch(xn, w_in, v_g, w_s, b_s, w_out):
    B, S, _ = xn.shape
    proj = xn @ w_in
    uv = jax.nn.gelu(proj[..., :2 * GMLP_WIDTH])
    zg = proj[..., 2 * GMLP_WIDTH:]
    u, v = jnp.split(uv, 2, axis=-1)
    v = rms_norm(v, v_g)
    vc = v.reshape(B, S // CHUNK, CHUNK, GMLP_GROUPS, GMLP_GROUP_DIM)
    causal = jnp.tril(jnp.ones((CHUNK, CHUNK), dtype=w_s.dtype))
    ws = w_s * causal[None]
    mixed = jnp.einsum('gts,bnsgc->bntgc', ws, vc) + jnp.transpose(b_s)[None, None, :, :, None]
    mixed = mixed.reshape(B, S, GMLP_WIDTH)
    y = u * mixed * jax.nn.silu(zg)
    return y @ w_out

def stick_breaking_attention(q, k, v):
    B, S, H, dh = q.shape
    nb = S // Q_BLOCK
    qh = jnp.transpose(q, (0, 2, 1, 3)) * (dh ** -0.5)
    kh = jnp.transpose(k, (0, 2, 1, 3))
    vh = jnp.transpose(v, (0, 2, 1, 3))
    qb = jnp.transpose(qh.reshape(B, H, nb, Q_BLOCK, dh), (2, 0, 1, 3, 4))
    t0 = jnp.arange(nb, dtype=jnp.int32) * Q_BLOCK
    s_idx = jnp.arange(S, dtype=jnp.int32)[None, :]

    def block(args):
        qblk, start = args
        z = jnp.einsum('bhqd,bhkd->bhqk', qblk, kh).astype(jnp.float32)
        t_idx = start + jnp.arange(Q_BLOCK, dtype=jnp.int32)[:, None]
        mask = s_idx < t_idx
        log_fail = jnp.where(mask, jax.nn.log_sigmoid(-z), 0.0)
        tail = lax.cumsum(log_fail, axis=3, reverse=True) - log_fail
        log_a = jax.nn.log_sigmoid(z) + tail
        a = jnp.where(mask, jnp.exp(log_a), 0.0)
        return jnp.einsum('bhqk,bhkd->bhqd', a.astype(vh.dtype), vh)

    ob = lax.map(block, (qb, t0))
    return jnp.transpose(ob, (1, 0, 3, 2, 4)).reshape(B, S, H, dh)

def stick_breaking_branch(xn, w_in, w_out):
    B, S, _ = xn.shape
    proj = xn @ w_in
    q, k, v, zg = jnp.split(proj, 4, axis=-1)
    shp = (B, S, SB_HEADS, SB_HEAD_DIM)
    o = stick_breaking_attention(q.reshape(shp), k.reshape(shp), v.reshape(shp))
    o = o.reshape(B, S, SB_WIDTH) * jax.nn.silu(zg)
    return o @ w_out

def first_inputs(seed: int = 0) -> dict:
    key = jax.random.key(seed)
    ks = jax.random.split(key, 12)
    f32 = jnp.float32
    x = jax.random.normal(ks[0], (BATCH, SEQ, D_MODEL), f32)
    norm_g = 1.0 + 0.02 * jax.random.normal(ks[1], (DEPTH, D_MODEL), f32)
    a_w_in = jax.random.normal(ks[2], (N_A, D_MODEL, 3 * GMLP_WIDTH), f32) * D_MODEL ** -0.5
    a_v_norm_g = 1.0 + 0.02 * jax.random.normal(ks[3], (N_A, GMLP_WIDTH), f32)
    a_w_s = jax.random.normal(ks[4], (N_A, GMLP_GROUPS, CHUNK, CHUNK), f32) * (0.5 * CHUNK ** -0.5)
    a_b_s = 1.0 + 0.1 * jax.random.normal(ks[5], (N_A, GMLP_GROUPS, CHUNK), f32)
    a_w_out = jax.random.normal(ks[6], (N_A, GMLP_WIDTH, D_MODEL), f32) * GMLP_WIDTH ** -0.5
    b_w_in = jax.random.normal(ks[7], (N_B, D_MODEL, 4 * SB_WIDTH), f32) * D_MODEL ** -0.5
    b_w_out = jax.random.normal(ks[8], (N_B, SB_WIDTH, D_MODEL), f32) * SB_WIDTH ** -0.5
    final_g = 1.0 + 0.02 * jax.random.normal(ks[9], (D_MODEL,), f32)
    return {"x": x, "norm_g": norm_g, "a_w_in": a_w_in, "a_v_norm_g": a_v_norm_g,
            "a_w_s": a_w_s, "a_b_s": a_b_s, "a_w_out": a_w_out,
            "b_w_in": b_w_in, "b_w_out": b_w_out, "final_g": final_g}

def first_block(x, norm_g, a_w_in, a_v_norm_g, a_w_s, a_b_s, a_w_out, b_w_in, b_w_out, final_g):
    h = x
    for i in range(DEPTH):
        hn = rms_norm(h, norm_g[i])
        j = i // N_MIXERS
        if i % N_MIXERS == 0:
            y = gmlp_branch(hn, a_w_in[j], a_v_norm_g[j], a_w_s[j], a_b_s[j], a_w_out[j])
        else:
            y = stick_breaking_branch(hn, b_w_in[j], b_w_out[j])
        h = h + y
    return rms_norm(h, final_g)


DEPTH_2 = 1

CHUNK_2 = 64
D_MIX = D_MODEL
D_CONV = D_MIX // 2
D_MLSTM = D_MIX - D_CONV
CONV_K = 3
M_HEADS = 8
M_HEAD_DIM = D_MLSTM // M_HEADS
D_IN = 3 * D_CONV + 4 * D_MLSTM + 2 * M_HEADS
PEER_HEADS = 8
N_KEYS = 128
N_EXPERTS = N_KEYS * N_KEYS
PEER_TOPK = 16
PEER_QDIM = 256
PEER_HALF = PEER_QDIM // 2
PEER_BLOCK = 128
ALPHA = (2 * DEPTH_2) ** 0.25
BETA = (8 * DEPTH_2) ** -0.25
LN_EPS = 1e-5


def layernorm(x, g, b):
    xf = x.astype(jnp.float32)
    mu = jnp.mean(xf, axis=-1, keepdims=True)
    xc = xf - mu
    var = jnp.mean(xc * xc, axis=-1, keepdims=True)
    y = xc * lax.rsqrt(var + LN_EPS) * g.astype(jnp.float32) + b.astype(jnp.float32)
    return y.astype(x.dtype)

def causal_dwconv(z, w, b):
    S = z.shape[1]
    zp = jnp.pad(z, ((0, 0), (CONV_K - 1, 0), (0, 0)))
    y = b
    for j in range(CONV_K):
        y = y + w[j] * zp[:, j:j + S]
    return y

def mlstm_chunkwise(q, k, v, logi, logf):
    Bn, S, H, dh = q.shape
    L = CHUNK_2
    NC = S // L
    f32 = jnp.float32
    def to_chunks(t):
        return t.astype(f32).reshape(Bn, NC, L, H, dh).transpose(1, 0, 3, 2, 4)
    qc = to_chunks(q)
    kc = to_chunks(k) * (dh ** -0.5)
    vc = to_chunks(v)
    li = logi.astype(f32).reshape(Bn, NC, L, H).transpose(1, 0, 3, 2)
    lf = logf.astype(f32).reshape(Bn, NC, L, H).transpose(1, 0, 3, 2)
    mask = jnp.tril(jnp.ones((L, L), dtype=bool))

    def step(carry, inp):
        C, n, m = carry
        qb, kb, vb, lib, lfb = inp
        bcum = jnp.cumsum(lfb, axis=-1)
        Dm = bcum[..., :, None] - bcum[..., None, :] + lib[..., None, :]
        Dm = jnp.where(mask, Dm, -jnp.inf)
        inter = bcum + m[..., None]
        m_t = jnp.maximum(inter, jnp.max(Dm, axis=-1))
        w_intra = jnp.exp(Dm - m_t[..., None])
        w_inter = jnp.exp(inter - m_t)
        s = jnp.einsum('bhld,bhjd->bhlj', qb, kb) * w_intra
        num = (jnp.einsum('bhlj,bhjd->bhld', s, vb)
               + w_inter[..., None] * jnp.einsum('bhed,bhld->bhle', C, qb))
        den = jnp.sum(s, axis=-1) + w_inter * jnp.einsum('bhd,bhld->bhl', n, qb)
        h = num / jnp.maximum(jnp.abs(den), jnp.exp(-m_t))[..., None]
        bL = bcum[..., -1]
        g = bL[..., None] - bcum + lib
        m_new = jnp.maximum(bL + m, jnp.max(g, axis=-1))
        wk = jnp.exp(g - m_new[..., None])
        decay = jnp.exp(bL + m - m_new)
        C_new = decay[..., None, None] * C + jnp.einsum('bhl,bhle,bhld->bhed', wk, vb, kb)
        n_new = decay[..., None] * n + jnp.einsum('bhl,bhld->bhd', wk, kb)
        return (C_new, n_new, m_new), h

    init = (jnp.zeros((Bn, H, dh, dh), f32), jnp.zeros((Bn, H, dh), f32),
            jnp.zeros((Bn, H), f32))
    _, hs = lax.scan(step, init, (qc, kc, vc, li, lf))
    return hs.transpose(1, 0, 3, 2, 4).reshape(Bn, S, H, dh).astype(q.dtype)

def peer_ffn(h, wq, keys, u, v):
    Bn, S, D = h.shape
    xb = h.reshape(-1, PEER_BLOCK, D)

    def block(xt):
        q = (xt @ wq).reshape(-1, PEER_HEADS, 2, PEER_HALF)
        s = jnp.einsum('thpc,hpnc->thpn', q, keys)
        sv, si = lax.top_k(s, PEER_TOPK)
        cand = (sv[:, :, 0, :, None] + sv[:, :, 1, None, :]).reshape(-1, PEER_HEADS, PEER_TOPK * PEER_TOPK)
        cid = (si[:, :, 0, :, None] * N_KEYS + si[:, :, 1, None, :]).reshape(-1, PEER_HEADS, PEER_TOPK * PEER_TOPK)
        top_s, top_j = lax.top_k(cand, PEER_TOPK)
        eid = jnp.take_along_axis(cid, top_j, axis=-1)
        gate = jax.nn.softmax(top_s.astype(jnp.float32), axis=-1)
        ue = jnp.take(u, eid, axis=0)
        act = jax.nn.gelu(jnp.einsum('thkd,td->thk', ue, xt).astype(jnp.float32), approximate=False)
        ve = jnp.take(v, eid, axis=0)
        return jnp.einsum('thk,thkd->td', (gate * act).astype(xt.dtype), ve)

    return lax.map(block, xb).reshape(Bn, S, D)

def second_inputs(seed: int = 0) -> dict:
    key = jax.random.key(seed)
    ks = jax.random.split(key, 20)
    f32 = jnp.float32
    nrm = lambda k, shape: jax.random.normal(k, shape, f32)
    x = nrm(ks[0], (BATCH, SEQ, D_MODEL))
    ln_in_g = 1.0 + 0.05 * nrm(ks[1], (D_MODEL,))
    ln_in_b = 0.01 * nrm(ks[2], (D_MODEL,))
    col_scale = jnp.concatenate([
        jnp.ones((2 * D_CONV,), f32), jnp.full((D_CONV,), BETA, f32),
        jnp.ones((2 * D_MLSTM,), f32), jnp.full((D_MLSTM,), BETA, f32),
        jnp.ones((D_MLSTM + 2 * M_HEADS,), f32)])
    w_in = nrm(ks[3], (DEPTH_2, D_MODEL, D_IN)) * (D_MODEL ** -0.5) * col_scale
    b_i = 0.1 * nrm(ks[4], (DEPTH_2, M_HEADS))
    b_f = jnp.linspace(3.0, 6.0, M_HEADS, dtype=f32) + 0.1 * nrm(ks[5], (DEPTH_2, M_HEADS))
    b_gate = jnp.concatenate([b_i, b_f], axis=-1)
    conv_w = nrm(ks[6], (DEPTH_2, CONV_K, D_CONV)) * (CONV_K ** -0.5)
    conv_b = 0.01 * nrm(ks[7], (DEPTH_2, D_CONV))
    mh_norm_g = 1.0 + 0.05 * nrm(ks[8], (DEPTH_2, D_MLSTM))
    w_out = nrm(ks[9], (DEPTH_2, D_MIX, D_MODEL)) * (D_MIX ** -0.5) * BETA
    ln1_g = 1.0 + 0.05 * nrm(ks[10], (DEPTH_2, D_MODEL))
    ln1_b = 0.01 * nrm(ks[11], (DEPTH_2, D_MODEL))
    peer_wq = nrm(ks[12], (DEPTH_2, D_MODEL, PEER_HEADS * PEER_QDIM)) * (D_MODEL ** -0.5)
    peer_keys = nrm(ks[13], (DEPTH_2, PEER_HEADS, 2, N_KEYS, PEER_HALF)) * (PEER_HALF ** -0.5)
    peer_u = nrm(ks[14], (DEPTH_2, N_EXPERTS, D_MODEL)) * (D_MODEL ** -0.5) * BETA
    peer_v = nrm(ks[15], (DEPTH_2, N_EXPERTS, D_MODEL)) * (PEER_HEADS ** -0.5) * BETA
    ln2_g = 1.0 + 0.05 * nrm(ks[16], (DEPTH_2, D_MODEL))
    ln2_b = 0.01 * nrm(ks[17], (DEPTH_2, D_MODEL))
    return {"x": x, "ln_in_g": ln_in_g, "ln_in_b": ln_in_b, "w_in": w_in, "b_gate": b_gate,
            "conv_w": conv_w, "conv_b": conv_b, "mh_norm_g": mh_norm_g, "w_out": w_out,
            "ln1_g": ln1_g, "ln1_b": ln1_b, "peer_wq": peer_wq, "peer_keys": peer_keys,
            "peer_u": peer_u, "peer_v": peer_v, "ln2_g": ln2_g, "ln2_b": ln2_b}

def second_block(x, ln_in_g, ln_in_b, w_in, b_gate, conv_w, conv_b, mh_norm_g, w_out,
              ln1_g, ln1_b, peer_wq, peer_keys, peer_u, peer_v, ln2_g, ln2_b):
    Bn, S, D = x.shape
    split_at = np.cumsum([D_CONV, D_CONV, D_CONV, D_MLSTM, D_MLSTM, D_MLSTM, D_MLSTM, M_HEADS]).tolist()
    h = layernorm(x, ln_in_g, ln_in_b)
    for l in range(DEPTH_2):
        proj = h @ w_in[l]
        cB, cC, ch, q, k, v, o, gi, gf = jnp.split(proj, split_at, axis=-1)
        y_conv = cB * causal_dwconv(cC * ch, conv_w[l], conv_b[l])
        gates = (jnp.concatenate([gi, gf], axis=-1) + b_gate[l]).astype(jnp.float32)
        logi = gates[..., :M_HEADS]
        logf = jax.nn.log_sigmoid(gates[..., M_HEADS:])
        hd = lambda t: t.reshape(Bn, S, M_HEADS, M_HEAD_DIM)
        hm = mlstm_chunkwise(hd(q), hd(k), hd(v), logi, logf)
        hm = layernorm(hm, mh_norm_g[l].reshape(M_HEADS, M_HEAD_DIM),
                       jnp.zeros((M_HEADS, M_HEAD_DIM), hm.dtype))
        y_m = jax.nn.sigmoid(o) * hm.reshape(Bn, S, D_MLSTM)
        mix = jnp.concatenate([y_conv, y_m], axis=-1) @ w_out[l]
        h = layernorm(ALPHA * h + mix, ln1_g[l], ln1_b[l])
        ff = peer_ffn(h, peer_wq[l], peer_keys[l], peer_u[l], peer_v[l])
        h = layernorm(ALPHA * h + ff, ln2_g[l], ln2_b[l])
    return h


def setup_inputs(seed=0):
    out = dict(first_inputs(seed))
    for name, value in second_inputs(seed + 1).items():
        if name != "x":
            out[name + "_2"] = value
    return out


def reference(
    x, norm_g, a_w_in, a_v_norm_g, a_w_s, a_b_s, a_w_out, b_w_in, b_w_out, final_g, ln_in_g_2,
    ln_in_b_2, w_in_2, b_gate_2, conv_w_2, conv_b_2, mh_norm_g_2, w_out_2, ln1_g_2, ln1_b_2,
    peer_wq_2, peer_keys_2, peer_u_2, peer_v_2, ln2_g_2, ln2_b_2,
):
    x = first_block(
        x, norm_g, a_w_in, a_v_norm_g, a_w_s, a_b_s, a_w_out, b_w_in, b_w_out, final_g,
    )
    return second_block(
        x, ln_in_g_2, ln_in_b_2, w_in_2, b_gate_2, conv_w_2, conv_b_2, mh_norm_g_2, w_out_2,
        ln1_g_2, ln1_b_2, peer_wq_2, peer_keys_2, peer_u_2, peer_v_2, ln2_g_2, ln2_b_2,
    )


_drawn_inputs = setup_inputs


def setup_inputs(seed=0):
    import zlib

    import numpy as np

    out = dict(_drawn_inputs(seed))
    spreads = {}
    factors = {'norm_g': 2.886,
     'a_v_norm_g': 8.0,
     'ln_in_b_2': 4.647,
     'conv_b_2': 8.0,
     'mh_norm_g_2': 5.156,
     'ln1_b_2': 5.039,
     'ln2_b_2': 5.617}
    for name, (base, spread) in spreads.items():
        noise = np.random.default_rng([zlib.crc32(name.encode()), seed]).standard_normal(out[name].shape)
        drawn = base * np.exp(spread * noise) if base else spread * noise
        out[name] = __import__('jax').numpy.asarray(drawn.astype(out[name].dtype))
    for name, factor in factors.items():
        out[name] = (out[name] * factor).astype(out[name].dtype)
    return out
```

```python
from contextlib import ExitStack

import concourse.bass as bass
from concourse import mybir

F32 = mybir.dt.float32
F32R = mybir.dt.float32r
U32 = mybir.dt.uint32
ALU = mybir.AluOpType
ACT = mybir.ActivationFunctionType
AX_X = mybir.AxisListType.X

P = 128
TOKENS = 256
TILES = TOKENS // P
D = 2048
KT = D // P
COLS = 1024
BANK = 512
GMLP_W = 4096
GROUPS = 16
GROUP_DIM = GMLP_W // GROUPS
HEADS = 16
DH = 128
M_HEADS = 8
D_HALF = 1024
CONV_K = 3
PEER_HEADS = 8
N_KEYS = 128
TOPK = 16
PICKS = PEER_HEADS * TOPK
RMS_EPS = 1e-6
LN_EPS = 1e-5
ALPHA = 2.0 ** 0.25
NEG = -1.0e30
LOWEST = -3.0e38

RAW_SLOTS = 4
SPLIT_SLOTS = 4
AHEAD = SPLIT_SLOTS
GATHER_SLOTS = 8
A, B = 0, 1

UNITS = (
    [("ws", A), ("params", B)]
    + [("xT_gmlp0", A), ("xT_gmlp1", B)]
    + [(f"gmlp_v{i}", i % 2) for i in range(4)]
    + [(f"gmlp_u{i}", i % 2) for i in range(4)]
    + [(f"mix{i}", i % 2) for i in range(4)]
    + [(f"gmlp_z{i}", i % 2) for i in range(4)]
    + [(f"yT_gmlp{i}", i % 2) for i in range(4)]
    + [(f"gmlp_out{i}", i % 2) for i in range(2)]
    + [("xT_att0", A), ("xT_att1", B)]
    + [(f"att_qk{i}", i % 2) for i in range(4)]
    + [(f"qkT{i}", i % 2) for i in range(4)]
    + [(f"att_vz{i}", i % 2) for i in range(4)]
    + [("Z0", A), ("Z1", B), ("L0", A), ("O0", B), ("L1", A), ("Z2", B),
       ("O1", A), ("L2", B), ("Z3", A), ("O2", B), ("L3", A), ("O3", B)]
    + [("yT_att0", A), ("yT_att1", B)]
    + [("att_out0", A), ("att_out1", B)]
    + [("xT_mix0", A), ("xT_mix1", B)]
    + [("mix_q", A), ("mix_k", B), ("gates", A), ("mqT", B), ("mkT", A), ("cum", B)]
    + [("mix_v", A), ("mix_o", B), ("cT", A), ("G_rows", B), ("G_cols", A)]
    + [("mix_cC", A), ("mix_ch", B), ("MS0", A), ("MS1", B), ("mix_cB", A), ("MO0", B), ("MO1", A)]
    + [("zT", B), ("cBT", A), ("ymT", B)]
    + [("mix_out0", A), ("mix_out1", B)]
    + [("xT_peer0", A), ("xT_peer1", B), ("peer_q0", A), ("peer_q1", B)]
    + [("pqT0", A), ("pqT1", B), ("keysT", A), ("scores0", B), ("scores1", A)]
)
PROJECTIONS = ("gmlp_v", "gmlp_u", "gmlp_z", "gmlp_out", "att_qk", "att_vz", "att_out", "mix_q", "mix_k", "mix_v",
               "mix_o", "mix_cC", "mix_ch", "mix_cB", "mix_out", "peer_q")

STREAM = [("gmlp_v", 4, KT), ("gmlp_u", 4, KT), ("gmlp_z", 4, KT), ("gmlp_out", 2, 2 * KT), ("att_qk", 4, KT),
          ("att_vz", 4, KT), ("att_out", 2, KT), ("mix_qk", 2, KT), ("mix_vo", 2, KT), ("mix_cc", 2, KT),
          ("mix_cB", 1, KT), ("mix_out", 2, KT), ("peer_q", 2, KT)]


def number_units():
    used, filled, nth, fill = [0, 0], [0, 0], {}, {}
    for name, half in UNITS:
        nth[name] = (half, used[half])
        used[half] += 1
        if not name.rstrip("0123456789").startswith(PROJECTIONS) or name.startswith("mix") and name[3:].isdigit():
            filled[half] += 1
            fill[name] = filled[half]
    return nth, fill


def number_chunks():
    first, at = {}, 0
    for name, blocks, kts in STREAM:
        first[name] = at
        at += blocks * kts
    return first, at


def build(nc, x, norm_g, a_w_in, a_v_norm_g, a_w_s, a_b_s, a_w_out, b_w_in, b_w_out, final_g, ln_in_g_2, ln_in_b_2,
          w_in_2, b_gate_2, conv_w_2, conv_b_2, mh_norm_g_2, w_out_2, ln1_g_2, ln1_b_2, peer_wq_2, peer_keys_2,
          peer_u_2, peer_v_2, ln2_g_2, ln2_b_2, out):
    NTH, FILL = number_units()
    FIRST, CHUNKS = number_chunks()

    ctx = ExitStack()
    with ctx:
        at = [(nc.sbuf_base + 31) // 32 * 32]

        def region(size):
            start = at[0]
            at[0] += (size + 31) // 32 * 32
            assert at[0] <= nc.sbuf_usable_end, at[0]
            return start

        def sb(name, shape, dt, offset):
            return nc.alloc_sbuf_tensor_at(name, shape, dt, offset=offset)

        KB = 1024
        T1 = region(32 * KB)
        T2 = region(32 * KB)
        SPLIT = region(32 * KB)
        RAW = region(16 * KB)
        H = region(16 * KB)
        ROWS = region(24 * KB)
        SCR = region(48 * KB + 512)
        CONST = region(6 * 512)
        SMALL = region(3 * KB)

        xT1 = sb("xT1", [P, 2, KT, TOKENS], F32R, T1)
        xT2 = sb("xT2", [P, 2, KT, TOKENS], F32R, T2)
        w_split = sb("w_split", [P, SPLIT_SLOTS, 2, COLS], F32R, SPLIT)
        w_raw = sb("w_raw", [P, RAW_SLOTS, COLS], F32, RAW)
        h = sb("h", [P, TILES, D], F32, H)

        ident = sb("ident", [P, P], F32, CONST)
        upto = sb("upto", [P, P], F32, CONST + 512)
        onward = sb("onward", [P, P], F32, CONST + 1024)
        before = sb("before", [P, P], F32, CONST + 1536)
        barred = sb("barred", [P, P], F32, CONST + 2048)
        ones = sb("ones", [P, 2 * P], F32, SMALL)
        iota16 = sb("iota16", [P, TOPK], F32, CONST + 2560)
        cols = sb("cols", [P, 48], F32, CONST + 2560 + 64)
        small = [SMALL + 1024]

        def tiny(name, shape, dt=F32):
            n = 4
            for s in shape[1:]:
                n *= s
            o = small[0]
            small[0] += (n + 31) // 32 * 32
            assert small[0] <= SMALL + 3 * KB
            return sb(name, shape, dt, o)

        sumsq = tiny("sumsq", [P, TILES])
        sumsq_v = tiny("sumsq_v", [P, TILES, 2])
        sums = tiny("sums", [P, TILES])
        mean = tiny("mean", [P, TILES])
        mean_neg = tiny("mean_neg", [P, TILES])
        meansq = tiny("meansq", [P, TILES])
        root = tiny("root", [P, TILES])
        rstd = tiny("rstd", [P, TILES])
        param_rows = sb("param_rows", [48, P], F32, SCR + 40 * KB)

        ws_raw = sb("ws_raw", [P, GROUPS, P], F32, T2)
        wsT = sb("wsT", [P, GROUPS, P], F32, SCR + 32 * KB)
        xn = sb("xn", [P, TILES, D], F32, SCR)
        gv = sb("gv", [P, TILES, GMLP_W], F32, T2)
        gu = sb("gu", [P, TILES, GMLP_W], F32, SCR)
        gz = sb("gz", [P, TILES, COLS], F32, SCR + 40 * KB)
        row_norm = sb("row_norm", [P, D], F32, ROWS)
        row_v = sb("row_v", [P, GMLP_W], F32, ROWS + 8 * KB)

        qk_tok = sb("qk_tok", [P, 2, TILES, D], F32, T2)
        qkT = sb("qkT", [P, 2, HEADS, TOKENS], F32, SCR)
        av = sb("av", [P, TILES, D], F32, SCR + 32 * KB)
        az = sb("az", [P, TILES, D], F32, T2)
        ZW = 3 * P
        zs = sb("zs", [P, 2, 4, ZW], F32, ROWS)
        sp_ = sb("softplus", [P, 2, 4, ZW], F32, ROWS + 12 * KB)

        row_a = sb("row_a", [P, D], F32, ROWS)
        row_b = sb("row_b", [P, D], F32, ROWS + 8 * KB)
        row_c = sb("row_c", [P, D], F32, ROWS + 16 * KB)
        mqk_tok = sb("mqk_tok", [P, 2, TILES, D_HALF], F32, T2)
        mw = sb("mw", [P, M_HEADS, ZW], F32, T2 + 16 * KB)
        mqkT = sb("mqkT", [P, 2, M_HEADS, TOKENS], F32, SCR)
        mv = sb("mv", [P, TILES, M_HEADS, DH + 1], F32, SCR + 16 * KB + 128)
        mo = sb("mo", [P, TILES, D_HALF], F32, SCR + 24 * KB + 256)
        cB = sb("cB", [P, TILES, D_HALF], F32, SCR + 32 * KB + 256)
        cz = sb("cz", [P, TILES, D_HALF], F32, SCR + 40 * KB + 256)
        trash = sb("trash", [P, D], F32, SCR)
        row_mh = sb("row_mh", [P, D_HALF], F32, ROWS)
        hm = sb("hm", [P, TILES, M_HEADS, DH], F32, ROWS + 4 * KB)
        ms = sb("ms", [P, 2, 4, ZW], F32, ROWS + 12 * KB)
        zT = sb("zT", [P, M_HEADS, TOKENS + 2], F32, SCR)
        cBT = sb("cBT", [P, M_HEADS, TOKENS], F32, SCR + 8256)
        yc = sb("yc", [P, M_HEADS, TOKENS], F32, SCR + 16 * KB + 128)
        hsq = sb("hsq", [P, TILES, M_HEADS, DH], F32, T2)
        wg_raw = sb("wg_raw", [P, KT, 16], F32, T2 + 28 * KB)
        wg_split = sb("wg_split", [P, 2, KT, 16], F32R, T2 + 29 * KB)
        row_gate = tiny("row_gate", [P, 16])
        gates = tiny("gates", [P, TILES, 16])
        gabs = tiny("gabs", [P, TILES, M_HEADS])
        logf = tiny("logf", [P, TILES, M_HEADS])
        Bc = tiny("Bc", [P, TILES, M_HEADS])
        cc = tiny("cc", [P, TILES, M_HEADS])
        cmin = tiny("cmin", [P, TILES, M_HEADS])
        G = sb("G", [M_HEADS, TOKENS], F32, T2 + 31 * KB)
        c_rows = sb("c_rows", [M_HEADS, TOKENS], F32, T2 + 28 * KB)
        mden = tiny("mden", [P, 4, TILES])
        mmu = tiny("mmu", [P, TILES, M_HEADS])
        mrs = tiny("mrs", [P, TILES, M_HEADS])

        pq_tok = sb("pq_tok", [P, TILES, D], F32, SCR)
        pqT = sb("pqT", [P, 2 * PEER_HEADS, TOKENS], F32, SCR + 16 * KB)
        keysT = sb("keysT", [P, 2 * PEER_HEADS, P], F32, SCR + 32 * KB)
        keys_raw = sb("keys_raw", [P, 2 * PEER_HEADS, P], F32, SCR + 40 * KB)
        scores = sb("scores", [P, TILES, 2 * PEER_HEADS, N_KEYS], F32, ROWS)
        left = sb("left", [P, 2 * PEER_HEADS, N_KEYS], F32, SCR)
        cand = sb("cand", [P, PEER_HEADS, TOPK * TOPK], F32, SCR + 8 * KB)
        cand_left = sb("cand_left", [P, PEER_HEADS, TOPK * TOPK], F32, SCR + 16 * KB)
        onehot = sb("onehot", [P, PICKS, TOPK], F32, SCR + 24 * KB)
        vacc = sb("vacc", [P, 2, D], F32, RAW)
        row_g2 = sb("row_g2", [P, D], F32, SPLIT)
        row_b2 = sb("row_b2", [P, D], F32, SPLIT + 8 * KB)
        pk = [SPLIT + 16 * KB]

        def pick(name, shape, dt=F32):
            n = 4
            for s in shape[1:]:
                n *= s
            o = pk[0]
            pk[0] += (n + 31) // 32 * 32
            assert pk[0] <= SPLIT + 32 * KB
            return sb(name, shape, dt, o)

        sv = pick("sv", [P, 2 * PEER_HEADS, TOPK])
        si = pick("si", [P, 2 * PEER_HEADS, TOPK], U32)
        sif = pick("sif", [P, 2 * PEER_HEADS, TOPK])
        tops = pick("tops", [P, PEER_HEADS, TOPK])
        topj = pick("topj", [P, PEER_HEADS, TOPK], U32)
        topa = pick("topa", [P, PEER_HEADS, TOPK], U32)
        topaf = pick("topaf", [P, PEER_HEADS, TOPK])
        rowid = pick("rowid", [P, 2, PICKS])
        eid = pick("eid", [P, TILES * PICKS + 2 * GATHER_SLOTS], U32)
        idx = pick("idx", [P, 2, GATHER_SLOTS], U32)
        gate = pick("gate", [P, TILES, PEER_HEADS, TOPK])
        gsum = pick("gsum", [P, PEER_HEADS])
        dots = pick("dots", [P, 2, GATHER_SLOTS])
        act_ = pick("act_", [P, TILES * PICKS])
        wgt = pick("wgt", [P, TILES * PICKS])
        ring = sb("ring", [P, GATHER_SLOTS, D], F32, T1)

        ps = [ctx.enter_context(nc.psum_tensor(f"half{n}", [P, 4, BANK], F32)) for n in range(2)]
        flat = [t[:, :, :].rearrange("p b n -> p (b n)") for t in ps]
        by_tile = [t[:, :, :].rearrange("p (t b) n -> p t (b n)", t=TILES) for t in ps]
        by_128 = [f.rearrange("p (k t) -> p k t", t=P) for f in flat]

        def sem(name):
            return ctx.enter_context(nc.semaphore(name))

        half_filled = [sem("half_filled_a"), sem("half_filled_b")]
        half_free = [sem("half_free_a"), sem("half_free_b")]
        raw_landed = [sem(f"raw_landed{n}") for n in range(RAW_SLOTS)]
        hi_done = sem("hi_done")
        split_done = sem("split_done")
        products = sem("products")
        dve_step = sem("dve_step")
        act_step = sem("act_step")
        pool_step = sem("pool_step")
        consts_done = sem("consts_done")
        xT_hi = sem("xT_hi")
        loaded = {n: sem("loaded_" + n) for n in (
            "x", "ws", "params", "row_norm", "row_v", "row_norm1", "rows_mix", "wg", "gate", "mh", "rows_ln1", "keys",
            "rows_ln2")}
        dve_mean = sem("dve_mean")
        v_squared = sem("v_squared")
        mv_ones = sem("mv_ones")
        mw_masked = sem("mw_masked")
        zT_pad = sem("zT_pad")
        stat = sem("stat")
        rooted = sem("rooted")
        meaned = sem("meaned")
        summed = sem("summed")
        squared = sem("squared")
        normed = sem("normed")
        v_normed = sem("v_normed")
        z_used = sem("z_used")
        zs_done = sem("zs_done")
        abs_done = sem("abs_done")
        ln_done = sem("ln_done")
        sp_done = sem("sp_done")
        la_done = sem("la_done")
        a_done = sem("a_done")
        wg_hi = sem("wg_hi")
        wg_done = sem("wg_done")
        gate_abs = sem("gate_abs")
        gate_ln = sem("gate_ln")
        logf_done = sem("logf_done")
        cc_done = sem("cc_done")
        G_done = sem("G_done")
        mw_done = sem("mw_done")
        m_exp = sem("m_exp")
        hm_sq = sem("hm_sq")
        hm_root = sem("hm_root")
        ym_done = sem("ym_done")
        yc_done = sem("yc_done")
        yc_hi = sem("yc_hi")
        yc_lo = sem("yc_lo")
        gate_sub = sem("gate_sub")
        gate_exp = sem("gate_exp")
        idx_ready = [sem("idx_ready0"), sem("idx_ready1")]
        row_landed = [sem(f"row_landed{n}") for n in range(GATHER_SLOTS)]
        rows_used = sem("rows_used")
        gelu_done = sem("gelu_done")
        y_stored = sem("y_stored")
        out_ready = sem("out_ready")

        block = ctx.enter_context(nc.Block())

        def is_free(eng, unit):
            half, n = NTH[unit]
            if n:
                eng.wait_ge(half_free[half], n)

        def is_filled(eng, unit):
            eng.wait_ge(half_filled[NTH[unit][0]], FILL[unit])

        def is_emptied(eng, unit):
            half, n = NTH[unit]
            eng.wait_ge(half_free[half], n + 1)

        def halves(unit):
            return NTH[unit][0]

        def step_counter(eng, s):
            count = [0]

            def step(ins):
                count[0] += 1
                ins.then_inc(s, 1)
                eng.wait_ge(s, count[0])
            return step

        @block.sync
        def _(sp):
            for t in range(TILES):
                sp.dma_start(h[:, t, :], x[0, t * P:(t + 1) * P, :]).then_inc(loaded["x"], 16)

            def load_block(w, c, col, kts=KT):
                for k in range(kts):
                    if not (isinstance(c, int) and c + k < RAW_SLOTS):
                        sp.wait_ge(split_done, c + (k + 1 - RAW_SLOTS))
                    sp.dma_start(w_raw[:, k % RAW_SLOTS, :], w[k * P:(k + 1) * P, bass.ds(col, COLS)])\
                        .then_inc(raw_landed[k % RAW_SLOTS], 16)

            def load_pairs(w, stage, col, pairs):
                c = FIRST[stage]
                with sp.Fori(0, pairs) as i:
                    for n in range(2):
                        load_block(w, i * (2 * KT) + (c + n * KT), i * (2 * COLS) + (col + n * COLS))

            for n in range(4):
                load_block(a_w_in[0], FIRST["gmlp_v"] + n * KT, GMLP_W + n * COLS)
            load_pairs(a_w_in[0], "gmlp_u", 0, 2)
            load_pairs(a_w_in[0], "gmlp_z", 2 * GMLP_W, 2)
            for n in range(2):
                load_block(a_w_out[0], FIRST["gmlp_out"] + n * 2 * KT, n * COLS, 2 * KT)
            load_pairs(b_w_in[0], "att_qk", 0, 2)
            load_pairs(b_w_in[0], "att_vz", 2 * D, 2)
            for n in range(2):
                load_block(b_w_out[0], FIRST["att_out"] + n * KT, n * COLS)
            for stage, blocks in (("mix_qk", (3, 4)), ("mix_vo", (5, 6)), ("mix_cc", (1, 2)), ("mix_cB", (0,))):
                for n, b in enumerate(blocks):
                    load_block(w_in_2[0], FIRST[stage] + n * KT, b * COLS)
            for n in range(2):
                load_block(w_out_2[0], FIRST["mix_out"] + n * KT, n * COLS)
            for n in range(2):
                load_block(peer_wq_2[0], FIRST["peer_q"] + n * KT, n * COLS)
            for t in range(TILES):
                sp.wait_ge(out_ready, t + 1)
                sp.dma_start(out[0, t * P:(t + 1) * P, :], h[:, t, :]).then_inc(y_stored, 16)
            sp.wait_ge(y_stored, 16 * TILES)

        @block.gpsimd
        def _(pool):
            step = step_counter(pool, pool_step)

            def row(dst, src, name):
                pool.dma_start(dst, src.partition_broadcast(P)).then_inc(loaded[name], 16)

            pool.dma_start(param_rows[0:16, :], a_b_s[0]).then_inc(loaded["params"], 16)
            pool.dma_start(param_rows[16:40, :], conv_w_2[0].rearrange("j (f p) -> (j f) p", p=P))\
                .then_inc(loaded["params"], 16)
            pool.dma_start(param_rows[40:48, :], conv_b_2[0].rearrange("(f p) -> f p", p=P))\
                .then_inc(loaded["params"], 16)
            pool.dma_start(ws_raw[:, :, :], a_w_s[0].rearrange("g t s -> t g s")).then_inc(loaded["ws"], 16)
            row(row_norm[:, :], norm_g[0], "row_norm")
            row(row_v[:, :], a_v_norm_g[0], "row_v")
            row(row_gate[:, :], b_gate_2[0], "gate")

            def triangle(m, base, fill, op, cm, st):
                step(nc.gpsimd.memset(m[:, :], base))
                step(nc.gpsimd.affine_select(out=m[:, :], in_=m[:, :], compare_op=op, fill=fill, base=0,
                                             pattern=[[st, P]], channel_multiplier=cm))
            triangle(ident, 0.0, 1.0, ALU.not_equal, 1, -1)
            triangle(upto, 1.0, 0.0, ALU.is_ge, -1, 1)
            triangle(onward, 1.0, 0.0, ALU.is_ge, 1, -1)
            triangle(before, 1.0, 0.0, ALU.is_gt, -1, 1)
            triangle(barred, 0.0, NEG, ALU.is_gt, -1, 1)
            step(nc.gpsimd.memset(ones[:, :], 1.0))
            nc.gpsimd.iota(iota16[:, :], pattern=[[1, TOPK]], base=0, channel_multiplier=0,
                           allow_small_or_imprecise_dtypes=True).then_inc(consts_done, 1)

            pool.wait_ge(normed, TILES)
            row(row_norm[:, :], norm_g[1], "row_norm1")
            is_emptied(pool, "O3")
            row(row_a[:, :], final_g, "rows_mix")
            row(row_b[:, :], ln_in_g_2, "rows_mix")
            row(row_c[:, :], ln_in_b_2, "rows_mix")
            is_emptied(pool, "yT_att1")
            pool.dma_start(wg_raw[:, :, :], w_in_2[0, :, 7 * D_HALF:].rearrange("(k p) n -> p k n", p=P))\
                .then_inc(loaded["wg"], 16)
            pool.wait_ge(normed, 3 * TILES)
            row(row_mh[:, :], mh_norm_g_2[0], "mh")
            is_emptied(pool, "ymT")
            row(row_a[:, :], ln1_g_2[0], "rows_ln1")
            row(row_b[:, :], ln1_b_2[0], "rows_ln1")
            pool.dma_start(keys_raw[:, :, :], peer_keys_2[0].rearrange("h s n c -> n (h s) c"))\
                .then_inc(loaded["keys"], 16)
            is_emptied(pool, "peer_q1")
            row(row_g2[:, :], ln2_g_2[0], "rows_ln2")
            row(row_b2[:, :], ln2_b_2[0], "rows_ln2")

            for table, base in ((peer_u_2[0], 0), (peer_v_2[0], TILES * PICKS)):
                with pool.Fori(0, TILES * PICKS // (2 * GATHER_SLOTS)) as i:
                    for n in range(2 * GATHER_SLOTS):
                        b, s = divmod(n, GATHER_SLOTS)
                        if s == 0:
                            pool.wait_ge(idx_ready[b], i + (base // (2 * GATHER_SLOTS) + 1))
                        pool.wait_ge(rows_used, i * (2 * GATHER_SLOTS) + (base + n + 1))
                        pool.nop(nofuse=True)
                        nc.gpsimd.indirect_dma_start(
                            out=ring[:, s, :], out_offset=None, in_=table,
                            in_offset=bass.IndirectOffsetOnAxis(ap=idx[:, b, s:s + 1], axis=0),
                        ).then_inc(row_landed[s], 16)

        @block.tensor
        def _(pe):
            mm = nc.tensor.matmul

            def multiply(half, c, xts=(xT1,)):
                kts = KT * len(xts)
                for k in range(kts):
                    pe.wait_ge(split_done, c + (k + 1))
                    xt, kk, s = xts[k // KT], k % KT, k % SPLIT_SLOTS
                    for t in range(TILES):
                        tok = slice(t * P, (t + 1) * P)
                        for xp, wp in ((0, 0), (0, 1), (1, 0)):
                            for n in range(2):
                                last = mm(ps[half][:, 2 * t + n, :], xt[:, xp, kk, tok],
                                          w_split[:, s, wp, n * BANK:(n + 1) * BANK],
                                          start=(k == 0 and xp == 0 and wp == 0), stop=(k == kts - 1 and xp == 1))
                    last.then_inc(products, 1)

            def pairs(stage, count):
                c = FIRST[stage]
                with pe.Fori(0, count) as i:
                    for n in range(2):
                        pe.wait_ge(half_free[n], i + NTH[f"{stage}{n}"][1])
                        multiply(n, i * (2 * KT) + (c + n * KT))

            def one(unit, c, xts=(xT1,)):
                is_free(pe, unit)
                multiply(halves(unit), c, xts)

            def turn(unit, tiles):
                is_free(pe, unit)
                hf = halves(unit)
                for n, (src, rows) in enumerate(tiles):
                    last = nc.tensor.transpose(by_128[hf][:, n, 0:rows], src, ident[0:rows, 0:rows])
                last.then_inc(half_filled[hf], 1)

            def turn_x(names, src, count):
                for t in range(TILES):
                    pe.wait_ge(normed, count + t + 1)
                    turn(names[t], [(src[:, t, k * P:(k + 1) * P], P) for k in range(KT)])
                for t in range(TILES):
                    is_emptied(pe, names[t])

            pe.wait_ge(consts_done, 1)
            pe.wait_ge(loaded["ws"], 16)
            turn("ws", [(ws_raw[:, g, :], P) for g in range(GROUPS)])
            pe.wait_ge(loaded["params"], 48)
            turn("params", [(param_rows[:, :], 48)])

            turn_x(("xT_gmlp0", "xT_gmlp1"), xn, 0)
            pairs("gmlp_v", 2)
            pairs("gmlp_u", 2)
            pe.wait_ge(v_normed, TILES)
            for u in range(4):
                unit = f"mix{u}"
                is_free(pe, unit)
                hf = halves(unit)
                for j in range(4):
                    g = 4 * u + j
                    for n in range(TILES):
                        last = mm(ps[hf][:, j, n * GROUP_DIM:(n + 1) * GROUP_DIM], wsT[:, g, :],
                                  gv[:, n, g * GROUP_DIM:(g + 1) * GROUP_DIM], start=True, stop=True)
                last.then_inc(half_filled[hf], 1)
            pairs("gmlp_z", 2)
            pe.wait_ge(z_used, 1 + 4)
            for u in range(4):
                src = [(gu[:, u % 2, (16 * (u // 2) + k) * P:(16 * (u // 2) + k + 1) * P], P) for k in range(KT)]
                turn(f"yT_gmlp{u}", src)
            for u in range(4):
                is_emptied(pe, f"yT_gmlp{u}")
            for n in range(2):
                one(f"gmlp_out{n}", FIRST["gmlp_out"] + n * 2 * KT, (xT1, xT2))

            turn_x(("xT_att0", "xT_att1"), xn, TILES)
            pairs("att_qk", 2)
            for u in range(4):
                w, t = divmod(u, 2)
                is_emptied(pe, f"att_qk{2 * w + 1}")
                is_emptied(pe, f"att_qk{2 * w}")
                turn(f"qkT{u}", [(qk_tok[:, w, t, n * P:(n + 1) * P], P) for n in range(HEADS)])
            pairs("att_vz", 2)

            def att_z(g):
                unit = f"Z{g}"
                is_free(pe, unit)
                hf = halves(unit)
                if g == 0:
                    for u in range(4):
                        is_emptied(pe, f"qkT{u}")
                for j in range(4):
                    n = 4 * g + j
                    mm(ps[hf][:, j, 0:TOKENS], qkT[:, 1, n, 0:P], qkT[:, 0, n, :], start=True, stop=True)
                    last = mm(ps[hf][:, j, TOKENS:ZW], qkT[:, 1, n, P:TOKENS], qkT[:, 0, n, P:TOKENS],
                              start=True, stop=True)
                last.then_inc(half_filled[hf], 1)

            def att_l(g):
                unit = f"L{g}"
                is_free(pe, unit)
                pe.wait_ge(sp_done, g + 1)
                hf = halves(unit)
                for j in range(4):
                    s = sp_[:, g % 2, j, :]
                    mm(ps[hf][:, j, 0:TOKENS], onward[:, :], s[:, 0:TOKENS], start=True, stop=False)
                    mm(ps[hf][:, j, P:TOKENS], ones[:, 0:P], s[:, TOKENS:ZW], start=False, stop=True)
                    last = mm(ps[hf][:, j, TOKENS:ZW], onward[:, :], s[:, TOKENS:ZW], start=True, stop=True)
                last.then_inc(half_filled[hf], 1)

            def att_o(g):
                unit = f"O{g}"
                is_free(pe, unit)
                pe.wait_ge(a_done, g + 1)
                hf = halves(unit)
                for j in range(4):
                    a = zs[:, g % 2, j, :]
                    c = (4 * g + j) * DH
                    mm(ps[hf][:, j, 0:DH], a[:, 0:P], av[:, 0, c:c + DH], start=True, stop=True)
                    mm(ps[hf][:, j, DH:2 * DH], a[:, P:TOKENS], av[:, 0, c:c + DH], start=True, stop=False)
                    last = mm(ps[hf][:, j, DH:2 * DH], a[:, TOKENS:ZW], av[:, 1, c:c + DH], start=False, stop=True)
                last.then_inc(half_filled[hf], 1)

            for u in range(4):
                is_emptied(pe, f"att_vz{u}")
            for name, g in (("Z", 0), ("Z", 1), ("L", 0), ("O", 0), ("L", 1), ("Z", 2), ("O", 1), ("L", 2), ("Z", 3),
                            ("O", 2), ("L", 3), ("O", 3)):
                {"Z": att_z, "L": att_l, "O": att_o}[name](g)
            is_emptied(pe, "O2")
            is_emptied(pe, "O3")
            for t in range(TILES):
                turn(f"yT_att{t}", [(az[:, t, k * P:(k + 1) * P], P) for k in range(KT)])
            for t in range(TILES):
                is_emptied(pe, f"yT_att{t}")
            for n in range(2):
                one(f"att_out{n}", FIRST["att_out"] + n * KT)

            turn_x(("xT_mix0", "xT_mix1"), h, 2 * TILES)
            for n, unit in enumerate(("mix_q", "mix_k")):
                one(unit, FIRST["mix_qk"] + n * KT)
            is_free(pe, "gates")
            pe.wait_ge(wg_done, 1)
            hf = halves("gates")
            for t in range(TILES):
                for k in range(KT):
                    for xp, wp in ((0, 0), (0, 1), (1, 0)):
                        last = mm(ps[hf][:, t, 0:16], xT1[:, xp, k, t * P:(t + 1) * P], wg_split[:, wp, k, :],
                                  start=(k == 0 and xp + wp == 0), stop=(k == KT - 1 and xp == 1))
            last.then_inc(half_filled[hf], 1)
            for w, unit in enumerate(("mqT", "mkT")):
                is_emptied(pe, ("mix_q", "mix_k")[w])
                turn(unit, [(mqk_tok[:, w, t, n * P:(n + 1) * P], P) for n in range(M_HEADS) for t in range(TILES)])
            is_free(pe, "cum")
            pe.wait_ge(logf_done, 1)
            hf = halves("cum")
            mm(ps[hf][:, 0, 0:M_HEADS], upto[:, :], logf[:, 0, :], start=True, stop=True)
            mm(ps[hf][:, 1, 0:M_HEADS], upto[:, :], logf[:, 1, :], start=True, stop=False)
            mm(ps[hf][:, 1, 0:M_HEADS], ones[:, 0:P], logf[:, 0, :], start=False, stop=True)\
                .then_inc(half_filled[hf], 1)
            for n, unit in enumerate(("mix_v", "mix_o")):
                one(unit, FIRST["mix_vo"] + n * KT)
            is_free(pe, "cT")
            pe.wait_ge(cc_done, 1)
            hf = halves("cT")
            for t in range(TILES):
                last = nc.tensor.transpose(ps[hf][0:M_HEADS, 0, t * P:(t + 1) * P], cc[:, t, :], ident[:, :])
            last.then_inc(half_filled[hf], 1)
            is_free(pe, "G_rows")
            pe.wait_ge(G_done, 1)
            hf = halves("G_rows")
            for n in range(M_HEADS):
                last = mm(flat[hf][:, n * TOKENS:(n + 1) * TOKENS], ident[0:M_HEADS, n:n + 1].to_broadcast([M_HEADS, P]),
                          G[:, :], start=True, stop=True)
            last.then_inc(half_filled[hf], 1)
            is_free(pe, "G_cols")
            hf = halves("G_cols")
            for t in range(TILES):
                last = nc.tensor.transpose(ps[hf][:, t, 0:M_HEADS], G[:, t * P:(t + 1) * P],
                                           ident[0:M_HEADS, 0:M_HEADS])
            last.then_inc(half_filled[hf], 1)
            for n, unit in enumerate(("mix_cC", "mix_ch")):
                one(unit, FIRST["mix_cc"] + n * KT)
            is_emptied(pe, "mqT")
            is_emptied(pe, "mkT")
            for g in range(2):
                unit = f"MS{g}"
                is_free(pe, unit)
                hf = halves(unit)
                for j in range(4):
                    n = 4 * g + j
                    mm(ps[hf][:, j, 0:TOKENS], mqkT[:, 1, n, 0:P], mqkT[:, 0, n, :], start=True, stop=True)
                    last = mm(ps[hf][:, j, TOKENS:ZW], mqkT[:, 1, n, P:TOKENS], mqkT[:, 0, n, P:TOKENS],
                              start=True, stop=True)
                last.then_inc(half_filled[hf], 1)
            one("mix_cB", FIRST["mix_cB"])
            is_emptied(pe, "mix_v")
            for g in range(2):
                unit = f"MO{g}"
                is_free(pe, unit)
                is_emptied(pe, f"MS{g}")
                hf = halves(unit)
                for j in range(4):
                    n, a = 4 * g + j, ms[:, g, j, :]
                    E = DH + 1
                    mm(ps[hf][:, j, 0:E], a[:, 0:P], mv[:, 0, n, :], start=True, stop=True)
                    mm(ps[hf][:, j, E:2 * E], a[:, P:TOKENS], mv[:, 0, n, :], start=True, stop=False)
                    last = mm(ps[hf][:, j, E:2 * E], a[:, TOKENS:ZW], mv[:, 1, n, :], start=False, stop=True)
                last.then_inc(half_filled[hf], 1)
            is_emptied(pe, "mix_ch")
            turn("zT", [(cz[:, t, n * P:(n + 1) * P], P) for n in range(M_HEADS) for t in range(TILES)])
            is_emptied(pe, "mix_cB")
            turn("cBT", [(cB[:, t, n * P:(n + 1) * P], P) for n in range(M_HEADS) for t in range(TILES)])
            pe.wait_ge(ym_done, 1)
            ym = hm[:, :, :, :].rearrange("p t n d -> p t (n d)")
            turn("ymT", [(ym[:, t, n * P:(n + 1) * P], P) for n in range(M_HEADS) for t in range(TILES)])
            pe.wait_ge(yc_lo, 1)
            is_emptied(pe, "ymT")
            for n in range(2):
                one(f"mix_out{n}", FIRST["mix_out"] + n * KT, (xT2,))

            turn_x(("xT_peer0", "xT_peer1"), h, 3 * TILES)
            for n in range(2):
                one(f"peer_q{n}", FIRST["peer_q"] + n * KT)
            for u in range(2):
                is_emptied(pe, f"peer_q{u}")
                turn(f"pqT{u}", [(pq_tok[:, t, (8 * u + n) * P:(8 * u + n + 1) * P], P)
                                 for n in range(8) for t in range(TILES)])
            pe.wait_ge(loaded["keys"], 16)
            turn("keysT", [(keys_raw[:, n, :], P) for n in range(2 * PEER_HEADS)])
            for unit in ("pqT0", "pqT1", "keysT"):
                is_emptied(pe, unit)
            for t in range(TILES):
                unit = f"scores{t}"
                is_free(pe, unit)
                hf = halves(unit)
                for n in range(2 * PEER_HEADS):
                    last = mm(by_128[hf][:, n, :], pqT[:, n, t * P:(t + 1) * P], keysT[:, n, :], start=True, stop=True)
                last.then_inc(half_filled[hf], 1)

        @block.scalar
        def _(act):
            fn = nc.scalar.activation
            step = step_counter(act, act_step)

            def round_hi(c, ks):
                for k in ks:
                    s = k % SPLIT_SLOTS
                    act.wait_ge(raw_landed[k % RAW_SLOTS], c * (16 // RAW_SLOTS) + 16 * (k // RAW_SLOTS + 1))
                    if not (isinstance(c, int) and c + k < SPLIT_SLOTS):
                        act.wait_ge(products, c + (k + 1 - SPLIT_SLOTS))
                    fn(w_split[:, s, 0, :], w_raw[:, k % RAW_SLOTS, :], ACT.Copy).then_inc(hi_done, 1)

            def through(c, kts, last=False):
                round_hi(c, range(AHEAD, kts))
                if not last:
                    round_hi(c + kts, range(AHEAD))

            def block_done(c, kts=KT):
                act.wait_ge(products, c + kts)

            def pairs(stage, count, empty):
                c = FIRST[stage]
                with act.Fori(0, count) as i:
                    for n in range(2):
                        cb = i * (2 * KT) + (c + n * KT)
                        through(cb, KT)
                        block_done(cb)
                        empty(i, n)

            def hi_x(unit, dst):
                is_filled(act, unit)
                fn(dst, by_128[halves(unit)], ACT.Copy).then_inc(xT_hi, 1)

            def take(unit, dst, src, func=ACT.Copy, **kw):
                fn(dst, src, func, **kw).then_inc(half_free[halves(unit)], 1)

            def root_of(n):
                act.wait_ge(stat, n)
                fn(root[:, :], meansq[:, :], ACT.Sqrt).then_inc(rooted, 1)

            round_hi(0, range(AHEAD))
            root_of(1)
            for t in range(TILES):
                hi_x(f"xT_gmlp{t}", xT1[:, 0, :, t * P:(t + 1) * P])

            def gelu_to(dst):
                def empty(i, n):
                    take(("gmlp_v0", "gmlp_v1")[n], dst[:, :, bass.ds(i * (2 * COLS) + n * COLS, COLS)], by_tile[n],
                         ACT.Gelu_apprx_tanh)
                return empty
            pairs("gmlp_v", 2, gelu_to(gv))
            for n in range(4):
                c = FIRST["gmlp_u"] + n * KT
                through(c, KT)
                if n == 0:
                    root_of(2)
                block_done(c)
                take(f"gmlp_u{n}", gu[:, :, n * COLS:(n + 1) * COLS], by_tile[n % 2], ACT.Gelu_apprx_tanh)

            def silu_z(i, n):
                act.wait_ge(z_used, i * 2 + (n + 1))
                fn(gz[:, :, :], by_tile[n], ACT.Silu).then_inc(half_free[n], 1)
            pairs("gmlp_z", 2, silu_z)
            for u in range(4):
                dst = (xT1 if u < 2 else xT2)[:, 0, :, (u % 2) * P:(u % 2 + 1) * P]
                hi_x(f"yT_gmlp{u}", dst)
            for n in range(2):
                through(FIRST["gmlp_out"] + n * 2 * KT, 2 * KT)

            root_of(3)
            for t in range(TILES):
                hi_x(f"xT_att{t}", xT1[:, 0, :, t * P:(t + 1) * P])
            for half_pair, scale in ((0, DH ** -0.5), (1, 1.0)):
                for n in range(2):
                    c = FIRST["att_qk"] + (2 * half_pair + n) * KT
                    through(c, KT)
                    block_done(c)
                    take(f"att_qk{n}", qk_tok[:, half_pair, :, n * COLS:(n + 1) * COLS], by_tile[n], scale=scale)
            for u in range(4):
                w, t = divmod(u, 2)
                unit = f"qkT{u}"
                is_filled(act, unit)
                take(unit, qkT[:, w, :, t * P:(t + 1) * P], by_128[halves(unit)])
            for u, (dst, func) in enumerate(((av, ACT.Copy), (av, ACT.Copy), (az, ACT.Silu), (az, ACT.Silu))):
                c = FIRST["att_vz"] + u * KT
                through(c, KT)
                block_done(c)
                take(f"att_vz{u}", dst[:, :, (u % 2) * COLS:(u % 2 + 1) * COLS], by_tile[u % 2], func)

            def att_copy(g):
                unit = f"Z{g}"
                is_filled(act, unit)
                if g >= 2:
                    is_emptied(act, f"O{g - 2}")
                fn(zs[:, g % 2, :, :], ps[halves(unit)][:, :, 0:ZW], ACT.Copy).then_inc(half_free[halves(unit)], 1)

            def att_ln(g):
                act.wait_ge(abs_done, g + 1)
                s = sp_[:, g % 2, :, :]
                step(fn(s, s, ACT.Exp, scale=-1.0))
                fn(s, s, ACT.Ln, bias=1.0).then_inc(ln_done, 1)

            def att_exp(g):
                act.wait_ge(la_done, g + 1)
                z = zs[:, g % 2, :, :]
                fn(z, z, ACT.Exp).then_inc(a_done, 1)

            for what, g in ((att_copy, 0), (att_ln, 0), (att_copy, 1), (att_exp, 0), (att_ln, 1), (att_copy, 2),
                            (att_exp, 1), (att_ln, 2), (att_copy, 3), (att_exp, 2), (att_ln, 3), (att_exp, 3)):
                what(g)
            for t in range(TILES):
                hi_x(f"yT_att{t}", xT1[:, 0, :, t * P:(t + 1) * P])
            for n in range(2):
                through(FIRST["att_out"] + n * KT, KT)

            def layer_sums(n, h_ready):
                for t in range(TILES):
                    h_ready(t)
                    if t:
                        act.wait_ge(meaned, 4 * n + t)
                    fn(trash[:, :], h[:, t, :], ACT.Copy, accum_out=sums[:, t:t + 1]).then_inc(meaned, 1)
                act.wait_ge(squared, n + 1)
                for t in range(TILES):
                    act.wait_ge(meaned, 4 * n + 2 + t)
                    fn(trash[:, :], h[:, t, :], ACT.Square, bias=mean_neg[:, t:t + 1], accum_out=sumsq[:, t:t + 1])\
                        .then_inc(meaned, 1)

            root_of(4)
            layer_sums(0, lambda t: act.wait_ge(summed, t + 1))
            root_of(5)
            act.wait_ge(loaded["wg"], 16)
            fn(wg_split[:, 0, :, :], wg_raw[:, :, :], ACT.Copy).then_inc(wg_hi, 1)
            for t in range(TILES):
                hi_x(f"xT_mix{t}", xT1[:, 0, :, t * P:(t + 1) * P])

            for w, scale in ((0, DH ** -0.5), (1, 1.0)):
                c = FIRST["mix_qk"] + w * KT
                through(c, KT)
                block_done(c)
                take(("mix_q", "mix_k")[w], mqk_tok[:, w, :, :], by_tile[w], scale=scale)
            act.wait_ge(gate_abs, 1)
            step(fn(gabs[:, :, :], gabs[:, :, :], ACT.Exp, scale=-1.0))
            fn(gabs[:, :, :], gabs[:, :, :], ACT.Ln, bias=1.0).then_inc(gate_ln, 1)
            for w, unit in enumerate(("mqT", "mkT")):
                is_filled(act, unit)
                take(unit, mqkT[:, w, :, :].rearrange("p n t -> p (n t)"), flat[halves(unit)])
            through(FIRST["mix_vo"], KT)
            block_done(FIRST["mix_vo"])
            take("mix_v", mv[:, :, :, 0:DH], by_tile[A].rearrange("p t (n d) -> p t n d", d=DH))
            through(FIRST["mix_vo"] + KT, KT)
            block_done(FIRST["mix_vo"] + KT)
            take("mix_o", mo[:, :, :], by_tile[B], ACT.Sigmoid)
            is_emptied(act, "G_rows")
            fn(mw[:, :, :], mw[:, :, :], ACT.Exp, scale=-1.0).then_inc(mw_done, 1)
            is_emptied(act, "G_cols")
            fn(cmin[:, :, :], cmin[:, :, :], ACT.Exp, scale=-1.0).then_inc(m_exp, 1)
            through(FIRST["mix_cc"], KT)
            block_done(FIRST["mix_cc"])
            take("mix_cC", cz[:, :, :], by_tile[A])
            through(FIRST["mix_cc"] + KT, KT)
            through(FIRST["mix_cB"], KT)
            block_done(FIRST["mix_cB"])
            take("mix_cB", cB[:, :, :], by_tile[A])
            is_filled(act, "zT")
            take("zT", zT[:, :, 2:], flat[halves("zT")].rearrange("p (n t) -> p n t", t=TOKENS))
            is_filled(act, "cBT")
            take("cBT", cBT[:, :, :].rearrange("p n t -> p (n t)"), flat[halves("cBT")])
            act.wait_ge(hm_sq, 1)
            fn(mrs[:, :, :], mrs[:, :, :], ACT.Sqrt).then_inc(hm_root, 1)
            act.wait_ge(yc_done, 1)
            fn(xT2[:, 0, 0:8, :], yc[:, :, :], ACT.Copy).then_inc(yc_hi, 1)
            is_filled(act, "ymT")
            fn(xT2[:, 0, 8:16, :].rearrange("p n t -> p (n t)"), flat[halves("ymT")], ACT.Copy).then_inc(xT_hi, 1)
            for n in range(2):
                through(FIRST["mix_out"] + n * KT, KT)

            layer_sums(1, lambda t: [is_emptied(act, f"mix_out{n}") for n in range(2)])
            root_of(6)
            for t in range(TILES):
                hi_x(f"xT_peer{t}", xT1[:, 0, :, t * P:(t + 1) * P])

            for n in range(2):
                c = FIRST["peer_q"] + n * KT
                through(c, KT, last=(n == 1))
                block_done(c)
                take(f"peer_q{n}", pq_tok[:, :, n * COLS:(n + 1) * COLS], by_tile[n])
            for u in range(2):
                unit = f"pqT{u}"
                is_filled(act, unit)
                take(unit, pqT[:, 8 * u:8 * u + 8, :].rearrange("p n t -> p (n t)"), flat[halves(unit)])
            is_filled(act, "keysT")
            take("keysT", keysT[:, :, :].rearrange("p n t -> p (n t)"), flat[A])
            for t in range(TILES):
                unit = f"scores{t}"
                is_filled(act, unit)
                take(unit, scores[:, t, :, :].rearrange("p n k -> p (n k)"), flat[halves(unit)])
            for t in range(TILES):
                act.wait_ge(gate_sub, t + 1)
                fn(gate[:, t, :, :], gate[:, t, :, :], ACT.Exp).then_inc(gate_exp, 1)
            for t in range(TILES):
                act.wait_ge(idx_ready[1], (t + 1) * PICKS // (2 * GATHER_SLOTS) + 1)
                pick_t = slice(t * PICKS, (t + 1) * PICKS)
                fn(wgt[:, pick_t], act_[:, pick_t], ACT.Gelu).then_inc(gelu_done, 1)
            layer_sums(2, lambda t: act.wait_ge(summed, TILES + t + 1))
            root_of(7)

        @block.vector
        def _(dve):
            v = nc.vector
            step = step_counter(dve, dve_step)
            xt_count = [0]

            def split_lo(c, ks):
                for k in ks:
                    s = k % SPLIT_SLOTS
                    dve.wait_ge(hi_done, c + (k + 1))
                    v.tensor_tensor(w_split[:, s, 1, :], w_raw[:, k % RAW_SLOTS, :], w_split[:, s, 0, :].bitcast(F32),
                                    ALU.subtract).then_inc(split_done, 1)

            def through(c, kts, last=False):
                split_lo(c, range(AHEAD, kts))
                if not last:
                    split_lo(c + kts, range(AHEAD))

            def pairs(stage, count, empty=None):
                c = FIRST[stage]
                with dve.Fori(0, count) as i:
                    for n in range(2):
                        through(i * (2 * KT) + (c + n * KT), KT)
                        if empty:
                            empty(i, n)

            def lo_x(unit, dst, view=None):
                xt_count[0] += 1
                dve.wait_ge(xT_hi, xt_count[0])
                src = by_128[halves(unit)] if view is None else view
                v.tensor_tensor(dst[1], src, dst[0].bitcast(F32), ALU.subtract).then_inc(half_free[halves(unit)], 1)

            def xT_of(xt, t):
                return xt[:, 0, :, t * P:(t + 1) * P], xt[:, 1, :, t * P:(t + 1) * P]

            def rms_norm(n, src, dst, gain, width):
                for t in range(TILES):
                    ins = v.tensor_tensor_reduce(out=dst[:, t, :], in0=src[:, t, :], in1=src[:, t, :], scale=1.0,
                                                 scalar=0.0, op0=ALU.mult, op1=ALU.add, accum_out=sumsq[:, t:t + 1])
                step(ins)
                v.tensor_scalar(meansq[:, :], sumsq[:, :], 1.0 / width, RMS_EPS, ALU.mult, ALU.add).then_inc(stat, 1)
                dve.wait_ge(rooted, n)
                step(v.reciprocal(rstd[:, :], root[:, :]))
                return [(dst[:, t, :], src[:, t, :], rstd[:, t:t + 1], gain) for t in range(TILES)]

            def scaled(d, s, r, g):
                return v.scalar_tensor_tensor(out=d, in0=s, scalar=r, in1=g, op0=ALU.mult, op1=ALU.mult)

            def magnitude(dst, src):
                return v.scalar_tensor_tensor(out=dst, in0=src, scalar=-1.0, in1=src, op0=ALU.mult, op1=ALU.max)

            def layer_norm(n, gain, bias, rows, signal):
                dve.wait_ge(meaned, 4 * n + 2)
                v.tensor_scalar(mean[:, :], sums[:, :], 1.0 / D, None, ALU.mult).then_inc(dve_mean, 1)
                v.tensor_scalar(mean_neg[:, :], sums[:, :], -1.0 / D, None, ALU.mult).then_inc(squared, 1)
                dve.wait_ge(meaned, 4 * n + 4)
                v.tensor_scalar(meansq[:, :], sumsq[:, :], 1.0 / D, LN_EPS, ALU.mult, ALU.add).then_inc(stat, 1)
                dve.wait_ge(rooted, 5 + n)
                dve.wait_ge(dve_mean, n + 1)
                step(v.reciprocal(rstd[:, :], root[:, :]))
                dve.wait_ge(loaded[rows[0]], rows[1])
                for t in range(TILES):
                    step(v.tensor_scalar(h[:, t, :], h[:, t, :], mean[:, t:t + 1], rstd[:, t:t + 1], ALU.subtract,
                                         ALU.mult))
                    step(v.tensor_tensor(h[:, t, :], h[:, t, :], gain[:, :], ALU.mult))
                    v.tensor_tensor(h[:, t, :], h[:, t, :], bias[:, :], ALU.add).then_inc(signal, 1)

            def add_to_h(unit, scale=1.0):
                n = int(unit[-1])
                dst = h[:, :, n * COLS:(n + 1) * COLS]
                src = by_tile[halves(unit)]
                v.scalar_tensor_tensor(out=dst, in0=dst, scalar=scale, in1=src, op0=ALU.mult, op1=ALU.add)\
                    .then_inc(half_free[halves(unit)], 1)

            def out_block(unit, c, kts=KT, scale=1.0):
                through(c, kts)
                dve.wait_ge(products, c + kts)
                add_to_h(unit, scale)

            split_lo(0, range(AHEAD))
            dve.wait_ge(loaded["x"], 16 * TILES)
            todo = rms_norm(1, h, xn, row_norm[:, :], D)
            dve.wait_ge(loaded["row_norm"], 16)
            for args in todo:
                scaled(*args).then_inc(normed, 1)
            is_filled(dve, "ws")
            dve.wait_ge(consts_done, 1)
            v.tensor_tensor(wsT[:, :, :], by_128[A], upto[:, :].unsqueeze(1).to_broadcast([P, GROUPS, P]), ALU.mult)\
                .then_inc(half_free[A], 1)
            is_filled(dve, "params")
            v.tensor_copy(cols[:, :], flat[B][:, 0:48]).then_inc(half_free[B], 1)
            for t in range(TILES):
                lo_x(f"xT_gmlp{t}", xT_of(xT1, t))

            pairs("gmlp_v", 2)
            c = FIRST["gmlp_u"]
            split_lo(c, range(AHEAD, 8))
            is_emptied(dve, "gmlp_v2")
            is_emptied(dve, "gmlp_v3")
            for n in range(4):
                t, part = divmod(n, 2)
                src = gv[:, t, part * D:(part + 1) * D]
                if n:
                    dve.wait_ge(v_squared, n)
                v.tensor_tensor_reduce(out=gz[:, :, :].rearrange("p a b -> p (a b)"), in0=src, in1=src, scale=1.0,
                                       scalar=0.0, op0=ALU.mult, op1=ALU.add, accum_out=sumsq_v[:, t, part:part + 1])\
                    .then_inc(v_squared, 1)
                split_lo(c, range(8 + 2 * n, 10 + 2 * n))
            dve.wait_ge(v_squared, 4)
            step(v.tensor_reduce(sumsq[:, :], sumsq_v[:, :, :], AX_X, ALU.add))
            v.tensor_scalar(meansq[:, :], sumsq[:, :], 1.0 / GMLP_W, RMS_EPS, ALU.mult, ALU.add).then_inc(stat, 1)
            split_lo(c + KT, range(AHEAD))
            dve.wait_ge(rooted, 2)
            v.reciprocal(rstd[:, :], root[:, :]).then_inc(z_used, 1)
            dve.wait_ge(z_used, 1)
            dve.wait_ge(loaded["row_v"], 16)
            for t in range(TILES):
                scaled(gv[:, t, :], gv[:, t, :], rstd[:, t:t + 1], row_v[:, :]).then_inc(v_normed, 1)
                split_lo(c + KT, range(AHEAD + 4 * t, AHEAD + 4 * t + 4))
            split_lo(c + KT, range(AHEAD + 8, KT))
            split_lo(c + 2 * KT, range(AHEAD))
            for n in (2, 3):
                through(c + n * KT, KT)
            for n in range(4):
                is_emptied(dve, f"gmlp_u{n}")
            for u in range(4):
                unit = f"mix{u}"
                is_filled(dve, unit)
                hf = halves(unit)
                for j in range(4):
                    g = 4 * u + j
                    for n in range(TILES):
                        dst = gu[:, n, g * GROUP_DIM:(g + 1) * GROUP_DIM]
                        ins = v.scalar_tensor_tensor(out=dst, in0=ps[hf][:, j, n * GROUP_DIM:(n + 1) * GROUP_DIM],
                                                     scalar=cols[:, g:g + 1], in1=dst, op0=ALU.add, op1=ALU.mult)
                ins.then_inc(half_free[hf], 1)

            def times_z(i, n):
                dve.wait_ge(half_free[n], i + (NTH[f"gmlp_z{n}"][1] + 1))
                dst = gu[:, :, bass.ds(i * (2 * COLS) + n * COLS, COLS)]
                v.tensor_tensor(dst, dst, gz[:, :, :], ALU.mult).then_inc(z_used, 1)
            pairs("gmlp_z", 2, times_z)
            for u in range(4):
                lo_x(f"yT_gmlp{u}", xT_of(xT1 if u < 2 else xT2, u % 2))
            for n in range(2):
                out_block(f"gmlp_out{n}", FIRST["gmlp_out"] + n * 2 * KT, 2 * KT)

            for n in range(2):
                is_emptied(dve, f"gmlp_out{n}")
            todo = rms_norm(3, h, xn, row_norm[:, :], D)
            dve.wait_ge(loaded["row_norm1"], 16)
            for args in todo:
                scaled(*args).then_inc(normed, 1)
            for t in range(TILES):
                lo_x(f"xT_att{t}", xT_of(xT1, t))
            pairs("att_qk", 2)
            pairs("att_vz", 2)
            diag = lambda m: m.rearrange("p j (k t) -> p j k t", t=P)[:, :, 0:3:2, :]
            over = lambda m, n: m.unsqueeze(1).unsqueeze(1).to_broadcast([P, n, 2, P])

            def att_abs(g):
                is_emptied(dve, f"Z{g}")
                magnitude(sp_[:, g % 2, :, :], zs[:, g % 2, :, :]).then_inc(abs_done, 1)

            def att_sp(g):
                dve.wait_ge(ln_done, g + 1)
                s = sp_[:, g % 2, :, :]
                step(v.scalar_tensor_tensor(out=s, in0=zs[:, g % 2, :, :], scalar=0.0, in1=s, op0=ALU.max, op1=ALU.add))
                v.tensor_tensor(diag(s), diag(s), over(before[:, :], 4), ALU.mult).then_inc(sp_done, 1)

            def att_la(g):
                unit = f"L{g}"
                is_filled(dve, unit)
                z = zs[:, g % 2, :, :]
                v.tensor_tensor(z, z, ps[halves(unit)][:, :, 0:ZW], ALU.subtract).then_inc(half_free[halves(unit)], 1)
                is_emptied(dve, unit)
                v.tensor_tensor(diag(z), diag(z), over(barred[:, :], 4), ALU.add).then_inc(la_done, 1)

            def att_out(g):
                unit = f"O{g}"
                is_filled(dve, unit)
                hf = halves(unit)
                src = ps[hf][:, :, 0:2 * DH].rearrange("p j (t d) -> p j t d", d=DH)
                dst = az[:, :, g * 4 * DH:(g + 1) * 4 * DH].rearrange("p t (j d) -> p j t d", d=DH)
                v.tensor_tensor(dst, src, dst, ALU.mult).then_inc(half_free[hf], 1)

            is_emptied(dve, "att_vz2")
            is_emptied(dve, "att_vz3")
            for what, g in ((att_abs, 0), (att_sp, 0), (att_abs, 1), (att_la, 0), (att_sp, 1), (att_out, 0), (att_abs, 2),
                            (att_la, 1), (att_sp, 2), (att_out, 1), (att_abs, 3), (att_la, 2), (att_sp, 3), (att_out, 2),
                            (att_la, 3), (att_out, 3)):
                what(g)
            for t in range(TILES):
                lo_x(f"yT_att{t}", xT_of(xT1, t))
            for n in range(2):
                out_block(f"att_out{n}", FIRST["att_out"] + n * KT)

            for n in range(2):
                is_emptied(dve, f"att_out{n}")
            todo = rms_norm(4, h, xn, row_a[:, :], D)
            dve.wait_ge(loaded["rows_mix"], 48)
            for _, s, r, g in todo:
                scaled(s, s, r, g).then_inc(summed, 1)
            layer_norm(0, row_b, row_c, ("rows_mix", 48), normed)
            dve.wait_ge(wg_hi, 1)
            v.tensor_tensor(wg_split[:, 1, :, :], wg_raw[:, :, :], wg_split[:, 0, :, :].bitcast(F32), ALU.subtract)\
                .then_inc(wg_done, 1)
            for t in range(TILES):
                lo_x(f"xT_mix{t}", xT_of(xT1, t))

            v.memset(mv[:, :, :, DH:DH + 1], 1.0).then_inc(mv_ones, 1)
            for n in range(2):
                through(FIRST["mix_qk"] + n * KT, KT)
            is_filled(dve, "gates")
            hf = halves("gates")
            dve.wait_ge(loaded["gate"], 16)
            v.tensor_tensor(gates[:, :, :], ps[hf][:, 0:2, 0:16], row_gate[:, :].unsqueeze(1).to_broadcast([P, TILES, 16]),
                            ALU.add).then_inc(half_free[hf], 1)
            is_emptied(dve, "gates")
            forget = gates[:, :, M_HEADS:]
            magnitude(gabs[:, :, :], forget).then_inc(gate_abs, 1)
            dve.wait_ge(gate_ln, 1)
            v.scalar_tensor_tensor(out=logf[:, :, :], in0=forget, scalar=0.0, in1=gabs[:, :, :], op0=ALU.min,
                                   op1=ALU.subtract).then_inc(logf_done, 1)
            is_filled(dve, "cum")
            hf = halves("cum")
            v.tensor_copy(Bc[:, :, :], ps[hf][:, 0:2, 0:M_HEADS]).then_inc(half_free[hf], 1)
            is_emptied(dve, "cum")
            v.tensor_tensor(cc[:, :, :], gates[:, :, 0:M_HEADS], Bc[:, :, :], ALU.subtract).then_inc(cc_done, 1)
            for n in range(2):
                through(FIRST["mix_vo"] + n * KT, KT)
            is_filled(dve, "cT")
            hf = halves("cT")
            v.tensor_copy(c_rows[:, :], ps[hf][0:M_HEADS, 0, 0:TOKENS]).then_inc(half_free[hf], 1)
            is_emptied(dve, "cT")
            v.tensor_tensor_scan(G[:, :], ones[0:M_HEADS, :], c_rows[:, :], 0.0, ALU.mult, ALU.max).then_inc(G_done, 1)
            is_filled(dve, "G_rows")
            hf = halves("G_rows")
            for n in range(M_HEADS):
                for t, (lo, hi) in enumerate(((0, TOKENS), (TOKENS, ZW))):
                    src = flat[hf][:, n * TOKENS + t * P:(n + 1) * TOKENS]
                    ins = v.tensor_scalar(mw[:, n, lo:hi], src, cc[:, t, n:n + 1], 0.0, ALU.subtract, ALU.max)
            ins.then_inc(half_free[hf], 1)
            is_filled(dve, "G_cols")
            hf = halves("G_cols")
            v.tensor_tensor(cmin[:, :, :], ps[hf][:, 0:2, 0:M_HEADS], Bc[:, :, :], ALU.add).then_inc(half_free[hf], 1)
            dve.wait_ge(mw_done, 1)
            v.tensor_tensor(diag(mw[:, :, :]), diag(mw[:, :, :]), over(upto[:, :], M_HEADS), ALU.mult).then_inc(mw_masked, 1)
            through(FIRST["mix_cc"], KT)
            through(FIRST["mix_cc"] + KT, KT)
            dve.wait_ge(products, FIRST["mix_cc"] + 2 * KT)
            is_emptied(dve, "mix_cC")
            v.tensor_tensor(cz[:, :, :], by_tile[B], cz[:, :, :], ALU.mult).then_inc(half_free[B], 1)
            dve.wait_ge(mw_masked, 1)
            for g in range(2):
                unit = f"MS{g}"
                is_filled(dve, unit)
                hf = halves(unit)
                v.tensor_tensor(ms[:, g, :, :], ps[hf][:, :, 0:ZW], mw[:, 4 * g:4 * g + 4, :], ALU.mult)\
                    .then_inc(half_free[hf], 1)
            v.memset(zT[:, :, 0:2], 0.0).then_inc(zT_pad, 1)
            through(FIRST["mix_cB"], KT)
            dve.wait_ge(m_exp, 1)
            for g in range(2):
                unit = f"MO{g}"
                is_filled(dve, unit)
                hf = halves(unit)
                o = ps[hf][:, :, 0:2 * (DH + 1)].rearrange("p j (t e) -> p j t e", e=DH + 1)
                floor = cmin[:, :, 4 * g:4 * g + 4].rearrange("p t j -> p j t")
                den = mden[:, :, :]
                step(v.tensor_copy(den, o[:, :, :, DH]))
                step(magnitude(den, den))
                step(v.tensor_tensor(den, den, floor, ALU.max))
                step(v.reciprocal(den, den))
                v.tensor_tensor(hm[:, :, 4 * g:4 * g + 4, :].rearrange("p t j d -> p j t d"), o[:, :, :, 0:DH],
                                den.unsqueeze(3).to_broadcast([P, 4, TILES, DH]), ALU.mult).then_inc(half_free[hf], 1)
                is_emptied(dve, unit)
            wide = lambda m: m.unsqueeze(3).to_broadcast([P, TILES, M_HEADS, DH])
            step(v.tensor_reduce(mmu[:, :, :], hm[:, :, :, :], AX_X, ALU.add))
            step(v.tensor_scalar(mmu[:, :, :], mmu[:, :, :], 1.0 / DH, None, ALU.mult))
            step(v.tensor_tensor(hm[:, :, :, :], hm[:, :, :, :], wide(mmu[:, :, :]), ALU.subtract))
            step(v.tensor_tensor(hsq[:, :, :, :], hm[:, :, :, :], hm[:, :, :, :], ALU.mult))
            step(v.tensor_reduce(mrs[:, :, :], hsq[:, :, :, :], AX_X, ALU.add))
            v.tensor_scalar(mrs[:, :, :], mrs[:, :, :], 1.0 / DH, LN_EPS, ALU.mult, ALU.add).then_inc(hm_sq, 1)
            dve.wait_ge(hm_root, 1)
            step(v.reciprocal(mrs[:, :, :], mrs[:, :, :]))
            step(v.tensor_tensor(hm[:, :, :, :], hm[:, :, :, :], wide(mrs[:, :, :]), ALU.mult))
            hmf = hm[:, :, :, :].rearrange("p t n d -> p t (n d)")
            dve.wait_ge(loaded["mh"], 16)
            step(v.tensor_tensor(hmf, hmf, row_mh[:, :].unsqueeze(1).to_broadcast([P, TILES, D_HALF]), ALU.mult))
            is_emptied(dve, "mix_o")
            v.tensor_tensor(hmf, hmf, mo[:, :, :], ALU.mult).then_inc(ym_done, 1)
            is_emptied(dve, "zT")
            for f in range(M_HEADS):
                ins = v.tensor_scalar(yc[:, f, :], zT[:, f, 2:2 + TOKENS], cols[:, 32 + f:33 + f], cols[:, 40 + f:41 + f],
                                      ALU.mult, ALU.add)
            step(ins)
            for j in (1, 0):
                for f in range(M_HEADS):
                    ins = v.scalar_tensor_tensor(out=yc[:, f, :], in0=zT[:, f, j:j + TOKENS],
                                                 scalar=cols[:, 16 + 8 * j + f:17 + 8 * j + f], in1=yc[:, f, :],
                                                 op0=ALU.mult, op1=ALU.add)
                step(ins)
            is_emptied(dve, "cBT")
            v.tensor_tensor(yc[:, :, :], yc[:, :, :], cBT[:, :, :], ALU.mult).then_inc(yc_done, 1)
            dve.wait_ge(yc_hi, 1)
            v.tensor_tensor(xT2[:, 1, 0:8, :], yc[:, :, :], xT2[:, 0, 0:8, :].bitcast(F32), ALU.subtract)\
                .then_inc(yc_lo, 1)
            lo_x("ymT", (xT2[:, 0, 8:16, :], xT2[:, 1, 8:16, :]),
                 flat[halves("ymT")].rearrange("p (n t) -> p n t", t=TOKENS))
            for n in range(2):
                out_block(f"mix_out{n}", FIRST["mix_out"] + n * KT, scale=ALPHA)
            for n in range(2):
                is_emptied(dve, f"mix_out{n}")
            layer_norm(1, row_a, row_b, ("rows_ln1", 32), normed)
            for t in range(TILES):
                lo_x(f"xT_peer{t}", xT_of(xT1, t))

            for n in range(2):
                through(FIRST["peer_q"] + n * KT, KT, last=(n == 1))

            def best16(values, rest, top, at, groups):
                for n in range(groups):
                    ins = v.max(top[:, n, 0:8], values[:, n, :])
                step(ins)
                for n in range(groups):
                    v.max_index(at[:, n, 0:8], top[:, n, 0:8], values[:, n, :])
                    ins = v.match_replace(rest[:, n, :], top[:, n, 0:8], values[:, n, :], LOWEST)
                step(ins)
                for n in range(groups):
                    ins = v.max(top[:, n, 8:16], rest[:, n, :])
                step(ins)
                for n in range(groups):
                    ins = v.max_index(at[:, n, 8:16], top[:, n, 8:16], rest[:, n, :])
                step(ins)

            four = [P, PEER_HEADS, TOPK, TOPK]
            onehot4 = onehot[:, :, :].rearrange("p (h k) a -> p h k a", k=TOPK)
            sv4 = sv[:, :, :].rearrange("p (h s) k -> p h s k", s=2)
            sif4 = sif[:, :, :].rearrange("p (h s) k -> p h s k", s=2)

            def choose(t):
                best16(scores[:, t, :, :], left, sv, si, 2 * PEER_HEADS)
                step(v.tensor_copy(sif[:, :, :], si[:, :, :]))
                step(v.tensor_tensor(cand[:, :, :].rearrange("p h (a b) -> p h a b", b=TOPK),
                                     sv4[:, :, 0, :].unsqueeze(3).to_broadcast(four),
                                     sv4[:, :, 1, :].unsqueeze(2).to_broadcast(four), ALU.add))
                best16(cand, cand_left, tops, topj, PEER_HEADS)
                v.tensor_tensor(gate[:, t, :, :], tops[:, :, :], tops[:, :, 0:1].to_broadcast([P, PEER_HEADS, TOPK]),
                                ALU.subtract).then_inc(gate_sub, 1)
                for half, (op, n) in enumerate(((ALU.logical_shift_right, 4), (ALU.bitwise_and, TOPK - 1))):
                    step(v.tensor_scalar(topa[:, :, :], topj[:, :, :], n, None, op))
                    step(v.tensor_copy(topaf[:, :, :], topa[:, :, :]))
                    step(v.tensor_tensor(onehot4, topaf[:, :, :].unsqueeze(3).to_broadcast(four),
                                         iota16[:, :].unsqueeze(1).unsqueeze(1).to_broadcast(four), ALU.is_equal))
                    step(v.tensor_tensor(onehot4, onehot4, sif4[:, :, half, :].unsqueeze(2).to_broadcast(four), ALU.mult))
                    step(v.tensor_reduce(rowid[:, half, :], onehot[:, :, :], AX_X, ALU.add))
                step(v.scalar_tensor_tensor(out=eid[:, t * PICKS:(t + 1) * PICKS], in0=rowid[:, 0, :],
                                            scalar=float(N_KEYS), in1=rowid[:, 1, :], op0=ALU.mult, op1=ALU.add))

            def gates_of(t):
                dve.wait_ge(gate_exp, t + 1)
                step(v.tensor_reduce(gsum[:, :], gate[:, t, :, :], AX_X, ALU.add))
                step(v.reciprocal(gsum[:, :], gsum[:, :]))
                step(v.tensor_tensor(gate[:, t, :, :], gate[:, t, :, :],
                                     gsum[:, :].unsqueeze(2).to_broadcast([P, PEER_HEADS, TOPK]), ALU.mult))

            def stage(b, first):
                v.tensor_copy(idx[:, b, :], eid[:, bass.ds(first, GATHER_SLOTS)]).then_inc(idx_ready[b], 1)

            is_emptied(dve, "scores0")
            is_emptied(dve, "scores1")
            choose(0)
            dve.sem_inc(rows_used, GATHER_SLOTS)
            for b in range(2):
                stage(b, b * GATHER_SLOTS)
            choose(1)
            step(v.tensor_copy(eid[:, TILES * PICKS:], eid[:, 0:2 * GATHER_SLOTS]))
            for t in range(TILES):
                gates_of(t)

            BODY = 2 * GATHER_SLOTS
            TURNS = PICKS // BODY

            def gathered(i, t, table, b, s):
                dve.wait_ge(row_landed[s], i * 32 + 16 * (2 * TURNS * (TILES * table + t) + b + 1))

            for t in range(TILES):
                with dve.Fori(0, TURNS) as i:
                    for b in range(2):
                        for s in range(GATHER_SLOTS):
                            gathered(i, t, 0, b, s)
                            v.tensor_tensor_reduce(out=ring[:, s, :], in0=ring[:, s, :], in1=h[:, t, :], scale=1.0,
                                                   scalar=0.0, op0=ALU.mult, op1=ALU.add,
                                                   accum_out=dots[:, b, s:s + 1]).then_inc(rows_used, 1)
                        dve.wait_ge(rows_used, i * BODY + (t * PICKS + (b + 2) * GATHER_SLOTS))
                        v.tensor_copy(act_[:, bass.ds(i * BODY + (t * PICKS + b * GATHER_SLOTS), GATHER_SLOTS)],
                                      dots[:, b, :])
                        stage(b, i * BODY + (t * PICKS + (b + 2) * GATHER_SLOTS))
            for t in range(TILES):
                dve.wait_ge(gelu_done, t + 1)
                w = wgt[:, t * PICKS:(t + 1) * PICKS]
                step(v.tensor_tensor(w, w, gate[:, t, :, :].rearrange("p h k -> p (h k)"), ALU.mult))
            for t in range(TILES):
                if t:
                    dve.wait_ge(summed, TILES + t)
                step(v.memset(vacc[:, :, :], 0.0))
                with dve.Fori(0, TURNS) as i:
                    for b in range(2):
                        for s in range(GATHER_SLOTS):
                            n = t * PICKS + b * GATHER_SLOTS + s
                            gathered(i, t, 1, b, s)
                            dve.wait_ge(rows_used, i * BODY + (TILES * PICKS + n + GATHER_SLOTS - 1))
                            v.scalar_tensor_tensor(out=vacc[:, s % 2, :], in0=ring[:, s, :],
                                                   scalar=wgt[:, bass.ds(i * BODY + n, 1)], in1=vacc[:, s % 2, :],
                                                   op0=ALU.mult, op1=ALU.add).then_inc(rows_used, 1)
                        stage(b, i * BODY + (t * PICKS + (b + 2) * GATHER_SLOTS))
                dve.wait_ge(rows_used, (TILES + t + 1) * PICKS + GATHER_SLOTS)
                step(v.tensor_tensor(vacc[:, 0, :], vacc[:, 0, :], vacc[:, 1, :], ALU.add))
                v.scalar_tensor_tensor(out=h[:, t, :], in0=h[:, t, :], scalar=ALPHA, in1=vacc[:, 0, :], op0=ALU.mult,
                                       op1=ALU.add).then_inc(summed, 1)
            layer_norm(2, row_g2, row_b2, ("rows_ln2", 32), out_ready)


_INS = ["x", "norm_g", "a_w_in", "a_v_norm_g", "a_w_s", "a_b_s", "a_w_out", "b_w_in", "b_w_out", "final_g", "ln_in_g_2",
        "ln_in_b_2", "w_in_2", "b_gate_2", "conv_w_2", "conv_b_2", "mh_norm_g_2", "w_out_2", "ln1_g_2", "ln1_b_2",
        "peer_wq_2", "peer_keys_2", "peer_u_2", "peer_v_2", "ln2_g_2", "ln2_b_2"]


def kernel(**inputs):
    import numpy as np
    import concourse.bacc as bacc
    from concourse.bass_utils import run_bass_kernel_spmd

    nc = bacc.Bacc("TRN2", target_bir_lowering=False, num_devices=1)
    arrays, args = {}, []
    for name in _INS:
        a = np.ascontiguousarray(inputs[name])
        arrays["in_" + name] = a
        args.append(nc.dram_tensor("in_" + name, a.shape, F32, kind="ExternalInput").ap())
    out = nc.dram_tensor("out_h", (1, TOKENS, D), F32, kind="ExternalOutput").ap()
    build(nc, *args, out)
    r = run_bass_kernel_spmd(nc, [arrays], core_ids=[0])
    return r.results[0]["out_h"]
```

```python
from contextlib import ExitStack

import concourse.bass as bass
from concourse import mybir

F32 = mybir.dt.float32
F32R = mybir.dt.float32r
U32 = mybir.dt.uint32
ALU = mybir.AluOpType
ACT = mybir.ActivationFunctionType
AX_X = mybir.AxisListType.X

P = 128
TOKENS = 256
TILES = TOKENS // P
D = 2048
KT = D // P
COLS = 1024
BANK = 512
GMLP_W = 4096
GROUPS = 16
GROUP_DIM = GMLP_W // GROUPS
HEADS = 16
DH = 128
M_HEADS = 8
D_HALF = 1024
CONV_K = 3
PEER_HEADS = 8
N_KEYS = 128
TOPK = 16
PICKS = PEER_HEADS * TOPK
RMS_EPS = 1e-6
LN_EPS = 1e-5
ALPHA = 2.0 ** 0.25
NEG = -1.0e30
LOWEST = -3.0e38
ZW = 3 * P
GROUP_PICKS = PICKS // 2

RAW_SLOTS = 4
SPLIT_SLOTS = 4
AHEAD = SPLIT_SLOTS
GATHER_SLOTS = 8
A, B = 0, 1

UNITS = (
    [(f"xT_gmlp{i}", i % 2, False) for i in range(4)]
    + [(f"gmlp_v{i}", i % 2, True) for i in range(4)]
    + [("gmlp_u0", A, True), ("ws", B, False), ("params", B, False), ("gmlp_u1", B, True),
       ("gmlp_u2", A, True), ("mix0", B, False), ("mix1", B, False),
       ("gmlp_u3", B, True), ("mix2", A, False), ("gmlp_z0", A, True), ("mix3", B, False),
       ("gmlp_z1", B, True), ("yT_gmlp0", A, False), ("gmlp_z2", A, True), ("yT_gmlp1", B, False),
       ("gmlp_z3", B, True), ("gmlp_out0", A, True), ("yT_gmlp2", B, False), ("yT_gmlp3", B, False)]
    + [("gmlp_out1", B, True), ("xT_att0", A, False), ("att_q0", A, True), ("xT_att1", B, False),
       ("att_q1", B, True), ("qkT0", A, False), ("att_k0", A, True), ("qkT1", B, False),
       ("att_k1", B, True), ("qkT2", A, False), ("att_v0", A, True), ("qkT3", B, False), ("att_v1", B, True)]
    + [("att_z0", A, True), ("Z0", B, False), ("Z1", B, False), ("L0", B, False), ("O0", B, False), ("L1", B, False),
       ("Z2", B, False), ("O1", B, False), ("att_z1", A, True), ("L2", B, False), ("Z3", B, False), ("O2", B, False),
       ("L3", B, False), ("O3", B, False), ("yT_att0", B, False)]
    + [("att_out0", B, True), ("yT_att1", A, False), ("att_out1", A, True)]
    + [("xT_mix0", B, False), ("xT_mix1", A, False), ("mix_q", A, True), ("xT_mix2", B, False), ("xT_mix3", B, False)]
    + [("mix_k", B, True), ("mqT", A, False), ("gates", A, False), ("cum", A, False)]
    + [("mix_v", A, True), ("mkT", B, False), ("cT", B, False), ("G_rows", B, False), ("G_cols", B, False)]
    + [("mix_cC", B, True), ("MS0", A, False), ("MS1", A, False), ("MO0", A, False), ("MO1", A, False)]
    + [("mix_ch", A, True), ("mix_cB", B, True), ("zT", A, False), ("mix_o", A, True), ("cBT", B, False)]
    + [("mix_out0", B, True), ("ymT", A, False), ("mix_out1", A, True)]
    + [("xT_peer0", B, False), ("xT_peer1", A, False), ("peer_q0", A, True), ("xT_peer2", B, False),
       ("xT_peer3", B, False), ("keysT", B, False)]
    + [("peer_q1", B, True), ("pqT0", A, False), ("scores0", A, False), ("pqT1", A, False), ("scores1", A, False)]
)

STREAM = [("gmlp_v", 4, KT), ("gmlp_u", 4, KT), ("gmlp_z", 4, KT), ("gmlp_out", 2, 2 * KT), ("att_q", 2, KT),
          ("att_k", 2, KT), ("att_v", 2, KT), ("att_z", 2, KT), ("att_out", 2, KT), ("mix_in", 7, KT),
          ("mix_out", 2, KT), ("peer_q", 2, KT)]
MIX_IN = {"mix_q": (0, 3), "mix_k": (1, 4), "mix_v": (2, 5), "mix_cC": (3, 1), "mix_ch": (4, 2), "mix_cB": (5, 0),
          "mix_o": (6, 6)}


def number_units():
    used, filled, nth, fill = [0, 0], [0, 0], {}, {}
    for name, half, streams in UNITS:
        nth[name] = (half, used[half])
        used[half] += 1
        if not streams:
            filled[half] += 1
            fill[name] = filled[half]
    return nth, fill


def number_chunks():
    first, at = {}, 0
    for name, blocks, kts in STREAM:
        for n in range(blocks):
            first[f"{name}{n}"] = at
            at += kts
    for name, (n, _) in MIX_IN.items():
        first[name] = first[f"mix_in{n}"]
    return first, at


def build(nc, x, norm_g, a_w_in, a_v_norm_g, a_w_s, a_b_s, a_w_out, b_w_in, b_w_out, final_g, ln_in_g_2, ln_in_b_2,
          w_in_2, b_gate_2, conv_w_2, conv_b_2, mh_norm_g_2, w_out_2, ln1_g_2, ln1_b_2, peer_wq_2, peer_keys_2,
          peer_u_2, peer_v_2, ln2_g_2, ln2_b_2, out):
    NTH, FILL = number_units()
    FIRST, CHUNKS = number_chunks()

    ctx = ExitStack()
    with ctx:
        at_byte = [(nc.sbuf_base + 31) // 32 * 32]

        def region(size):
            start = at_byte[0]
            at_byte[0] += (size + 31) // 32 * 32
            assert at_byte[0] <= nc.sbuf_usable_end, at_byte[0]
            return start

        def sb(name, shape, dt, offset):
            return nc.alloc_sbuf_tensor_at(name, shape, dt, offset=offset)

        def packer(start, size):
            place = [start]

            def put(name, shape, dt=F32):
                n = 4
                for s in shape[1:]:
                    n *= s
                o = place[0]
                place[0] += (n + 31) // 32 * 32
                assert place[0] <= start + size, name
                return sb(name, shape, dt, o)
            return put

        KB = 1024
        T2 = region(32 * KB)
        T1 = region(32 * KB)
        SPLIT = region(32 * KB)
        RAW = region(16 * KB)
        H = region(16 * KB)
        ROWS = region(24 * KB)
        SCR = region(48 * KB + 512)
        SMALL = region(7 * KB)

        xT1 = sb("xT1", [P, 2, KT, TOKENS], F32R, T1)
        xT2 = sb("xT2", [P, 2, KT, TOKENS], F32R, T2)
        w_split = sb("w_split", [P, SPLIT_SLOTS, 2, COLS], F32R, SPLIT)
        w_raw = sb("w_raw", [P, RAW_SLOTS, COLS], F32, RAW)
        h = sb("h", [P, TILES, D], F32, H)

        tiny = packer(SMALL, 7 * KB)
        ident = tiny("ident", [P, P])
        upto = tiny("upto", [P, P])
        onward = tiny("onward", [P, P])
        before = tiny("before", [P, P])
        barred = tiny("barred", [P, P])
        ones = tiny("ones", [P, TOKENS])
        iota16 = tiny("iota16", [P, TOPK])
        cols = tiny("cols", [P, 48])
        sumsq = tiny("sumsq", [P, TILES, 2])
        meansq = tiny("meansq", [P, TILES])
        root = tiny("root", [P, TILES])
        rstd = tiny("rstd", [P, TILES])
        rstd_v = tiny("rstd_v", [P, TILES])
        rstd_q = tiny("rstd_q", [P, TILES])
        bn = tiny("bn", [P, TILES, 4, 6])
        moments = tiny("moments", [P, TILES, 2])

        xg = sb("xg", [P, TILES, D], F32, SCR)
        gu = sb("gu", [P, TILES, GMLP_W], F32, SCR)
        ws_raw = sb("ws_raw", [P, GROUPS, P], F32, SCR + 16 * KB)
        x_trash = sb("x_trash", [P, D], F32, SCR + 24 * KB)
        wsT = sb("wsT", [P, GROUPS, P], F32, SCR + 32 * KB)
        gz = sb("gz", [P, TILES, COLS], F32, SCR + 40 * KB)
        param_rows = sb("param_rows", [48, P], F32, SCR + 40 * KB)
        gv = sb("gv", [P, TILES, GMLP_W], F32, T2)
        row_norm = sb("row_norm", [P, D], F32, ROWS)
        row_v = sb("row_v", [P, GMLP_W], F32, ROWS + 8 * KB)

        q_trash = sb("q_trash", [P, COLS], F32, SCR + 40 * KB)
        q_tok = sb("q_tok", [P, 2, TILES, COLS], F32, T1)
        k_tok = sb("k_tok", [P, 2, TILES, COLS], F32, T1 + 16 * KB)
        qkT = sb("qkT", [P, 2, HEADS, TOKENS], F32, SCR)
        av = sb("av", [P, TILES, D], F32, SCR + 32 * KB)
        ao = sb("ao", [P, 2, TILES, COLS], F32, T1)
        az = sb("az", [P, 2, TILES, COLS], F32, T1 + 16 * KB)
        ay = sb("ay", [P, 2, TILES, COLS], F32, SCR)
        zs = sb("zs", [P, 2, 4, ZW], F32, ROWS)
        sp_ = sb("softplus", [P, 2, 4, ZW], F32, ROWS + 12 * KB)

        row_a = sb("row_a", [P, D], F32, ROWS)
        row_b = sb("row_b", [P, D], F32, ROWS + 8 * KB)
        row_c = sb("row_c", [P, D], F32, ROWS + 16 * KB)
        p_ = sb("h_gained", [P, TILES, D], F32, SCR + 16 * KB)
        p_trash = sb("p_trash", [P, COLS], F32, SCR + 32 * KB)
        mqk_tok = sb("mqk_tok", [P, 2, TILES, D_HALF], F32, T1)
        mw = sb("mw", [P, M_HEADS, ZW], F32, T1 + 16 * KB)
        wg_raw = sb("wg_raw", [P, KT, 16], F32, T1 + 28 * KB)
        wg_split = sb("wg_split", [P, 2, KT, 16], F32R, T1 + 29 * KB)
        G = sb("G", [M_HEADS, TOKENS], F32, T1 + 31 * KB)
        c_rows = sb("c_rows", [M_HEADS, TOKENS], F32, T1 + 28 * KB)
        hsq = sb("hsq", [P, TILES, M_HEADS, DH], F32, T1 + 8 * KB)
        mqkT = sb("mqkT", [P, 2, M_HEADS, TOKENS], F32, SCR)
        mv = sb("mv", [P, TILES, M_HEADS, DH + 1], F32, SCR + 16 * KB + 128)
        mo = sb("mo", [P, TILES, D_HALF], F32, SCR + 24 * KB + 256)
        cB = sb("cB", [P, TILES, D_HALF], F32, SCR + 32 * KB + 256)
        cz = sb("cz", [P, TILES, D_HALF], F32, SCR + 40 * KB + 256)
        row_mh = sb("row_mh", [P, D_HALF], F32, ROWS)
        hm = sb("hm", [P, TILES, M_HEADS, DH], F32, ROWS + 4 * KB)
        ms = sb("ms", [P, 2, 4, ZW], F32, ROWS + 12 * KB)
        zT = sb("zT", [P, M_HEADS, TOKENS + 2], F32, SCR)
        cBT = sb("cBT", [P, M_HEADS, TOKENS], F32, SCR + 8256)
        yc = sb("yc", [P, M_HEADS, TOKENS], F32, SCR + 16 * KB + 128)
        row_gate = tiny("row_gate", [P, 16])
        gates = tiny("gates", [P, TILES, 16])
        gabs = tiny("gabs", [P, TILES, M_HEADS])
        logf = tiny("logf", [P, TILES, M_HEADS])
        Bc = tiny("Bc", [P, TILES, M_HEADS])
        cc = tiny("cc", [P, TILES, M_HEADS])
        cmin = tiny("cmin", [P, TILES, M_HEADS])
        mden = tiny("mden", [P, 4, TILES])
        mmu = tiny("mmu", [P, TILES, M_HEADS])
        mrs = tiny("mrs", [P, TILES, M_HEADS])

        pq_tok = sb("pq_tok", [P, 2, TILES, COLS], F32, SCR)
        pqT = sb("pqT", [P, 2 * PEER_HEADS, TOKENS], F32, SCR + 16 * KB)
        keysT = sb("keysT", [P, 2 * PEER_HEADS, P], F32, SCR + 32 * KB)
        keys_raw = sb("keys_raw", [P, 2 * PEER_HEADS, P], F32, SCR + 40 * KB)
        scores = [sb("scores_a", [P, TILES, PEER_HEADS, N_KEYS], F32, SCR + 40 * KB),
                  sb("scores_b", [P, TILES, PEER_HEADS, N_KEYS], F32, RAW)]
        pick = packer(ROWS, 24 * KB)
        left = pick("left", [P, PEER_HEADS, N_KEYS])
        cand = pick("cand", [P, 4, TOPK * TOPK])
        onehot = pick("onehot", [P, 4 * TOPK, TOPK])
        cand_left = left[:, :, :].rearrange("p (h a) b -> p h (a b)", a=2)
        sv = pick("sv", [P, PEER_HEADS, TOPK])
        si = pick("si", [P, PEER_HEADS, TOPK], U32)
        sif = pick("sif", [P, PEER_HEADS, TOPK])
        tops = pick("tops", [P, 4, TOPK])
        topj = pick("topj", [P, 4, TOPK], U32)
        topa = pick("topa", [P, 4, TOPK], U32)
        topaf = pick("topaf", [P, 4, TOPK])
        rowid = pick("rowid", [P, 2, 4 * TOPK])
        eid = pick("eid", [P, 2 * TILES * PICKS + 2 * GATHER_SLOTS], U32)
        idx = pick("idx", [P, 2, GATHER_SLOTS], U32)
        gate = pick("gate", [P, TILES, PEER_HEADS, TOPK])
        gsum = pick("gsum", [P, 4])
        dots = pick("dots", [P, 2, GATHER_SLOTS])
        act_ = pick("act_", [P, TILES * PICKS])
        wgt = pick("wgt", [P, TILES * PICKS])
        vacc = sb("vacc", [P, 2, D], F32, T2 + 16 * KB)
        row_g2 = sb("row_g2", [P, D], F32, T2)
        row_b2 = sb("row_b2", [P, D], F32, T2 + 8 * KB)
        ring = sb("ring", [P, GATHER_SLOTS, D], F32, T1)

        ps = [ctx.enter_context(nc.psum_tensor(f"half{n}", [P, 4, BANK], F32)) for n in range(2)]
        flat = [t[:, :, :].rearrange("p b n -> p (b n)") for t in ps]
        by_tile = [t[:, :, :].rearrange("p (t b) n -> p t (b n)", t=TILES) for t in ps]
        by_128 = [f.rearrange("p (k t) -> p k t", t=P) for f in flat]
        by_tok = [f.rearrange("p (k t) -> p k t", t=TOKENS) for f in flat]

        def sem(name):
            return ctx.enter_context(nc.semaphore(name))

        half_filled = [sem("half_filled_a"), sem("half_filled_b")]
        half_free = [sem("half_free_a"), sem("half_free_b")]
        raw_landed = [sem(f"raw_landed{n}") for n in range(RAW_SLOTS)]
        hi_done = sem("hi_done")
        split_done = sem("split_done")
        products = sem("products")
        dve_step = sem("dve_step")
        act_step = sem("act_step")
        pool_step = sem("pool_step")
        consts_done = sem("consts_done")
        xT_hi = sem("xT_hi")
        loaded = {n: sem("loaded_" + n) for n in (
            "x", "ws", "params", "row_norm", "row_v", "row_norm1", "rows_mix", "wg", "gate", "mh", "rows_ln1", "keys",
            "rows_ln2")}
        xg_ready = sem("xg_ready")
        squares = sem("squares")
        stat = sem("stat")
        rooted = sem("rooted")
        rstd_ready = sem("rstd_ready")
        v_squared = sem("v_squared")
        v_normed = sem("v_normed")
        z_used = sem("z_used")
        abs_done = sem("abs_done")
        ln_done = sem("ln_done")
        sp_done = sem("sp_done")
        la_done = sem("la_done")
        a_done = sem("a_done")
        ay_done = sem("ay_done")
        wg_hi = sem("wg_hi")
        wg_done = sem("wg_done")
        gate_abs = sem("gate_abs")
        gate_ln = sem("gate_ln")
        logf_done = sem("logf_done")
        cc_done = sem("cc_done")
        G_done = sem("G_done")
        mw_done = sem("mw_done")
        mw_masked = sem("mw_masked")
        m_exp = sem("m_exp")
        mv_ones = sem("mv_ones")
        zT_pad = sem("zT_pad")
        hm_sq = sem("hm_sq")
        hm_root = sem("hm_root")
        ym_done = sem("ym_done")
        yc_done = sem("yc_done")
        yc_hi = sem("yc_hi")
        yc_lo = sem("yc_lo")
        gate_sub = sem("gate_sub")
        gate_exp = sem("gate_exp")
        idx_ready = [sem("idx_ready0"), sem("idx_ready1")]
        row_landed = [sem(f"row_landed{n}") for n in range(GATHER_SLOTS)]
        rows_used = sem("rows_used")
        eid_pad = sem("eid_pad")
        gelu_done = sem("gelu_done")
        y_stored = sem("y_stored")
        out_ready = sem("out_ready")

        block = ctx.enter_context(nc.Block())

        def is_free(eng, unit):
            half, n = NTH[unit]
            if n:
                eng.wait_ge(half_free[half], n)

        def is_filled(eng, unit):
            eng.wait_ge(half_filled[NTH[unit][0]], FILL[unit])

        def is_emptied(eng, unit):
            half, n = NTH[unit]
            eng.wait_ge(half_free[half], n + 1)

        def halves(unit):
            return NTH[unit][0]

        def step_counter(eng, s):
            count = [0]

            def step(ins):
                count[0] += 1
                ins.then_inc(s, 1)
                eng.wait_ge(s, count[0])
            return step

        @block.sync
        def _(sp):
            for t in range(TILES):
                sp.dma_start(h[:, t, :], x[0, t * P:(t + 1) * P, :]).then_inc(loaded["x"], 16)

            def load_block(w, c, col, kts=KT):
                for k in range(kts):
                    if not (isinstance(c, int) and c + k < RAW_SLOTS):
                        sp.wait_ge(split_done, c + (k + 1 - RAW_SLOTS))
                    sp.dma_start(w_raw[:, k % RAW_SLOTS, :], w[k * P:(k + 1) * P, bass.ds(col, COLS)])\
                        .then_inc(raw_landed[k % RAW_SLOTS], 16)

            def load_pairs(w, stage, col, pairs):
                c = FIRST[stage + "0"]
                with sp.Fori(0, pairs) as i:
                    for n in range(2):
                        load_block(w, i * (2 * KT) + (c + n * KT), i * (2 * COLS) + (col + n * COLS))

            for n in range(4):
                load_block(a_w_in[0], FIRST[f"gmlp_v{n}"], GMLP_W + n * COLS)
            load_pairs(a_w_in[0], "gmlp_u", 0, 2)
            load_pairs(a_w_in[0], "gmlp_z", 2 * GMLP_W, 2)
            for n in range(2):
                load_block(a_w_out[0], FIRST[f"gmlp_out{n}"], n * COLS, 2 * KT)
            load_pairs(b_w_in[0], "att_q", 0, 4)
            load_pairs(b_w_out[0], "att_out", 0, 1)
            for name, (_, b) in MIX_IN.items():
                load_block(w_in_2[0], FIRST[name], b * COLS)
            load_pairs(w_out_2[0], "mix_out", 0, 1)
            load_pairs(peer_wq_2[0], "peer_q", 0, 1)
            for t in range(TILES):
                sp.wait_ge(out_ready, t + 1)
                sp.dma_start(out[0, t * P:(t + 1) * P, :], h[:, t, :]).then_inc(y_stored, 16)
            sp.wait_ge(y_stored, 16 * TILES)

        @block.gpsimd
        def _(pool):
            step = step_counter(pool, pool_step)

            def row(dst, src, name):
                pool.dma_start(dst, src.partition_broadcast(P)).then_inc(loaded[name], 16)

            row(row_norm[:, :], norm_g[0], "row_norm")

            def triangle(m, base, fill, op, cm, st):
                step(nc.gpsimd.memset(m[:, :], base))
                step(nc.gpsimd.affine_select(out=m[:, :], in_=m[:, :], compare_op=op, fill=fill, base=0,
                                             pattern=[[st, P]], channel_multiplier=cm))
            triangle(ident, 0.0, 1.0, ALU.not_equal, 1, -1)
            step(nc.gpsimd.memset(ones[:, :], 1.0))
            nc.gpsimd.iota(iota16[:, :], pattern=[[1, TOPK]], base=0, channel_multiplier=0,
                           allow_small_or_imprecise_dtypes=True).then_inc(consts_done, 1)
            triangle(upto, 1.0, 0.0, ALU.is_ge, -1, 1)
            triangle(onward, 1.0, 0.0, ALU.is_ge, 1, -1)
            triangle(before, 1.0, 0.0, ALU.is_gt, -1, 1)
            step(nc.gpsimd.memset(barred[:, :], 0.0))
            nc.gpsimd.affine_select(out=barred[:, :], in_=barred[:, :], compare_op=ALU.is_gt, fill=NEG, base=0,
                                    pattern=[[1, P]], channel_multiplier=-1).then_inc(consts_done, 1)
            pool.dma_start(param_rows[0:16, :], a_b_s[0]).then_inc(loaded["params"], 16)
            pool.dma_start(param_rows[16:40, :], conv_w_2[0].rearrange("j (f p) -> (j f) p", p=P))\
                .then_inc(loaded["params"], 16)
            pool.dma_start(param_rows[40:48, :], conv_b_2[0].rearrange("(f p) -> f p", p=P))\
                .then_inc(loaded["params"], 16)
            pool.dma_start(ws_raw[:, :, :], a_w_s[0].rearrange("g t s -> t g s")).then_inc(loaded["ws"], 16)
            row(row_v[:, :], a_v_norm_g[0], "row_v")
            row(row_gate[:, :], b_gate_2[0], "gate")

            pool.wait_ge(xg_ready, 4)
            row(row_norm[:, :], norm_g[1], "row_norm1")
            is_emptied(pool, "O3")
            row(row_a[:, :], final_g, "rows_mix")
            row(row_b[:, :], ln_in_g_2, "rows_mix")
            row(row_c[:, :], ln_in_b_2, "rows_mix")
            pool.wait_ge(products, FIRST["att_out1"] + KT)
            pool.dma_start(wg_raw[:, :, :], w_in_2[0, :, 7 * D_HALF:].rearrange("(k p) n -> p k n", p=P))\
                .then_inc(loaded["wg"], 16)
            pool.wait_ge(xg_ready, 6 + 4)
            row(row_mh[:, :], mh_norm_g_2[0], "mh")
            is_emptied(pool, "ymT")
            row(row_a[:, :], ln1_g_2[0], "rows_ln1")
            row(row_b[:, :], ln1_b_2[0], "rows_ln1")
            pool.dma_start(keys_raw[:, :, :], peer_keys_2[0].rearrange("h s n c -> n (h s) c"))\
                .then_inc(loaded["keys"], 16)

            BODY = 2 * GATHER_SLOTS
            for table, base in ((peer_u_2[0], 0), (peer_v_2[0], TILES * PICKS)):
                with pool.Fori(0, TILES * PICKS // BODY) as i:
                    for n in range(BODY):
                        b, s = divmod(n, GATHER_SLOTS)
                        if s == 0:
                            pool.wait_ge(idx_ready[b], i + (base // BODY + 1))
                        if s == GATHER_SLOTS // 2:
                            pool.wait_ge(products, CHUNKS)
                        pool.wait_ge(rows_used, i * BODY + (base + n + 1))
                        pool.nop(nofuse=True)
                        nc.gpsimd.indirect_dma_start(
                            out=ring[:, s, :], out_offset=None, in_=table,
                            in_offset=bass.IndirectOffsetOnAxis(ap=idx[:, b, s:s + 1], axis=0),
                        ).then_inc(row_landed[s], 16)
                if base == 0:
                    row(row_g2[:, :], ln2_g_2[0], "rows_ln2")
                    row(row_b2[:, :], ln2_b_2[0], "rows_ln2")

        @block.tensor
        def _(pe):
            mm = nc.tensor.matmul

            def multiply(half, c, xts, at):
                kts = KT * len(xts)
                for k in range(kts):
                    pe.wait_ge(split_done, c + (k + 1))
                    xt, kk, s = xts[k // KT], k % KT, k % SPLIT_SLOTS
                    for t in range(TILES):
                        tok = slice(t * P, (t + 1) * P)
                        for xp, wp in ((0, 0), (0, 1), (1, 0)):
                            for n in range(2):
                                last = mm(ps[half][:, 2 * t + n, :], xt[:, xp, kk, tok],
                                          w_split[:, s, wp, n * BANK:(n + 1) * BANK],
                                          start=(k == 0 and xp == 0 and wp == 0), stop=(k == kts - 1 and xp == 1))
                    last.then_inc(products, 1)
                    for job in at.get(k, ()):
                        job()

            def block_of(unit, xts, at={}):
                is_free(pe, unit)
                multiply(halves(unit), FIRST[unit], xts, at)

            def filled_by(last, unit):
                last.then_inc(half_filled[halves(unit)], 1)

            def turn(unit, tiles):
                is_free(pe, unit)
                hf = halves(unit)
                for n, (src, rows) in enumerate(tiles):
                    last = nc.tensor.transpose(by_128[hf][:, n, 0:rows], src, ident[0:rows, 0:rows])
                filled_by(last, unit)

            def turn_tokens(unit, src, first, count):
                turn(unit, [(src[:, t, k * P:(k + 1) * P], P) for k in range(first, first + count) for t in range(TILES)])

            def turn_part(name, q, src, count):
                def job():
                    pe.wait_ge(xg_ready, count + 1)
                    turn_tokens(f"{name}{q}", src, 4 * q, 4)
                return job

            def emptied(*units):
                def job():
                    for unit in units:
                        is_emptied(pe, unit)
                return job

            pe.wait_ge(consts_done, 1)
            for q in range(4):
                turn_part("xT_gmlp", q, xg, q)()
            emptied("xT_gmlp0", "xT_gmlp1", "xT_gmlp2", "xT_gmlp3")()
            with pe.Fori(0, 2) as i:
                for n in range(2):
                    pe.wait_ge(half_free[n], i + NTH[f"gmlp_v{n}"][1])
                    multiply(n, i * (2 * KT) + FIRST[f"gmlp_v{n}"], (xT1,), {})

            def turn_ws():
                pe.wait_ge(loaded["ws"], 16)
                turn("ws", [(ws_raw[:, g, :], P) for g in range(GROUPS)])

            def turn_params():
                pe.wait_ge(loaded["params"], 48)
                turn("params", [(param_rows[:, :], 48)])

            def mix(u):
                def job():
                    unit = f"mix{u}"
                    pe.wait_ge(v_normed, TILES)
                    is_free(pe, unit)
                    hf = halves(unit)
                    for j in range(4):
                        g = 4 * u + j
                        for n in range(TILES):
                            last = mm(ps[hf][:, j, n * GROUP_DIM:(n + 1) * GROUP_DIM], wsT[:, g, :],
                                      gv[:, n, g * GROUP_DIM:(g + 1) * GROUP_DIM], start=True, stop=True)
                    filled_by(last, unit)
                return job

            def turn_y(u):
                def job():
                    pe.wait_ge(z_used, u + 2)
                    turn_tokens(f"yT_gmlp{u}", gu, 8 * u, 8)
                return job

            block_of("gmlp_u0", (xT1,), {3: [turn_ws], 6: [turn_params]})
            block_of("gmlp_u1", (xT1,))
            block_of("gmlp_u2", (xT1,), {4: [mix(0)], 9: [mix(1)]})
            block_of("gmlp_u3", (xT1,), {4: [mix(2)]})
            block_of("gmlp_z0", (xT1,), {4: [mix(3)]})
            block_of("gmlp_z1", (xT1,), {4: [turn_y(0)]})
            block_of("gmlp_z2", (xT1,), {4: [turn_y(1)]})
            emptied("yT_gmlp0", "yT_gmlp1")()
            block_of("gmlp_z3", (xT1,))
            block_of("gmlp_out0", (xT2, xT1), {4: [turn_y(2)], 8: [turn_y(3)], 15: [emptied("yT_gmlp2")],
                                               23: [emptied("yT_gmlp3")]})

            def turn_xg(u, count):
                def job():
                    pe.wait_ge(xg_ready, count)
                    turn_tokens(f"xT_att{u}", xg, 8 * u, 8)
                return job

            def turn_qk(u):
                def job():
                    w, b = divmod(u, 2)
                    is_emptied(pe, ("att_q", "att_k")[w] + str(b))
                    turn_tokens(f"qkT{u}", (q_tok, k_tok)[w][:, b, :, :], 0, 8)
                return job

            def att_z(g):
                unit = f"Z{g}"
                if g == 0:
                    emptied("qkT0", "qkT1", "qkT2", "qkT3")()
                is_free(pe, unit)
                hf = halves(unit)
                for j in range(4):
                    n = 4 * g + j
                    mm(ps[hf][:, j, 0:TOKENS], qkT[:, 1, n, 0:P], qkT[:, 0, n, :], start=True, stop=True)
                    last = mm(ps[hf][:, j, TOKENS:ZW], qkT[:, 1, n, P:TOKENS], qkT[:, 0, n, P:TOKENS],
                              start=True, stop=True)
                filled_by(last, unit)

            def att_l(g):
                unit = f"L{g}"
                pe.wait_ge(sp_done, g + 1)
                is_free(pe, unit)
                hf = halves(unit)
                for j in range(4):
                    s = sp_[:, g % 2, j, :]
                    mm(ps[hf][:, j, 0:TOKENS], onward[:, :], s[:, 0:TOKENS], start=True, stop=False)
                    mm(ps[hf][:, j, P:TOKENS], ones[:, 0:P], s[:, TOKENS:ZW], start=False, stop=True)
                    last = mm(ps[hf][:, j, TOKENS:ZW], onward[:, :], s[:, TOKENS:ZW], start=True, stop=True)
                filled_by(last, unit)

            def att_o(g):
                unit = f"O{g}"
                pe.wait_ge(a_done, g + 1)
                is_emptied(pe, f"att_v{g // 2}")
                is_free(pe, unit)
                hf = halves(unit)
                for j in range(4):
                    a = zs[:, g % 2, j, :]
                    c = (4 * g + j) * DH
                    mm(ps[hf][:, j, 0:DH], a[:, 0:P], av[:, 0, c:c + DH], start=True, stop=True)
                    mm(ps[hf][:, j, DH:2 * DH], a[:, P:TOKENS], av[:, 0, c:c + DH], start=True, stop=False)
                    last = mm(ps[hf][:, j, DH:2 * DH], a[:, TOKENS:ZW], av[:, 1, c:c + DH], start=False, stop=True)
                filled_by(last, unit)

            def turn_ay(u):
                def job():
                    pe.wait_ge(ay_done, u + 1)
                    turn_tokens(f"yT_att{u}", ay[:, u, :, :], 0, 8)
                return job

            block_of("gmlp_out1", (xT2, xT1), {18: [turn_xg(0, 5)]})
            is_emptied(pe, "xT_att0")
            block_of("att_q0", (xT2,), {4: [turn_xg(1, 6)], 7: [emptied("xT_att1")]})
            block_of("att_q1", (xT2,), {4: [turn_qk(0)]})
            block_of("att_k0", (xT2,), {4: [turn_qk(1)]})
            block_of("att_k1", (xT2,), {4: [turn_qk(2)]})
            block_of("att_v0", (xT2,), {4: [turn_qk(3)]})
            block_of("att_v1", (xT2,))
            block_of("att_z0", (xT2,), {0: [lambda: att_z(0)], 2: [lambda: att_z(1)], 5: [lambda: att_l(0)],
                                        8: [lambda: att_o(0)], 10: [lambda: att_l(1)], 12: [lambda: att_z(2)],
                                        15: [lambda: att_o(1)]})
            block_of("att_z1", (xT2,), {2: [lambda: att_l(2)], 4: [lambda: att_z(3)], 7: [lambda: att_o(2)],
                                        9: [lambda: att_l(3)], 12: [lambda: att_o(3)], 14: [turn_ay(0)]})
            is_emptied(pe, "yT_att0")
            block_of("att_out0", (xT1,), {4: [turn_ay(1)], 7: [emptied("yT_att1")]})
            block_of("att_out1", (xT1,))

            def normed_block(unit, name, count, at):
                parts = [turn_part(name, q, h, count + q) for q in range(4)]
                parts[0]()
                parts[1]()
                is_emptied(pe, f"{name}0")
                jobs = {0: [parts[2]], 3: [emptied(f"{name}1"), parts[3]], 7: [emptied(f"{name}2")],
                        11: [emptied(f"{name}3")]}
                for k, more in at.items():
                    jobs.setdefault(k, []).extend(more)
                block_of(unit, (xT2,), jobs)

            def turn_heads(unit, src, after):
                def job():
                    is_emptied(pe, after)
                    turn_tokens(unit, src, 0, M_HEADS)
                return job

            def gate_products():
                pe.wait_ge(wg_done, 1)
                is_free(pe, "gates")
                hf = halves("gates")
                for t in range(TILES):
                    for k in range(KT):
                        for xp, wp in ((0, 0), (0, 1), (1, 0)):
                            last = mm(ps[hf][:, t, 0:16], xT2[:, xp, k, t * P:(t + 1) * P], wg_split[:, wp, k, :],
                                      start=(k == 0 and xp + wp == 0), stop=(k == KT - 1 and xp == 1))
                filled_by(last, "gates")

            def cumulate():
                pe.wait_ge(logf_done, 1)
                is_free(pe, "cum")
                hf = halves("cum")
                mm(ps[hf][:, 0, 0:M_HEADS], upto[:, :], logf[:, 0, :], start=True, stop=True)
                mm(ps[hf][:, 1, 0:M_HEADS], upto[:, :], logf[:, 1, :], start=True, stop=False)
                filled_by(mm(ps[hf][:, 1, 0:M_HEADS], ones[:, 0:P], logf[:, 0, :], start=False, stop=True), "cum")

            def turn_c():
                pe.wait_ge(cc_done, 1)
                is_free(pe, "cT")
                hf = halves("cT")
                for t in range(TILES):
                    last = nc.tensor.transpose(ps[hf][0:M_HEADS, 0, t * P:(t + 1) * P], cc[:, t, :], ident[:, :])
                filled_by(last, "cT")

            def spread_g():
                pe.wait_ge(G_done, 1)
                is_free(pe, "G_rows")
                hf = halves("G_rows")
                for n in range(M_HEADS):
                    last = mm(flat[hf][:, n * TOKENS:(n + 1) * TOKENS],
                              ident[0:M_HEADS, n:n + 1].to_broadcast([M_HEADS, P]), G[:, :], start=True, stop=True)
                filled_by(last, "G_rows")

            def turn_g():
                is_free(pe, "G_cols")
                hf = halves("G_cols")
                for t in range(TILES):
                    last = nc.tensor.transpose(ps[hf][:, t, 0:M_HEADS], G[:, t * P:(t + 1) * P],
                                               ident[0:M_HEADS, 0:M_HEADS])
                filled_by(last, "G_cols")

            def m_scores(g):
                unit = f"MS{g}"
                emptied("mqT", "mkT")()
                is_free(pe, unit)
                hf = halves(unit)
                for j in range(4):
                    n = 4 * g + j
                    mm(ps[hf][:, j, 0:TOKENS], mqkT[:, 1, n, 0:P], mqkT[:, 0, n, :], start=True, stop=True)
                    last = mm(ps[hf][:, j, TOKENS:ZW], mqkT[:, 1, n, P:TOKENS], mqkT[:, 0, n, P:TOKENS],
                              start=True, stop=True)
                filled_by(last, unit)

            def m_out(g):
                unit = f"MO{g}"
                emptied(f"MS{g}", "mix_v")()
                pe.wait_ge(mv_ones, 1)
                is_free(pe, unit)
                hf = halves(unit)
                for j in range(4):
                    n, a = 4 * g + j, ms[:, g, j, :]
                    E = DH + 1
                    mm(ps[hf][:, j, 0:E], a[:, 0:P], mv[:, 0, n, :], start=True, stop=True)
                    mm(ps[hf][:, j, E:2 * E], a[:, P:TOKENS], mv[:, 0, n, :], start=True, stop=False)
                    last = mm(ps[hf][:, j, E:2 * E], a[:, TOKENS:ZW], mv[:, 1, n, :], start=False, stop=True)
                filled_by(last, unit)

            def turn_ym():
                pe.wait_ge(ym_done, 1)
                turn_tokens("ymT", hm[:, :, :, :].rearrange("p t n d -> p t (n d)"), 0, M_HEADS)

            normed_block("mix_q", "xT_mix", 6, {})
            block_of("mix_k", (xT2,), {4: [turn_heads("mqT", mqk_tok[:, 0, :, :], "mix_q")], 7: [gate_products],
                                       12: [cumulate]})
            block_of("mix_v", (xT2,), {4: [turn_heads("mkT", mqk_tok[:, 1, :, :], "mix_k")], 6: [turn_c], 8: [spread_g],
                                       12: [turn_g]})
            block_of("mix_cC", (xT2,), {4: [lambda: m_scores(0)], 7: [lambda: m_scores(1)], 10: [lambda: m_out(0)],
                                        13: [lambda: m_out(1)]})
            block_of("mix_ch", (xT2,))
            block_of("mix_cB", (xT2,), {4: [turn_heads("zT", cz, "mix_ch")]})
            block_of("mix_o", (xT2,), {4: [turn_heads("cBT", cB, "mix_cB")]})
            pe.wait_ge(yc_lo, 1)
            block_of("mix_out0", (xT1,), {4: [turn_ym], 7: [emptied("ymT")]})
            block_of("mix_out1", (xT1,))

            def turn_keys():
                pe.wait_ge(loaded["keys"], 16)
                turn("keysT", [(keys_raw[:, n, :], P) for n in range(2 * PEER_HEADS)])

            def turn_pq(u):
                def job():
                    is_emptied(pe, f"peer_q{u}")
                    turn_tokens(f"pqT{u}", pq_tok[:, u, :, :], 0, 8)
                return job

            def score(u):
                def job():
                    unit = f"scores{u}"
                    emptied(f"pqT{u}", "keysT")()
                    is_free(pe, unit)
                    hf = halves(unit)
                    for t in range(TILES):
                        for n in range(8):
                            last = mm(by_128[hf][:, 8 * t + n, :], pqT[:, 8 * u + n, t * P:(t + 1) * P],
                                      keysT[:, 8 * u + n, :], start=True, stop=True)
                    filled_by(last, unit)
                return job

            normed_block("peer_q0", "xT_peer", 10, {8: [turn_keys]})
            block_of("peer_q1", (xT2,), {3: [turn_pq(0)], 5: [score(0)]})
            turn_pq(1)()
            score(1)()

        @block.scalar
        def _(act):
            fn = nc.scalar.activation
            step = step_counter(act, act_step)
            root_count = [0]
            square_count = [0]

            def round_hi(c, k):
                act.wait_ge(raw_landed[k % RAW_SLOTS], c * (16 // RAW_SLOTS) + 16 * (k // RAW_SLOTS + 1))
                if not (isinstance(c, int) and c + k < SPLIT_SLOTS):
                    act.wait_ge(products, c + (k + 1 - SPLIT_SLOTS))
                fn(w_split[:, k % SPLIT_SLOTS, 0, :], w_raw[:, k % RAW_SLOTS, :], ACT.Copy).then_inc(hi_done, 1)

            def through(c, kts=KT, at={}, last=False):
                for k in range(kts):
                    if not (last and k + AHEAD >= kts):
                        round_hi(c, k + AHEAD)
                    for job in at.get(k, ()):
                        job()
                act.wait_ge(products, c + kts)

            def block_of(unit, kts=KT, at={}, last=False):
                through(FIRST[unit], kts, at, last)

            def hi_x(unit, dst, count):
                def job():
                    is_filled(act, unit)
                    fn(dst[:, 0, :, :], by_tok[halves(unit)][:, 0:count, :], ACT.Copy).then_inc(xT_hi, 1)
                return job

            def take(unit, dst, src, func=ACT.Copy, **kw):
                fn(dst, src, func, **kw).then_inc(half_free[halves(unit)], 1)

            def take_scaled(hf, dst, func, scales):
                for t in range(TILES):
                    ins = fn(dst[t], by_tile[hf][:, t, :], func, scale=scales[:, t:t + 1])
                ins.then_inc(half_free[hf], 1)

            def copy_out(unit, dst, func=ACT.Copy):
                def job():
                    is_filled(act, unit)
                    take(unit, dst, flat[halves(unit)], func)
                return job

            def root_next():
                root_count[0] += 1
                act.wait_ge(stat, root_count[0])
                fn(root[:, :], meansq[:, :], ACT.Sqrt).then_inc(rooted, 1)

            def sum_squares(src, part, trash):
                for t in range(TILES):
                    if square_count[0]:
                        act.wait_ge(squares, square_count[0])
                    square_count[0] += 1
                    fn(trash, src[:, t, :], ACT.Square, accum_out=sumsq[:, t, part:part + 1]).then_inc(squares, 1)

            for k in range(AHEAD):
                round_hi(0, k)
            act.wait_ge(loaded["x"], 16 * TILES)
            sum_squares(h[:, :, :], 0, x_trash[:, :])
            for q in range(4):
                hi_x(f"xT_gmlp{q}", xT1[:, :, 4 * q:4 * q + 4, :], 4)()
            root_next()
            act.wait_ge(rstd_ready, 1)
            with act.Fori(0, 2) as i:
                for n in range(2):
                    through(i * (2 * KT) + FIRST[f"gmlp_v{n}"])
                    cut = bass.ds(i * (2 * COLS) + n * COLS, COLS)
                    take_scaled(n, [gv[:, t, cut] for t in range(TILES)], ACT.Gelu_apprx_tanh, rstd)
            for n in range(4):
                block_of(f"gmlp_u{n}", at={14: [root_next]} if n == 0 else {})
                take_scaled(n % 2, [gu[:, t, n * COLS:(n + 1) * COLS] for t in range(TILES)], ACT.Gelu_apprx_tanh, rstd)
            for n in range(4):
                jobs = {}
                if n in (1, 2):
                    jobs = {4: [hi_x(f"yT_gmlp{n - 1}", xT2[:, :, 8 * (n - 1):8 * n, :], 8)]}
                block_of(f"gmlp_z{n}", at=jobs)
                act.wait_ge(z_used, n + 1)
                take_scaled(n % 2, [gz[:, t, :] for t in range(TILES)], ACT.Silu, rstd)
            block_of("gmlp_out0", 2 * KT, {4: [hi_x("yT_gmlp2", xT1[:, :, 0:8, :], 8)],
                                           8: [hi_x("yT_gmlp3", xT1[:, :, 8:16, :], 8)]})

            def att_squares(b):
                def job():
                    is_emptied(act, f"gmlp_out{b}")
                    sum_squares(h[:, :, b * COLS:(b + 1) * COLS], b, q_trash[:, :])
                return job

            block_of("gmlp_out1", 2 * KT, {2: [att_squares(0)], 18: [hi_x("xT_att0", xT2[:, :, 0:8, :], 8)]})
            block_of("att_q0", at={1: [att_squares(1)], 4: [hi_x("xT_att1", xT2[:, :, 8:16, :], 8)], 6: [root_next]})
            act.wait_ge(rstd_ready, 2)
            take_scaled(A, [q_tok[:, 0, t, :] for t in range(TILES)], ACT.Copy, rstd_q)

            def qk_turned(u):
                w, b = divmod(u, 2)
                return copy_out(f"qkT{u}", qkT[:, w, 8 * b:8 * b + 8, :].rearrange("p n t -> p (n t)"))

            block_of("att_q1", at={4: [qk_turned(0)]})
            take_scaled(B, [q_tok[:, 1, t, :] for t in range(TILES)], ACT.Copy, rstd_q)
            for b in range(2):
                block_of(f"att_k{b}", at={4: [qk_turned(1 + b)]})
                take_scaled(b, [k_tok[:, b, t, :] for t in range(TILES)], ACT.Copy, rstd)
            for b in range(2):
                block_of(f"att_v{b}", at={4: [qk_turned(3)]} if b == 0 else {})
                take_scaled(b, [av[:, t, b * COLS:(b + 1) * COLS] for t in range(TILES)], ACT.Copy, rstd)

            def att_copy(g):
                unit = f"Z{g}"
                is_filled(act, unit)
                if g >= 2:
                    is_emptied(act, f"O{g - 2}")
                take(unit, zs[:, g % 2, :, :], ps[halves(unit)][:, :, 0:ZW])

            def att_ln(g):
                act.wait_ge(abs_done, g + 1)
                s = sp_[:, g % 2, :, :]
                step(fn(s, s, ACT.Exp, scale=-1.0))
                fn(s, s, ACT.Ln, bias=1.0).then_inc(ln_done, 1)

            def att_exp(g):
                act.wait_ge(la_done, g + 1)
                z = zs[:, g % 2, :, :]
                fn(z, z, ACT.Exp).then_inc(a_done, 1)

            block_of("att_z0", at={0: [lambda: att_copy(0)], 1: [lambda: att_ln(0)], 2: [lambda: att_copy(1)],
                                   3: [lambda: att_ln(1)], 5: [lambda: att_exp(0)], 10: [lambda: att_exp(1)],
                                   12: [lambda: att_copy(2)], 13: [lambda: att_ln(2)]})
            take_scaled(A, [az[:, 0, t, :] for t in range(TILES)], ACT.Silu, rstd)
            block_of("att_z1", at={2: [lambda: att_exp(2)], 4: [lambda: att_copy(3)], 5: [lambda: att_ln(3)],
                                   9: [lambda: att_exp(3)], 14: [hi_x("yT_att0", xT1[:, :, 0:8, :], 8)]})
            take_scaled(A, [az[:, 1, t, :] for t in range(TILES)], ACT.Silu, rstd)
            block_of("att_out0", at={4: [hi_x("yT_att1", xT1[:, :, 8:16, :], 8)]})

            def mix_squares(b):
                def job():
                    is_emptied(act, f"att_out{b}")
                    sum_squares(h[:, :, b * COLS:(b + 1) * COLS], b, p_trash[:, :])
                return job

            def normed_parts(name):
                return [hi_x(f"{name}{q}", xT2[:, :, 4 * q:4 * q + 4, :], 4) for q in range(4)]

            block_of("att_out1", at={2: [mix_squares(0)]})
            mix_squares(1)()
            root_next()

            def gate_hi():
                act.wait_ge(loaded["wg"], 16)
                fn(wg_split[:, 0, :, :], wg_raw[:, :, :], ACT.Copy).then_inc(wg_hi, 1)

            def gate_log():
                act.wait_ge(gate_abs, 1)
                step(fn(gabs[:, :, :], gabs[:, :, :], ACT.Exp, scale=-1.0))
                fn(gabs[:, :, :], gabs[:, :, :], ACT.Ln, bias=1.0).then_inc(gate_ln, 1)

            def m_weights():
                is_emptied(act, "G_rows")
                fn(mw[:, :, :], mw[:, :, :], ACT.Exp, scale=-1.0).then_inc(mw_done, 1)

            def m_floor():
                is_emptied(act, "G_cols")
                fn(cmin[:, :, :], cmin[:, :, :], ACT.Exp, scale=-1.0).then_inc(m_exp, 1)

            def turned(unit, dst):
                return copy_out(unit, dst.rearrange("p n t -> p (n t)"))

            def head_root():
                act.wait_ge(hm_sq, 1)
                fn(mrs[:, :, :], mrs[:, :, :], ACT.Sqrt).then_inc(hm_root, 1)

            def conv_hi():
                act.wait_ge(yc_done, 1)
                fn(xT1[:, 0, 0:8, :], yc[:, :, :], ACT.Copy).then_inc(yc_hi, 1)

            parts = normed_parts("xT_mix")
            parts[0]()
            parts[1]()
            block_of("mix_q", at={0: [parts[2]], 3: [parts[3]], 8: [gate_hi]})
            take("mix_q", mqk_tok[:, 0, :, :], by_tile[A], scale=DH ** -0.5)
            block_of("mix_k", at={4: [turned("mqT", mqkT[:, 0, :, :])], 9: [gate_log]})
            take("mix_k", mqk_tok[:, 1, :, :], by_tile[B])
            block_of("mix_v", at={4: [turned("mkT", mqkT[:, 1, :, :])], 11: [m_weights], 14: [m_floor]})
            take("mix_v", mv[:, :, :, 0:DH], by_tile[A].rearrange("p t (n d) -> p t n d", d=DH))
            block_of("mix_cC")
            take("mix_cC", cz[:, :, :], by_tile[B])
            block_of("mix_ch", at={11: [head_root]})
            block_of("mix_cB", at={4: [lambda: (is_filled(act, "zT"),
                                                take("zT", zT[:, :, 2:], by_tok[halves("zT")]))]})
            take("mix_cB", cB[:, :, :], by_tile[B])
            block_of("mix_o", at={4: [turned("cBT", cBT[:, :, :])], 7: [conv_hi]})
            take("mix_o", mo[:, :, :], by_tile[A], ACT.Sigmoid)
            block_of("mix_out0", at={4: [hi_x("ymT", xT1[:, :, 8:16, :], 8)]})
            block_of("mix_out1")
            root_next()

            parts = normed_parts("xT_peer")
            parts[0]()
            parts[1]()
            block_of("peer_q0", at={0: [parts[2]], 3: [parts[3]], 8: [turned("keysT", keysT[:, :, :])]})
            take("peer_q0", pq_tok[:, 0, :, :], by_tile[A])

            def scores_out(u):
                return copy_out(f"scores{u}", scores[u][:, :, :, :].rearrange("p t n k -> p (t n k)"))

            block_of("peer_q1", at={3: [turned("pqT0", pqT[:, 0:8, :])], 5: [scores_out(0)]}, last=True)
            take("peer_q1", pq_tok[:, 1, :, :], by_tile[B])
            turned("pqT1", pqT[:, 8:16, :])()
            scores_out(1)()
            for n in range(2 * TILES):
                g, t = divmod(n, TILES)
                act.wait_ge(gate_sub, n + 1)
                cut = gate[:, t, 4 * g:4 * g + 4, :]
                fn(cut, cut, ACT.Exp).then_inc(gate_exp, 1)
            for n in range(2 * TILES):
                g, t = divmod(n, TILES)
                act.wait_ge(idx_ready[1], (n + 1) * GROUP_PICKS // (2 * GATHER_SLOTS) + 1)
                fn(wgt[:, (2 * t + g) * GROUP_PICKS:(2 * t + g + 1) * GROUP_PICKS],
                   act_[:, n * GROUP_PICKS:(n + 1) * GROUP_PICKS], ACT.Gelu).then_inc(gelu_done, 1)
            for t in range(TILES):
                root_next()

        @block.vector
        def _(dve):
            v = nc.vector
            step = step_counter(dve, dve_step)
            xt_count = [0]
            root_count = [0]
            rstd_count = [0]

            def split_lo(c, k):
                dve.wait_ge(hi_done, c + (k + 1))
                s = k % SPLIT_SLOTS
                v.tensor_tensor(w_split[:, s, 1, :], w_raw[:, k % RAW_SLOTS, :], w_split[:, s, 0, :].bitcast(F32),
                                ALU.subtract).then_inc(split_done, 1)

            def through(c, kts=KT, at={}, last=False):
                for k in range(kts):
                    if not (last and k + AHEAD >= kts):
                        split_lo(c, k + AHEAD)
                    for job in at.get(k, ()):
                        job()

            def block_of(unit, kts=KT, at={}, last=False):
                through(FIRST[unit], kts, at, last)

            def lo_x(unit, dst, count):
                def job():
                    xt_count[0] += 1
                    dve.wait_ge(xT_hi, xt_count[0])
                    hf = halves(unit)
                    v.tensor_tensor(dst[:, 1, :, :], by_tok[hf][:, 0:count, :], dst[:, 0, :, :].bitcast(F32), ALU.subtract)\
                        .then_inc(half_free[hf], 1)
                return job

            def gained(dst, src, gain, lo, hi):
                return v.tensor_tensor(dst[:, :, lo:hi], src[:, :, lo:hi],
                                       gain[:, lo:hi].unsqueeze(1).to_broadcast([P, TILES, hi - lo]), ALU.mult)

            def mean_square(parts, width, count):
                dve.wait_ge(squares, count)
                total = sumsq[:, :, 0]
                if parts == 2:
                    total = meansq[:, :]
                    step(v.tensor_tensor(total, sumsq[:, :, 0], sumsq[:, :, 1], ALU.add))
                return v.tensor_scalar(meansq[:, :], total, 1.0 / width, RMS_EPS, ALU.mult, ALU.add)

            def inverse_root(dst):
                root_count[0] += 1
                dve.wait_ge(rooted, root_count[0])
                return v.reciprocal(dst, root[:, :])

            def add_to_h(unit, scale=1.0):
                n, hf = int(unit[-1]), halves(unit)
                dst = h[:, :, n * COLS:(n + 1) * COLS]
                v.scalar_tensor_tensor(out=dst, in0=dst, scalar=scale, in1=by_tile[hf], op0=ALU.mult, op1=ALU.add)\
                    .then_inc(half_free[hf], 1)
                is_emptied(dve, unit)

            def block_stats(src, b):
                for t in range(TILES):
                    for n in (2 * b, 2 * b + 1):
                        ins = v.bn_stats(bn[:, t, n, :], src[:, t, n * BANK:(n + 1) * BANK])
                return ins

            def tile_moments(t):
                return v.bn_aggr(moments[:, t, :], bn[:, t, :, :].rearrange("p n s -> p (n s)"))

            def normalise(src, t, lo, hi):
                return v.tensor_scalar(h[:, t, lo:hi], src[:, t, lo:hi], moments[:, t, 0:1], rstd[:, t:t + 1],
                                       ALU.subtract, ALU.mult)

            def norm_quarter(q, src, gain, bias):
                def job():
                    lo, hi = q * BANK, (q + 1) * BANK
                    for t in range(TILES):
                        ins = normalise(src, t, lo, hi)
                    step(ins)
                    step(gained(h, h, gain, lo, hi))
                    cut = h[:, :, lo:hi]
                    v.tensor_tensor(cut, cut, bias[:, lo:hi].unsqueeze(1).to_broadcast([P, TILES, BANK]), ALU.add)\
                        .then_inc(xg_ready, 1)
                return job

            def magnitude(dst, src):
                return v.scalar_tensor_tensor(out=dst, in0=src, scalar=-1.0, in1=src, op0=ALU.mult, op1=ALU.max)

            def both(*jobs):
                return list(jobs)

            for k in range(AHEAD):
                split_lo(0, k)
            dve.wait_ge(loaded["x"], 16 * TILES)
            dve.wait_ge(loaded["row_norm"], 16)
            for q in range(4):
                gained(xg, h, row_norm, q * BANK, (q + 1) * BANK).then_inc(xg_ready, 1)
            mean_square(1, D, TILES).then_inc(stat, 1)
            for q in range(4):
                lo_x(f"xT_gmlp{q}", xT1[:, :, 4 * q:4 * q + 4, :], 4)()
            inverse_root(rstd[:, :]).then_inc(rstd_ready, 1)
            with dve.Fori(0, 2) as i:
                for n in range(2):
                    through(i * (2 * KT) + FIRST[f"gmlp_v{n}"])

            def causal_ws():
                is_filled(dve, "ws")
                dve.wait_ge(consts_done, 2)
                hf = halves("ws")
                v.tensor_tensor(wsT[:, :, :], by_128[hf], upto[:, :].unsqueeze(1).to_broadcast([P, GROUPS, P]), ALU.mult)\
                    .then_inc(half_free[hf], 1)

            def take_params():
                is_filled(dve, "params")
                hf = halves("params")
                v.tensor_copy(cols[:, :], flat[hf][:, 0:48]).then_inc(half_free[hf], 1)

            def v_square(n):
                def job():
                    t, part = divmod(n, 2)
                    is_emptied(dve, "gmlp_v2")
                    is_emptied(dve, "gmlp_v3")
                    if n:
                        dve.wait_ge(v_squared, n)
                    src = gv[:, t, part * D:(part + 1) * D]
                    v.tensor_tensor_reduce(out=gz[:, :, :].rearrange("p a b -> p (a b)"), in0=src, in1=src, scale=1.0,
                                           scalar=0.0, op0=ALU.mult, op1=ALU.add,
                                           accum_out=sumsq[:, t, part:part + 1]).then_inc(v_squared, 1)
                return job

            def v_stat():
                dve.wait_ge(v_squared, 4)
                step(v.tensor_tensor(meansq[:, :], sumsq[:, :, 0], sumsq[:, :, 1], ALU.add))
                v.tensor_scalar(meansq[:, :], meansq[:, :], 1.0 / GMLP_W, RMS_EPS, ALU.mult, ALU.add).then_inc(stat, 1)

            def v_norm(t):
                def job():
                    if t == 0:
                        inverse_root(rstd_v[:, :]).then_inc(z_used, 1)
                        dve.wait_ge(z_used, 1)
                        dve.wait_ge(loaded["row_v"], 16)
                    v.scalar_tensor_tensor(out=gv[:, t, :], in0=gv[:, t, :], scalar=rstd_v[:, t:t + 1], in1=row_v[:, :],
                                           op0=ALU.mult, op1=ALU.mult).then_inc(v_normed, 1)
                return job

            def mixed(u):
                def job():
                    unit = f"mix{u}"
                    is_filled(dve, unit)
                    is_emptied(dve, f"gmlp_u{u}")
                    hf = halves(unit)
                    for j in range(4):
                        g = 4 * u + j
                        for n in range(TILES):
                            dst = gu[:, n, g * GROUP_DIM:(g + 1) * GROUP_DIM]
                            ins = v.scalar_tensor_tensor(out=dst, in0=ps[hf][:, j, n * GROUP_DIM:(n + 1) * GROUP_DIM],
                                                         scalar=cols[:, g:g + 1], in1=dst, op0=ALU.add, op1=ALU.mult)
                    ins.then_inc(half_free[hf], 1)
                return job

            def times_z(n):
                def job():
                    is_emptied(dve, f"gmlp_z{n}")
                    is_emptied(dve, f"mix{n}")
                    dst = gu[:, :, n * COLS:(n + 1) * COLS]
                    v.tensor_tensor(dst, dst, gz[:, :, :], ALU.mult).then_inc(z_used, 1)
                return job

            block_of("gmlp_u0", at={3: [causal_ws], 6: [take_params], 7: [v_square(0)], 9: [v_square(1)],
                                    11: [v_square(2)], 13: [v_square(3), v_stat]})
            block_of("gmlp_u1", at={1: [v_norm(0)], 5: [v_norm(1)]})
            block_of("gmlp_u2", at={4: [mixed(0)], 9: [mixed(1)]})
            block_of("gmlp_u3", at={4: [mixed(2)]})
            block_of("gmlp_z0", at={4: [mixed(3)]})
            block_of("gmlp_z1", at={0: [times_z(0)], 4: [lo_x("yT_gmlp0", xT2[:, :, 0:8, :], 8)]})
            block_of("gmlp_z2", at={0: [times_z(1)], 4: [lo_x("yT_gmlp1", xT2[:, :, 8:16, :], 8)]})
            block_of("gmlp_z3", at={0: [times_z(2)]})
            block_of("gmlp_out0", 2 * KT, {0: [times_z(3)], 4: [lo_x("yT_gmlp2", xT1[:, :, 0:8, :], 8)],
                                           8: [lo_x("yT_gmlp3", xT1[:, :, 8:16, :], 8)]})

            def att_gain(b):
                def job():
                    unit = f"gmlp_out{b}"
                    dve.wait_ge(products, FIRST[unit] + 2 * KT)
                    add_to_h(unit)
                    dve.wait_ge(loaded["row_norm1"], 16)
                    gained(xg, h, row_norm, b * COLS, (b + 1) * COLS).then_inc(xg_ready, 1)
                return job

            def att_rstd():
                step(inverse_root(rstd[:, :]))
                v.tensor_scalar(rstd_q[:, :], rstd[:, :], DH ** -0.5, None, ALU.mult).then_inc(rstd_ready, 1)

            att_gain(0)()
            block_of("gmlp_out1", 2 * KT, {18: [lo_x("xT_att0", xT2[:, :, 0:8, :], 8)]})
            att_gain(1)()
            block_of("att_q0", at={4: [lo_x("xT_att1", xT2[:, :, 8:16, :], 8),
                                       lambda: mean_square(2, D, 3 * TILES).then_inc(stat, 1)],
                                   7: [att_rstd]})
            for unit in ("att_q1", "att_k0", "att_k1", "att_v0", "att_v1"):
                block_of(unit)
            diag = lambda m: m.rearrange("p j (k t) -> p j k t", t=P)[:, :, 0:3:2, :]
            over = lambda m, n: m.unsqueeze(1).unsqueeze(1).to_broadcast([P, n, 2, P])

            def att_abs(g):
                is_emptied(dve, f"Z{g}")
                magnitude(sp_[:, g % 2, :, :], zs[:, g % 2, :, :]).then_inc(abs_done, 1)

            def att_sp(g):
                dve.wait_ge(ln_done, g + 1)
                s = sp_[:, g % 2, :, :]
                step(v.scalar_tensor_tensor(out=s, in0=zs[:, g % 2, :, :], scalar=0.0, in1=s, op0=ALU.max, op1=ALU.add))
                v.tensor_tensor(diag(s), diag(s), over(before[:, :], 4), ALU.mult).then_inc(sp_done, 1)

            def att_la(g):
                unit = f"L{g}"
                is_filled(dve, unit)
                z = zs[:, g % 2, :, :]
                v.tensor_tensor(z, z, ps[halves(unit)][:, :, 0:ZW], ALU.subtract).then_inc(half_free[halves(unit)], 1)
                is_emptied(dve, unit)
                v.tensor_tensor(diag(z), diag(z), over(barred[:, :], 4), ALU.add).then_inc(la_done, 1)

            def att_out(g):
                unit = f"O{g}"
                is_filled(dve, unit)
                hf = halves(unit)
                src = ps[hf][:, :, 0:2 * DH].rearrange("p j (t d) -> p j t d", d=DH)
                b, c = g // 2, (g % 2) * 4 * DH
                dst = ao[:, b, :, c:c + 4 * DH].rearrange("p t (j d) -> p j t d", d=DH)
                v.tensor_copy(dst, src).then_inc(half_free[hf], 1)

            def att_gate(b):
                def job():
                    for unit in (f"O{2 * b}", f"O{2 * b + 1}", f"att_z{b}"):
                        is_emptied(dve, unit)
                    v.tensor_tensor(ay[:, b, :, :], ao[:, b, :, :], az[:, b, :, :], ALU.mult).then_inc(ay_done, 1)
                return job

            block_of("att_z0", at={0: [lambda: att_abs(0)], 1: [lambda: att_sp(0)], 2: [lambda: att_abs(1)],
                                   3: [lambda: att_sp(1)], 5: [lambda: att_la(0)], 8: [lambda: att_out(0)],
                                   10: [lambda: att_la(1)], 12: [lambda: att_abs(2)], 13: [lambda: att_sp(2)],
                                   15: [lambda: att_out(1)]})
            block_of("att_z1", at={2: [lambda: att_la(2)], 4: [lambda: att_abs(3)], 5: [lambda: att_sp(3)],
                                   7: [lambda: att_out(2)], 8: [att_gate(0)], 9: [lambda: att_la(3)],
                                   12: [lambda: att_out(3)], 14: [lo_x("yT_att0", xT1[:, :, 0:8, :], 8)]})
            block_of("att_out0", at={0: [att_gate(1)], 4: [lo_x("yT_att1", xT1[:, :, 8:16, :], 8)]})

            def mix_gain(b):
                unit = f"att_out{b}"
                dve.wait_ge(products, FIRST[unit] + KT)
                add_to_h(unit)
                dve.wait_ge(loaded["rows_mix"], 48)
                step(gained(p_, h, row_a, b * COLS, (b + 1) * COLS))
                return block_stats(p_, b)

            mix_gain(0)
            block_of("att_out1")
            step(mix_gain(1))
            for t in range(TILES):
                tile_moments(t)
            step(mean_square(2, D, 5 * TILES))
            v.scalar_tensor_tensor(out=meansq[:, :], in0=meansq[:, :], scalar=LN_EPS, in1=moments[:, :, 1], op0=ALU.mult,
                                   op1=ALU.add).then_inc(stat, 1)
            step(inverse_root(rstd[:, :]))

            def gate_lo():
                dve.wait_ge(wg_hi, 1)
                v.tensor_tensor(wg_split[:, 1, :, :], wg_raw[:, :, :], wg_split[:, 0, :, :].bitcast(F32), ALU.subtract)\
                    .then_inc(wg_done, 1)

            def gate_values():
                is_filled(dve, "gates")
                hf = halves("gates")
                dve.wait_ge(loaded["gate"], 16)
                v.tensor_tensor(gates[:, :, :], ps[hf][:, 0:2, 0:16],
                                row_gate[:, :].unsqueeze(1).to_broadcast([P, TILES, 16]), ALU.add)\
                    .then_inc(half_free[hf], 1)
                is_emptied(dve, "gates")
                magnitude(gabs[:, :, :], gates[:, :, M_HEADS:]).then_inc(gate_abs, 1)

            def gate_logs():
                dve.wait_ge(gate_ln, 1)
                v.scalar_tensor_tensor(out=logf[:, :, :], in0=gates[:, :, M_HEADS:], scalar=0.0, in1=gabs[:, :, :],
                                       op0=ALU.min, op1=ALU.subtract).then_inc(logf_done, 1)

            def cumulated():
                is_filled(dve, "cum")
                hf = halves("cum")
                v.tensor_copy(Bc[:, :, :], ps[hf][:, 0:2, 0:M_HEADS]).then_inc(half_free[hf], 1)
                is_emptied(dve, "cum")
                v.tensor_tensor(cc[:, :, :], gates[:, :, 0:M_HEADS], Bc[:, :, :], ALU.subtract).then_inc(cc_done, 1)

            def running_max():
                is_filled(dve, "cT")
                hf = halves("cT")
                v.tensor_copy(c_rows[:, :], ps[hf][0:M_HEADS, 0, 0:TOKENS]).then_inc(half_free[hf], 1)
                is_emptied(dve, "cT")
                v.tensor_tensor_scan(G[:, :], ones[0:M_HEADS, :], c_rows[:, :], 0.0, ALU.mult, ALU.max).then_inc(G_done, 1)

            def m_arguments():
                is_filled(dve, "G_rows")
                hf = halves("G_rows")
                for n in range(M_HEADS):
                    for t, (lo, hi) in enumerate(((0, TOKENS), (TOKENS, ZW))):
                        src = flat[hf][:, n * TOKENS + t * P:(n + 1) * TOKENS]
                        ins = v.tensor_scalar(mw[:, n, lo:hi], src, cc[:, t, n:n + 1], 0.0, ALU.subtract, ALU.max)
                ins.then_inc(half_free[hf], 1)

            def m_mask():
                dve.wait_ge(mw_done, 1)
                v.tensor_tensor(diag(mw[:, :, :]), diag(mw[:, :, :]), over(upto[:, :], M_HEADS), ALU.mult)\
                    .then_inc(mw_masked, 1)

            def m_totals():
                is_filled(dve, "G_cols")
                hf = halves("G_cols")
                v.tensor_tensor(cmin[:, :, :], ps[hf][:, 0:2, 0:M_HEADS], Bc[:, :, :], ALU.add).then_inc(half_free[hf], 1)

            def m_weigh(g):
                def job():
                    unit = f"MS{g}"
                    is_filled(dve, unit)
                    dve.wait_ge(mw_masked, 1)
                    hf = halves(unit)
                    v.tensor_tensor(ms[:, g, :, :], ps[hf][:, :, 0:ZW], mw[:, 4 * g:4 * g + 4, :], ALU.mult)\
                        .then_inc(half_free[hf], 1)
                return job

            def m_divide(g):
                def job():
                    unit = f"MO{g}"
                    is_filled(dve, unit)
                    dve.wait_ge(m_exp, 1)
                    hf = halves(unit)
                    o = ps[hf][:, :, 0:2 * (DH + 1)].rearrange("p j (t e) -> p j t e", e=DH + 1)
                    den = mden[:, :, :]
                    step(v.tensor_copy(den, o[:, :, :, DH]))
                    step(magnitude(den, den))
                    step(v.tensor_tensor(den, den, cmin[:, :, 4 * g:4 * g + 4].rearrange("p t j -> p j t"), ALU.max))
                    step(v.reciprocal(den, den))
                    v.tensor_tensor(hm[:, :, 4 * g:4 * g + 4, :].rearrange("p t j d -> p j t d"), o[:, :, :, 0:DH],
                                    den.unsqueeze(3).to_broadcast([P, 4, TILES, DH]), ALU.mult).then_inc(half_free[hf], 1)
                    is_emptied(dve, unit)
                return job

            wide = lambda m: m.unsqueeze(3).to_broadcast([P, TILES, M_HEADS, DH])
            hm4 = hm[:, :, :, :]
            hm3 = hm4.rearrange("p t n d -> p t (n d)")

            def head_sum():
                step(v.tensor_reduce(mmu[:, :, :], hm4, AX_X, ALU.add))
                step(v.tensor_scalar(mmu[:, :, :], mmu[:, :, :], 1.0 / DH, None, ALU.mult))

            def head_centre():
                step(v.tensor_tensor(hm4, hm4, wide(mmu[:, :, :]), ALU.subtract))

            def head_square():
                step(v.tensor_tensor(hsq[:, :, :, :], hm4, hm4, ALU.mult))

            def head_variance():
                step(v.tensor_reduce(mrs[:, :, :], hsq[:, :, :, :], AX_X, ALU.add))
                v.tensor_scalar(mrs[:, :, :], mrs[:, :, :], 1.0 / DH, LN_EPS, ALU.mult, ALU.add).then_inc(hm_sq, 1)

            def head_scale():
                dve.wait_ge(hm_root, 1)
                step(v.reciprocal(mrs[:, :, :], mrs[:, :, :]))
                step(v.tensor_tensor(hm4, hm4, wide(mrs[:, :, :]), ALU.mult))

            def head_gain():
                dve.wait_ge(loaded["mh"], 16)
                step(v.tensor_tensor(hm3, hm3, row_mh[:, :].unsqueeze(1).to_broadcast([P, TILES, D_HALF]), ALU.mult))

            def conv_tap(j):
                def job():
                    if j == CONV_K - 1:
                        is_emptied(dve, "zT")
                        dve.wait_ge(zT_pad, 1)
                    for f in range(M_HEADS):
                        w = cols[:, 16 + 8 * j + f:17 + 8 * j + f]
                        src = zT[:, f, j:j + TOKENS]
                        if j == CONV_K - 1:
                            ins = v.tensor_scalar(yc[:, f, :], src, w, cols[:, 40 + f:41 + f], ALU.mult, ALU.add)
                        else:
                            ins = v.scalar_tensor_tensor(out=yc[:, f, :], in0=src, scalar=w, in1=yc[:, f, :],
                                                         op0=ALU.mult, op1=ALU.add)
                    step(ins)
                return job

            def conv_gate():
                is_emptied(dve, "cBT")
                v.tensor_tensor(yc[:, :, :], yc[:, :, :], cBT[:, :, :], ALU.mult).then_inc(yc_done, 1)

            def conv_lo():
                dve.wait_ge(yc_hi, 1)
                v.tensor_tensor(xT1[:, 1, 0:8, :], yc[:, :, :], xT1[:, 0, 0:8, :].bitcast(F32), ALU.subtract)\
                    .then_inc(yc_lo, 1)

            def m_gate():
                is_emptied(dve, "mix_o")
                v.tensor_tensor(hm3, hm3, mo[:, :, :], ALU.mult).then_inc(ym_done, 1)

            def zero_pad():
                v.memset(zT[:, :, 0:2], 0.0).then_inc(zT_pad, 1)

            def normed_parts(name, src, gain, bias):
                return ([norm_quarter(q, src, gain, bias) for q in range(4)],
                        [lo_x(f"{name}{q}", xT2[:, :, 4 * q:4 * q + 4, :], 4) for q in range(4)])

            quarter, lo_of = normed_parts("xT_mix", p_, row_b, row_c)
            for job in (quarter[0], quarter[1], lo_of[0], quarter[2], lo_of[1], quarter[3]):
                job()
            block_of("mix_q", at={0: [lo_of[2]], 3: [lo_of[3]], 8: [gate_lo]})
            block_of("mix_k", at={7: [gate_values], 10: [gate_logs], 12: [cumulated]})
            v.memset(mv[:, :, :, DH:DH + 1], 1.0).then_inc(mv_ones, 1)
            block_of("mix_v", at={6: [running_max], 8: [m_arguments], 12: [m_mask, m_totals]})
            block_of("mix_cC", at={4: [m_weigh(0)], 7: [m_weigh(1), zero_pad], 10: [m_divide(0)], 13: [m_divide(1)]})
            block_of("mix_ch", at={1: [head_sum], 4: [head_centre], 6: [head_square], 8: [head_variance],
                                   11: [head_scale], 13: [head_gain]})
            is_emptied(dve, "mix_cC")
            dve.wait_ge(products, FIRST["mix_ch"] + KT)
            v.tensor_tensor(cz[:, :, :], by_tile[A], cz[:, :, :], ALU.mult).then_inc(half_free[A], 1)
            block_of("mix_cB", at={7: [conv_tap(2)], 10: [conv_tap(1)], 13: [conv_tap(0)]})
            block_of("mix_o", at={5: [conv_gate], 7: [conv_lo]})
            block_of("mix_out0", at={0: [m_gate], 4: [lo_x("ymT", xT1[:, :, 8:16, :], 8)]})

            def mix_add(b):
                unit = f"mix_out{b}"
                dve.wait_ge(products, FIRST[unit] + KT)
                add_to_h(unit, ALPHA)
                return block_stats(h, b)

            def deviation():
                v.tensor_scalar(meansq[:, :], moments[:, :, 1], LN_EPS, None, ALU.add).then_inc(stat, 1)
                step(inverse_root(rstd[:, :]))

            mix_add(0)
            block_of("mix_out1")
            step(mix_add(1))
            for t in range(TILES):
                ins = tile_moments(t)
            step(ins)
            deviation()
            dve.wait_ge(loaded["rows_ln1"], 32)
            quarter, lo_of = normed_parts("xT_peer", h, row_a, row_b)
            for job in (quarter[0], quarter[1], lo_of[0], quarter[2], lo_of[1], quarter[3]):
                job()
            block_of("peer_q0", at={0: [lo_of[2]], 3: [lo_of[3]]})

            def best16(values, rest, top, where, groups):
                for n in range(groups):
                    ins = v.max(top[:, n, 0:8], values[:, n, :])
                step(ins)
                for n in range(groups):
                    v.max_index(where[:, n, 0:8], top[:, n, 0:8], values[:, n, :])
                    ins = v.match_replace(rest[:, n, :], top[:, n, 0:8], values[:, n, :], LOWEST)
                step(ins)
                for n in range(groups):
                    ins = v.max(top[:, n, 8:16], rest[:, n, :])
                step(ins)
                for n in range(groups):
                    ins = v.max_index(where[:, n, 8:16], top[:, n, 8:16], rest[:, n, :])
                step(ins)

            four = [P, 4, TOPK, TOPK]
            onehot4 = onehot[:, :, :].rearrange("p (h k) a -> p h k a", k=TOPK)
            sv4 = sv[:, :, :].rearrange("p (h s) k -> p h s k", s=2)
            sif4 = sif[:, :, :].rearrange("p (h s) k -> p h s k", s=2)

            def choose(g, t):
                is_emptied(dve, f"scores{g}")
                best16(scores[g][:, t, :, :], left, sv, si, PEER_HEADS)
                step(v.tensor_copy(sif[:, :, :], si[:, :, :]))
                step(v.tensor_tensor(cand[:, :, :].rearrange("p h (a b) -> p h a b", b=TOPK),
                                     sv4[:, :, 0, :].unsqueeze(3).to_broadcast(four),
                                     sv4[:, :, 1, :].unsqueeze(2).to_broadcast(four), ALU.add))
                best16(cand, cand_left, tops, topj, 4)
                v.tensor_tensor(gate[:, t, 4 * g:4 * g + 4, :], tops[:, :, :], tops[:, :, 0:1].to_broadcast([P, 4, TOPK]),
                                ALU.subtract).then_inc(gate_sub, 1)
                for half, (op, n) in enumerate(((ALU.logical_shift_right, 4), (ALU.bitwise_and, TOPK - 1))):
                    step(v.tensor_scalar(topa[:, :, :], topj[:, :, :], n, None, op))
                    step(v.tensor_copy(topaf[:, :, :], topa[:, :, :]))
                    step(v.tensor_tensor(onehot4, topaf[:, :, :].unsqueeze(3).to_broadcast(four),
                                         iota16[:, :].unsqueeze(1).unsqueeze(1).to_broadcast(four), ALU.is_equal))
                    step(v.tensor_tensor(onehot4, onehot4, sif4[:, :, half, :].unsqueeze(2).to_broadcast(four), ALU.mult))
                    step(v.tensor_reduce(rowid[:, half, :], onehot[:, :, :], AX_X, ALU.add))
                for first in ((TILES * g + t) * GROUP_PICKS, TILES * PICKS + (2 * t + g) * GROUP_PICKS):
                    step(v.scalar_tensor_tensor(out=eid[:, first:first + GROUP_PICKS], in0=rowid[:, 0, :],
                                                scalar=float(N_KEYS), in1=rowid[:, 1, :], op0=ALU.mult, op1=ALU.add))

            def finish_gate(g, t):
                dve.wait_ge(gate_exp, TILES * g + t + 1)
                cut = gate[:, t, 4 * g:4 * g + 4, :]
                step(v.tensor_reduce(gsum[:, :], cut, AX_X, ALU.add))
                step(v.reciprocal(gsum[:, :], gsum[:, :]))
                step(v.tensor_tensor(cut, cut, gsum[:, :].unsqueeze(2).to_broadcast([P, 4, TOPK]), ALU.mult))

            def stage(b, first):
                v.tensor_copy(idx[:, b, :], eid[:, bass.ds(first, GATHER_SLOTS)]).then_inc(idx_ready[b], 1)

            BODY = 2 * GATHER_SLOTS

            def gathered(i, m, s):
                dve.wait_ge(row_landed[s], i * (16 * 2) + 16 * (m // GATHER_SLOTS + 1))

            def dot_rows(g, t):
                first = (TILES * g + t) * GROUP_PICKS
                with dve.Fori(0, GROUP_PICKS // BODY) as i:
                    for b in range(2):
                        for s in range(GATHER_SLOTS):
                            gathered(i, first + b * GATHER_SLOTS, s)
                            v.tensor_tensor_reduce(out=ring[:, s, :], in0=ring[:, s, :], in1=h[:, t, :], scale=1.0,
                                                   scalar=0.0, op0=ALU.mult, op1=ALU.add,
                                                   accum_out=dots[:, b, s:s + 1]).then_inc(rows_used, 1)
                        dve.wait_ge(rows_used, i * BODY + (first + (b + 2) * GATHER_SLOTS))
                        v.tensor_copy(act_[:, bass.ds(i * BODY + (first + b * GATHER_SLOTS), GATHER_SLOTS)], dots[:, b, :])
                        stage(b, i * BODY + (first + (b + 2) * GATHER_SLOTS))

            v.memset(eid[:, 2 * TILES * PICKS:], 0).then_inc(eid_pad, 1)
            dve.sem_inc(rows_used, GATHER_SLOTS)

            def first_picks():
                choose(0, 0)
                for b in range(2):
                    stage(b, b * GATHER_SLOTS)

            block_of("peer_q1", at={11: [first_picks]}, last=True)
            choose(0, 1)
            finish_gate(0, 0)
            dot_rows(0, 0)
            choose(1, 0)
            finish_gate(0, 1)
            dot_rows(0, 1)
            choose(1, 1)
            finish_gate(1, 0)
            dot_rows(1, 0)
            finish_gate(1, 1)
            dot_rows(1, 1)
            dve.wait_ge(eid_pad, 1)

            def weigh_rows(t):
                first = t * PICKS
                dve.wait_ge(gelu_done, TILES + t + 1)
                w = wgt[:, first:first + PICKS]
                step(v.tensor_tensor(w, w, gate[:, t, :, :].rearrange("p h k -> p (h k)"), ALU.mult))
                step(v.tensor_scalar(vacc[:, 0, :], h[:, t, :], ALPHA, None, ALU.mult))
                step(v.memset(vacc[:, 1, :], 0.0))
                with dve.Fori(0, PICKS // BODY) as i:
                    for b in range(2):
                        for s in range(GATHER_SLOTS):
                            n = first + b * GATHER_SLOTS + s
                            gathered(i, TILES * PICKS + n - s, s)
                            dve.wait_ge(rows_used, i * BODY + (TILES * PICKS + n + GATHER_SLOTS - 1))
                            v.scalar_tensor_tensor(out=vacc[:, s % 2, :], in0=ring[:, s, :],
                                                   scalar=wgt[:, bass.ds(i * BODY + n, 1)], in1=vacc[:, s % 2, :],
                                                   op0=ALU.mult, op1=ALU.add).then_inc(rows_used, 1)
                        if t < TILES - 1 or b < 2:
                            stage(b, i * BODY + (TILES * PICKS + first + (b + 2) * GATHER_SLOTS))
                dve.wait_ge(rows_used, TILES * PICKS + first + PICKS + GATHER_SLOTS)

            for t in range(TILES):
                weigh_rows(t)
                step(v.tensor_tensor(h[:, t, :], vacc[:, 0, :], vacc[:, 1, :], ALU.add))
                for n in range(4):
                    ins = v.bn_stats(bn[:, t, n, :], h[:, t, n * BANK:(n + 1) * BANK])
                step(ins)
                step(tile_moments(t))
                deviation()
                dve.wait_ge(loaded["rows_ln2"], 32)
                step(normalise(h, t, 0, D))
                step(v.tensor_tensor(h[:, t, :], h[:, t, :], row_g2[:, :], ALU.mult))
                v.tensor_tensor(h[:, t, :], h[:, t, :], row_b2[:, :], ALU.add).then_inc(out_ready, 1)


_INS = ["x", "norm_g", "a_w_in", "a_v_norm_g", "a_w_s", "a_b_s", "a_w_out", "b_w_in", "b_w_out", "final_g", "ln_in_g_2",
        "ln_in_b_2", "w_in_2", "b_gate_2", "conv_w_2", "conv_b_2", "mh_norm_g_2", "w_out_2", "ln1_g_2", "ln1_b_2",
        "peer_wq_2", "peer_keys_2", "peer_u_2", "peer_v_2", "ln2_g_2", "ln2_b_2"]


def kernel(**inputs):
    import numpy as np
    import concourse.bacc as bacc
    from concourse.bass_utils import run_bass_kernel_spmd

    nc = bacc.Bacc("TRN2", target_bir_lowering=False, num_devices=1)
    arrays, args = {}, []
    for name in _INS:
        a = np.ascontiguousarray(inputs[name])
        arrays["in_" + name] = a
        args.append(nc.dram_tensor("in_" + name, a.shape, F32, kind="ExternalInput").ap())
    out = nc.dram_tensor("out_h", (1, TOKENS, D), F32, kind="ExternalOutput").ap()
    build(nc, *args, out)
    r = run_bass_kernel_spmd(nc, [arrays], core_ids=[0])
    return r.results[0]["out_h"]
```

```python
from contextlib import ExitStack

import concourse.bass as bass
from concourse import mybir

F32 = mybir.dt.float32
F32R = mybir.dt.float32r
U32 = mybir.dt.uint32
ALU = mybir.AluOpType
ACT = mybir.ActivationFunctionType
AX_X = mybir.AxisListType.X

P = 128
TOKENS = 256
TILES = TOKENS // P
D = 2048
KT = D // P
COLS = 1024
BANK = 512
GMLP_W = 4096
GROUPS = 16
GROUP_DIM = GMLP_W // GROUPS
HEADS = 16
DH = 128
M_HEADS = 8
D_HALF = 1024
CONV_K = 3
PEER_HEADS = 8
N_KEYS = 128
TOPK = 16
PICKS = PEER_HEADS * TOPK
RMS_EPS = 1e-6
LN_EPS = 1e-5
ALPHA = 2.0 ** 0.25
NEG = -1.0e30
LOWEST = -3.0e38
ZW = 3 * P
GROUP_HEADS = 2
TILE_GROUPS = PEER_HEADS // GROUP_HEADS
GROUP_PICKS = GROUP_HEADS * TOPK
V_PARTS = 4
V_GATHERED = D // V_PARTS
V_DENSE = D - V_GATHERED
V_BANKS = V_DENSE // BANK
V_SLOTS = 4
SCATTER = 8

RAW_SLOTS = 4
SPLIT_SLOTS = 4
AHEAD = SPLIT_SLOTS
GATHER_SLOTS = 8
LN_PARTS = ((0, 2), (2, 2), (4, 4), (8, 4), (12, 4))
A, B = 0, 1

UNITS = (
    [(f"xT_gmlp{i}", i % 2, False) for i in range(4)]
    + [(f"gmlp_v{i}", i % 2, True) for i in range(4)]
    + [("gmlp_u0", A, True), ("ws", B, False), ("params", B, False), ("gmlp_u1", B, True),
       ("gmlp_u2", A, True), ("mix0", B, False), ("mix1", B, False),
       ("gmlp_u3", B, True), ("mix2", A, False), ("gmlp_z0", A, True), ("mix3", B, False),
       ("gmlp_z1", B, True), ("yT_gmlp0", A, False), ("gmlp_z2", A, True), ("yT_gmlp1", B, False),
       ("gmlp_z3", B, True), ("gmlp_out0", A, True), ("yT_gmlp2", B, False), ("yT_gmlp3", B, False)]
    + [("gmlp_out1", B, True), ("xT_att0", A, False), ("att_q0", A, True), ("xT_att1", B, False),
       ("att_q1", B, True), ("qkT0", A, False), ("att_k0", A, True), ("qkT1", B, False),
       ("att_k1", B, True), ("qkT2", A, False), ("att_v0", A, True), ("qkT3", B, False), ("att_v1", B, True)]
    + [("att_z0", A, True), ("Z0", B, False), ("Z1", B, False), ("L0", B, False), ("O0", B, False), ("L1", B, False),
       ("Z2", B, False), ("O1", B, False), ("att_z1", A, True), ("L2", B, False), ("Z3", B, False), ("O2", B, False),
       ("L3", B, False), ("O3", B, False), ("yT_att0", B, False)]
    + [("att_out0", B, True), ("yT_att1", A, False), ("att_out1", A, True)]
    + [("xT_mix0", B, False), ("mix_q", A, True)] + [(f"xT_mix{i}", B, False) for i in range(1, len(LN_PARTS))]
    + [("mix_k", B, True), ("mqT", A, False), ("gates", A, False), ("cum", A, False)]
    + [("mix_v", A, True), ("mkT", B, False), ("cT", B, False), ("G_rows", B, False), ("G_cols", B, False)]
    + [("mix_cC", B, True), ("MS0", A, False), ("MS1", A, False), ("MO0", A, False), ("MO1", A, False)]
    + [("mix_ch", A, True), ("mix_cB", B, True), ("zT", A, False), ("mix_o", A, True), ("cBT", B, False)]
    + [("mix_out0", B, True), ("ymT", A, False), ("mix_out1", A, True)]
    + [("xT_peer0", B, False), ("peer_q0", A, True)] + [(f"xT_peer{i}", B, False) for i in range(1, len(LN_PARTS))]
    + [("keysT", B, False)]
    + [("peer_q1", B, True), ("pqT0", A, False), ("scores0", A, False), ("pqT1", A, False), ("scores1", A, False),
       ("pkT0", A, False), ("wgtT0", A, False), ("pkT1", A, False), ("wgtT1", A, False)]
)

STREAM = [("gmlp_v", 4, KT), ("gmlp_u", 4, KT), ("gmlp_z", 4, KT), ("gmlp_out", 2, 2 * KT), ("att_q", 2, KT),
          ("att_k", 2, KT), ("att_v", 2, KT), ("att_z", 2, KT), ("att_out", 2, KT), ("mix_in", 7, KT),
          ("mix_out", 2, KT), ("peer_q", 2, KT)]
MIX_IN = {"mix_q": (0, 3), "mix_k": (1, 4), "mix_v": (2, 5), "mix_cC": (3, 1), "mix_ch": (4, 2), "mix_cB": (5, 0),
          "mix_o": (6, 6)}


def number_units():
    used, filled, nth, fill = [0, 0], [0, 0], {}, {}
    for name, half, streams in UNITS:
        nth[name] = (half, used[half])
        used[half] += 1
        if not streams:
            filled[half] += 1
            fill[name] = filled[half]
    return nth, fill


def number_chunks():
    first, at = {}, 0
    for name, blocks, kts in STREAM:
        for n in range(blocks):
            first[f"{name}{n}"] = at
            at += kts
    for name, (n, _) in MIX_IN.items():
        first[name] = first[f"mix_in{n}"]
    return first, at


def build(nc, x, norm_g, a_w_in, a_v_norm_g, a_w_s, a_b_s, a_w_out, b_w_in, b_w_out, final_g, ln_in_g_2, ln_in_b_2,
          w_in_2, b_gate_2, conv_w_2, conv_b_2, mh_norm_g_2, w_out_2, ln1_g_2, ln1_b_2, peer_wq_2, peer_keys_2,
          peer_u_2, peer_v_2, ln2_g_2, ln2_b_2, out):
    NTH, FILL = number_units()
    FIRST, CHUNKS = number_chunks()

    ctx = ExitStack()
    with ctx:
        at_byte = [(nc.sbuf_base + 31) // 32 * 32]

        def region(size):
            start = at_byte[0]
            at_byte[0] += (size + 31) // 32 * 32
            assert at_byte[0] <= nc.sbuf_usable_end, at_byte[0]
            return start

        def sb(name, shape, dt, offset):
            return nc.alloc_sbuf_tensor_at(name, shape, dt, offset=offset)

        def packer(start, size):
            place = [start]

            def put(name, shape, dt=F32):
                n = 4
                for s in shape[1:]:
                    n *= s
                o = place[0]
                place[0] += (n + 31) // 32 * 32
                assert place[0] <= start + size, name
                return sb(name, shape, dt, o)
            return put

        KB = 1024
        RAW = region(16 * KB)
        H = region(16 * KB)
        ROWS = region(24 * KB)
        SMALL = region(7 * KB)
        T1 = region(32 * KB)
        SPLIT = region(32 * KB)
        T2 = region(32 * KB)
        SCR = region(48 * KB + 512)

        xT1 = sb("xT1", [P, 2, KT, TOKENS], F32R, T1)
        xT2 = sb("xT2", [P, 2, KT, TOKENS], F32R, T2)
        w_split = sb("w_split", [P, SPLIT_SLOTS, 2, COLS], F32R, SPLIT)
        w_raw = sb("w_raw", [P, RAW_SLOTS, COLS], F32, RAW)
        h = sb("h", [P, TILES, D], F32, H)

        tiny = packer(SMALL, 7 * KB)
        MASKS = SMALL + P * 4
        ident = tiny("ident", [P, P])
        upto = tiny("upto", [P, P])
        onward = tiny("onward", [P, P])
        before = tiny("before", [P, P])
        barred = tiny("barred", [P, P])
        ones = tiny("ones", [P, TOKENS])
        iota16 = tiny("iota16", [P, TOPK])
        cols = tiny("cols", [P, 48])
        sumsq = tiny("sumsq", [P, TILES, 2])
        meansq = tiny("meansq", [P, TILES])
        root = tiny("root", [P, TILES])
        rstd = tiny("rstd", [P, TILES])
        rstd_v = tiny("rstd_v", [P, TILES])
        rstd_q = tiny("rstd_q", [P, TILES])
        bn = tiny("bn", [P, TILES, 4, 6])
        moments = tiny("moments", [P, TILES, 2])
        shift = tiny("shift", [P, TILES])
        warm = tiny("warm", [P, 1])

        xg = sb("xg", [P, TILES, D], F32, SCR)
        gu = sb("gu", [P, TILES, GMLP_W], F32, SCR)
        ws_raw = sb("ws_raw", [P, GROUPS, P], F32, SCR + 16 * KB)
        x_trash = sb("x_trash", [P, D], F32, SCR + 24 * KB)
        wsT = sb("wsT", [P, GROUPS, P], F32, SCR + 32 * KB)
        gz = sb("gz", [P, TILES, COLS], F32, SCR + 40 * KB)
        param_rows = sb("param_rows", [48, P], F32, SCR + 40 * KB)
        gv = sb("gv", [P, TILES, GMLP_W], F32, T2)
        row_norm = sb("row_norm", [P, D], F32, ROWS)
        row_v = sb("row_v", [P, GMLP_W], F32, ROWS + 8 * KB)

        q_trash = sb("q_trash", [P, COLS], F32, SCR + 40 * KB)
        q_tok = sb("q_tok", [P, 2, TILES, COLS], F32, T1)
        k_tok = sb("k_tok", [P, 2, TILES, COLS], F32, T1 + 16 * KB)
        qkT = sb("qkT", [P, 2, HEADS, TOKENS], F32, SCR)
        av = sb("av", [P, TILES, D], F32, SCR + 32 * KB)
        ao = sb("ao", [P, 2, TILES, COLS], F32, T1)
        az = sb("az", [P, 2, TILES, COLS], F32, T1 + 16 * KB)
        ay = sb("ay", [P, 2, TILES, COLS], F32, SCR)
        zs = sb("zs", [P, 2, 4, ZW], F32, ROWS)
        sp_ = sb("softplus", [P, 2, 4, ZW], F32, ROWS + 12 * KB)

        row_a = sb("row_a", [P, D], F32, ROWS)
        row_b = sb("row_b", [P, D], F32, ROWS + 8 * KB)
        row_c = sb("row_c", [P, D], F32, ROWS + 16 * KB)
        p_ = sb("h_gained", [P, TILES, D], F32, SCR + 16 * KB)
        p_trash = sb("p_trash", [P, COLS], F32, SCR + 32 * KB)
        mqk_tok = sb("mqk_tok", [P, 2, TILES, D_HALF], F32, T1)
        mw = sb("mw", [P, M_HEADS, ZW], F32, T1 + 16 * KB)
        wg_raw = sb("wg_raw", [P, KT, 16], F32, T1 + 28 * KB)
        wg_split = sb("wg_split", [P, 2, KT, 16], F32R, T1 + 29 * KB)
        G = sb("G", [M_HEADS, TOKENS], F32, T1 + 31 * KB)
        c_rows = sb("c_rows", [M_HEADS, TOKENS], F32, T1 + 28 * KB)
        hsq = sb("hsq", [P, TILES, M_HEADS, DH], F32, T1 + 8 * KB)
        mqkT = sb("mqkT", [P, 2, M_HEADS, TOKENS], F32, SCR)
        mv = sb("mv", [P, TILES, M_HEADS, DH + 1], F32, SCR + 16 * KB + 128)
        mo = sb("mo", [P, TILES, D_HALF], F32, SCR + 24 * KB + 256)
        cB = sb("cB", [P, TILES, D_HALF], F32, SCR + 32 * KB + 256)
        cz = sb("cz", [P, TILES, D_HALF], F32, SCR + 40 * KB + 256)
        row_mh = sb("row_mh", [P, D_HALF], F32, ROWS)
        hm = sb("hm", [P, TILES, M_HEADS, DH], F32, ROWS + 4 * KB)
        ms = sb("ms", [P, 2, 4, ZW], F32, ROWS + 12 * KB)
        zT = sb("zT", [P, M_HEADS, TOKENS + 2], F32, SCR)
        cBT = sb("cBT", [P, M_HEADS, TOKENS], F32, SCR + 8256)
        yc = sb("yc", [P, M_HEADS, TOKENS], F32, SCR + 16 * KB + 128)
        row_gate = tiny("row_gate", [P, 16])
        gates = tiny("gates", [P, TILES, 16])
        gabs = tiny("gabs", [P, TILES, M_HEADS])
        logf = tiny("logf", [P, TILES, M_HEADS])
        Bc = tiny("Bc", [P, TILES, M_HEADS])
        cc = tiny("cc", [P, TILES, M_HEADS])
        cmin = tiny("cmin", [P, TILES, M_HEADS])
        mden = tiny("mden", [P, 4, TILES])
        mmu = tiny("mmu", [P, TILES, M_HEADS])
        mrs = tiny("mrs", [P, TILES, M_HEADS])

        pq_tok = sb("pq_tok", [P, 2, TILES, COLS], F32, SCR)
        pqT = sb("pqT", [P, 2 * PEER_HEADS, TOKENS], F32, SCR + 16 * KB)
        keysT = sb("keysT", [P, 2 * PEER_HEADS, P], F32, SCR + 32 * KB)
        keys_raw = sb("keys_raw", [P, 2 * PEER_HEADS, P], F32, SCR + 40 * KB)
        scores = [sb("scores_a", [P, TILES, PEER_HEADS, N_KEYS], F32, SCR + 40 * KB),
                  sb("scores_b", [P, TILES, PEER_HEADS, N_KEYS], F32, RAW)]
        LISTS = 14848
        lists = packer(ROWS, LISTS)
        left = lists("left", [P, 2 * GROUP_HEADS, N_KEYS])
        cand = lists("cand", [P, GROUP_HEADS, TOPK * TOPK])
        onehot = lists("onehot", [P, GROUP_PICKS, TOPK])
        cand_left = left[:, :, :].rearrange("p (h a) b -> p h (a b)", a=2)
        sv = lists("sv", [P, 2 * GROUP_HEADS, TOPK])
        si = lists("si", [P, 2 * GROUP_HEADS, TOPK], U32)
        sif = lists("sif", [P, 2 * GROUP_HEADS, TOPK])
        tops = lists("tops", [P, GROUP_HEADS, TOPK])
        topj = lists("topj", [P, GROUP_HEADS, TOPK], U32)
        topa = lists("topa", [P, GROUP_HEADS, TOPK], U32)
        topaf = lists("topaf", [P, GROUP_HEADS, TOPK])
        pick = packer(ROWS + LISTS, 24 * KB - LISTS)
        eid = pick("eid", [P, 2 * TILES * PICKS + 2 * GATHER_SLOTS], U32)
        idx = pick("idx", [P, 2, GATHER_SLOTS], U32)
        gsum = pick("gsum", [P, GROUP_HEADS])
        dots = pick("dots", [P, 2, GATHER_SLOTS])
        wgt = pick("wgt", [P, TILES * PICKS])
        gate = pick("gate", [P, TILES, PEER_HEADS, TOPK])
        pick_keys = pick("pick_keys", [P, TILES, 2, PICKS])
        picksT = pick("picksT", [P, 3, TOKENS])
        ring = sb("ring", [P, GATHER_SLOTS, D], F32, T1)

        wT = sb("wT", [P, TILES, N_KEYS, P], F32, T1)
        onehot_a = sb("onehot_a", [P, 2, SCATTER, N_KEYS], F32, SCR + 32 * KB)
        onehot_b = sb("onehot_b", [P, 2, SCATTER, N_KEYS], F32, SCR + 40 * KB)
        iota_keys = sb("iota_keys", [P, N_KEYS], F32, MASKS + 5 * P * 4)
        v_odd = sb("v_odd", [P, V_GATHERED], F32, MASKS)
        V_CHUNK = V_DENSE * 4
        lists = packer(ROWS, LISTS)
        v_raw = [lists("v_raw0", [P, V_DENSE]),
                 sb("v_raw1", [P, V_DENSE], F32, ROWS + 24 * KB - 288 - V_CHUNK)]
        w_x = [lists(f"w_x{n}", [P, 2, TILES, 1, P], F32R) for n in range(2)]
        v_split = [sb("v_split0", [P, 2, V_DENSE], F32R, RAW), sb("v_split1", [P, 2, V_DENSE], F32R, SCR + 32 * KB)]
        v_rows = ([sb(f"v_rows{n}", [P, V_GATHERED], F32, RAW + 2 * V_CHUNK + n * V_GATHERED * 4) for n in range(2)]
                  + [lists(f"v_rows{n}", [P, V_GATHERED]) for n in (2, 3)])
        row_g2 = sb("row_g2", [P, D], F32, T1)
        row_b2 = sb("row_b2", [P, D], F32, T2)

        ps = [ctx.enter_context(nc.psum_tensor(f"half{n}", [P, 4, BANK], F32)) for n in range(2)]
        flat = [t[:, :, :].rearrange("p b n -> p (b n)") for t in ps]
        by_tile = [t[:, :, :].rearrange("p (t b) n -> p t (b n)", t=TILES) for t in ps]
        by_128 = [f.rearrange("p (k t) -> p k t", t=P) for f in flat]
        by_tok = [f.rearrange("p (k t) -> p k t", t=TOKENS) for f in flat]

        def sem(name):
            return ctx.enter_context(nc.semaphore(name))

        half_filled = [sem("half_filled_a"), sem("half_filled_b")]
        half_free = [sem("half_free_a"), sem("half_free_b")]
        raw_landed = [sem(f"raw_landed{n}") for n in range(RAW_SLOTS)]
        hi_done = sem("hi_done")
        split_done = sem("split_done")
        products = sem("products")
        dve_step = sem("dve_step")
        act_step = sem("act_step")
        pool_step = sem("pool_step")
        consts_done = sem("consts_done")
        xT_hi = sem("xT_hi")
        loaded = {n: sem("loaded_" + n) for n in (
            "x0", "x1", "ws", "params", "gain0", "gain1", "row_v", "row_norm1", "rows_mix", "wg", "gate", "mh", "rows_ln1", "keys",
            "rows_ln2")}
        xg_ready = sem("xg_ready")
        squares = sem("squares")
        stat = sem("stat")
        rooted = sem("rooted")
        rstd_ready = sem("rstd_ready")
        v_squared = sem("v_squared")
        v_normed = sem("v_normed")
        z_used = sem("z_used")
        abs_done = sem("abs_done")
        ln_done = sem("ln_done")
        sp_done = sem("sp_done")
        la_done = sem("la_done")
        a_done = sem("a_done")
        ay_done = sem("ay_done")
        wg_hi = sem("wg_hi")
        wg_done = sem("wg_done")
        gate_abs = sem("gate_abs")
        gate_ln = sem("gate_ln")
        logf_done = sem("logf_done")
        cc_done = sem("cc_done")
        G_done = sem("G_done")
        mw_done = sem("mw_done")
        mw_masked = sem("mw_masked")
        m_exp = sem("m_exp")
        mv_ones = sem("mv_ones")
        zT_pad = sem("zT_pad")
        hm_sq = sem("hm_sq")
        hm_root = sem("hm_root")
        ym_done = sem("ym_done")
        yc_done = sem("yc_done")
        yc_hi = sem("yc_hi")
        yc_lo = sem("yc_lo")
        gate_sub = sem("gate_sub")
        gate_exp = sem("gate_exp")
        idx_ready = [sem("idx_ready0"), sem("idx_ready1")]
        row_landed = [sem(f"row_landed{n}") for n in range(GATHER_SLOTS)]
        rows_used = sem("rows_used")
        gelu_done = sem("gelu_done")
        keys_known = sem("keys_known")
        wgt_done = sem("wgt_done")
        onehot_done = sem("onehot_done")
        scattered = sem("scattered")
        w_stored = sem("w_stored")
        v_raw_landed = [sem("v_raw_landed0"), sem("v_raw_landed1")]
        v_hi = sem("v_hi")
        w_hi = sem("w_hi")
        v_lo = sem("v_lo")
        w_lo = sem("w_lo")
        v_products = sem("v_products")
        v_landed = [sem(f"v_landed{n}") for n in range(V_SLOTS)]
        v_used = sem("v_used")
        y_stored = sem("y_stored")
        shift_ready = sem("shift_ready")
        normed = sem("normed")
        out_ready = sem("out_ready")

        block = ctx.enter_context(nc.Block())

        def is_free(eng, unit):
            half, n = NTH[unit]
            if n:
                eng.wait_ge(half_free[half], n)

        def is_filled(eng, unit):
            eng.wait_ge(half_filled[NTH[unit][0]], FILL[unit])

        def is_emptied(eng, unit):
            half, n = NTH[unit]
            eng.wait_ge(half_free[half], n + 1)

        def halves(unit):
            return NTH[unit][0]

        def step_counter(eng, s):
            count = [0]

            def step(ins):
                count[0] += 1
                ins.then_inc(s, 1)
                eng.wait_ge(s, count[0])
            return step

        @block.sync
        def _(sp):
            for b in range(2):
                cut = slice(b * COLS, (b + 1) * COLS)
                sp.dma_start(h[:, :, cut], x[0].rearrange("(t p) d -> p t d", p=P)[:, :, cut])\
                    .then_inc(loaded[f"x{b}"], 16)

            def load_block(w, c, col, kts=KT):
                for k in range(kts):
                    if not (isinstance(c, int) and c + k < RAW_SLOTS):
                        sp.wait_ge(split_done, c + (k + 1 - RAW_SLOTS))
                    sp.dma_start(w_raw[:, k % RAW_SLOTS, :], w[k * P:(k + 1) * P, bass.ds(col, COLS)])\
                        .then_inc(raw_landed[k % RAW_SLOTS], 16)

            def load_pairs(w, stage, col, pairs):
                c = FIRST[stage + "0"]
                with sp.Fori(0, pairs) as i:
                    for n in range(2):
                        load_block(w, i * (2 * KT) + (c + n * KT), i * (2 * COLS) + (col + n * COLS))

            for n in range(4):
                load_block(a_w_in[0], FIRST[f"gmlp_v{n}"], GMLP_W + n * COLS)
            load_pairs(a_w_in[0], "gmlp_u", 0, 2)
            load_pairs(a_w_in[0], "gmlp_z", 2 * GMLP_W, 2)
            for n in range(2):
                load_block(a_w_out[0], FIRST[f"gmlp_out{n}"], n * COLS, 2 * KT)
            load_pairs(b_w_in[0], "att_q", 0, 4)
            load_pairs(b_w_out[0], "att_out", 0, 1)
            for name, (_, b) in MIX_IN.items():
                load_block(w_in_2[0], FIRST[name], b * COLS)
            load_pairs(w_out_2[0], "mix_out", 0, 1)
            load_pairs(peer_wq_2[0], "peer_q", 0, 1)

            def load_v(c, s):
                if s == 1 and isinstance(c, int):
                    sp.wait_ge(scattered, TOKENS // SCATTER + 2)
                if not isinstance(c, int):
                    sp.wait_ge(v_lo, c - 1)
                sp.dma_start(v_raw[s][:, :], peer_v_2[0, bass.ds(c * N_KEYS, N_KEYS), 0:V_DENSE])\
                    .then_inc(v_raw_landed[s], 16)

            sp.wait_ge(keys_known, TILES)
            for s in range(2):
                load_v(s, s)
            with sp.Fori(1, N_KEYS // 2) as i:
                for s in range(2):
                    load_v(i * 2 + s, s)
            for n in range(2 * TILES):
                t, b = divmod(n, 2)
                cols_ = slice(b * COLS, (b + 1) * COLS)
                sp.wait_ge(out_ready, n + 1)
                sp.dma_start(out[0, t * P:(t + 1) * P, cols_], h[:, t, cols_]).then_inc(y_stored, 16)
            sp.wait_ge(y_stored, 2 * 16 * TILES)

        @block.gpsimd
        def _(pool):
            step = step_counter(pool, pool_step)

            def row(dst, src, name):
                pool.dma_start(dst, src.partition_broadcast(P)).then_inc(loaded[name], 16)

            for b in range(2):
                row(row_norm[:, b * COLS:(b + 1) * COLS], norm_g[0, b * COLS:(b + 1) * COLS], f"gain{b}")

            def triangle(m, base, fill, op, cm, st):
                step(nc.gpsimd.memset(m[:, :], base))
                step(nc.gpsimd.affine_select(out=m[:, :], in_=m[:, :], compare_op=op, fill=fill, base=0,
                                             pattern=[[st, P]], channel_multiplier=cm))
            triangle(ident, 0.0, 1.0, ALU.not_equal, 1, -1)
            step(nc.gpsimd.memset(ones[:, :], 1.0))
            nc.gpsimd.iota(iota16[:, :], pattern=[[1, TOPK]], base=0, channel_multiplier=0,
                           allow_small_or_imprecise_dtypes=True).then_inc(consts_done, 1)
            triangle(upto, 1.0, 0.0, ALU.is_ge, -1, 1)
            triangle(onward, 1.0, 0.0, ALU.is_ge, 1, -1)
            triangle(before, 1.0, 0.0, ALU.is_gt, -1, 1)
            step(nc.gpsimd.memset(barred[:, :], 0.0))
            nc.gpsimd.affine_select(out=barred[:, :], in_=barred[:, :], compare_op=ALU.is_gt, fill=NEG, base=0,
                                    pattern=[[1, P]], channel_multiplier=-1).then_inc(consts_done, 1)
            pool.dma_start(param_rows[0:16, :], a_b_s[0]).then_inc(loaded["params"], 16)
            pool.dma_start(param_rows[16:40, :], conv_w_2[0].rearrange("j (f p) -> (j f) p", p=P))\
                .then_inc(loaded["params"], 16)
            pool.dma_start(param_rows[40:48, :], conv_b_2[0].rearrange("(f p) -> f p", p=P))\
                .then_inc(loaded["params"], 16)
            pool.dma_start(ws_raw[:, :, :], a_w_s[0].rearrange("g t s -> t g s")).then_inc(loaded["ws"], 16)
            row(row_v[:, :], a_v_norm_g[0], "row_v")
            row(row_gate[:, :], b_gate_2[0], "gate")

            pool.wait_ge(xg_ready, 4)
            row(row_norm[:, :], norm_g[1], "row_norm1")
            is_emptied(pool, "O3")
            row(row_a[:, :], final_g, "rows_mix")
            row(row_b[:, :], ln_in_g_2, "rows_mix")
            row(row_c[:, :], ln_in_b_2, "rows_mix")
            pool.wait_ge(products, FIRST["att_out1"] + KT)
            pool.dma_start(wg_raw[:, :, :], w_in_2[0, :, 7 * D_HALF:].rearrange("(k p) n -> p k n", p=P))\
                .then_inc(loaded["wg"], 16)
            pool.wait_ge(xg_ready, 6 + len(LN_PARTS))
            row(row_mh[:, :], mh_norm_g_2[0], "mh")
            is_emptied(pool, "ymT")
            row(row_a[:, :], ln1_g_2[0], "rows_ln1")
            row(row_b[:, :], ln1_b_2[0], "rows_ln1")
            pool.dma_start(keys_raw[:, :, :], peer_keys_2[0].rearrange("h s n c -> n (h s) c"))\
                .then_inc(loaded["keys"], 16)

            nc.gpsimd.iota(iota_keys[:, :], pattern=[[1, N_KEYS]], base=0, channel_multiplier=0,
                           allow_small_or_imprecise_dtypes=True).then_inc(consts_done, 1)

            BODY = 2 * GATHER_SLOTS
            with pool.Fori(0, TILES * PICKS // BODY) as i:
                for n in range(BODY):
                    b, s = divmod(n, GATHER_SLOTS)
                    if s == 0:
                        pool.wait_ge(idx_ready[b], i + 1)
                    if s == GATHER_SLOTS // 2:
                        pool.wait_ge(products, CHUNKS)
                    pool.wait_ge(rows_used, i * BODY + (n + 1))
                    pool.nop(nofuse=True)
                    nc.gpsimd.indirect_dma_start(
                        out=ring[:, s, :], out_offset=None, in_=peer_u_2[0],
                        in_offset=bass.IndirectOffsetOnAxis(ap=idx[:, b, s:s + 1], axis=0),
                    ).then_inc(row_landed[s], 16)
            for t in range(TILES):
                with pool.Fori(0, PICKS // BODY) as i:
                    for n in range(BODY):
                        b, s = divmod(n, GATHER_SLOTS)
                        if s == 0:
                            pool.wait_ge(idx_ready[b], i + ((TILES + t) * PICKS // BODY + 1))
                        pool.wait_ge(v_used, i * BODY + (t * PICKS + n + 1))
                        pool.nop(nofuse=True)
                        nc.gpsimd.indirect_dma_start(
                            out=v_rows[n % V_SLOTS][:, :], out_offset=None,
                            in_=peer_v_2[0].rearrange("e (s d) -> (e s) d", s=V_PARTS),
                            in_offset=bass.IndirectOffsetOnAxis(ap=idx[:, b, s:s + 1], axis=0),
                        ).then_inc(v_landed[n % V_SLOTS], 16)
                if t == 0:
                    pool.wait_ge(v_products, D // P)
                    row(row_g2[:, :], ln2_g_2[0], "rows_ln2")
                    row(row_b2[:, :], ln2_b_2[0], "rows_ln2")

        @block.tensor
        def _(pe):
            mm = nc.tensor.matmul

            def multiply(half, c, xts, at):
                kts = KT * len(xts)
                for k in range(kts):
                    pe.wait_ge(split_done, c + (k + 1))
                    xt, kk, s = xts[k // KT], k % KT, k % SPLIT_SLOTS
                    for t in range(TILES):
                        tok = slice(t * P, (t + 1) * P)
                        for xp, wp in ((0, 0), (0, 1), (1, 0)):
                            for n in range(2):
                                last = mm(ps[half][:, 2 * t + n, :], xt[:, xp, kk, tok],
                                          w_split[:, s, wp, n * BANK:(n + 1) * BANK],
                                          start=(k == 0 and xp == 0 and wp == 0), stop=(k == kts - 1 and xp == 1))
                    last.then_inc(products, 1)
                    for job in at.get(k, ()):
                        job()

            def block_of(unit, xts, at={}):
                is_free(pe, unit)
                multiply(halves(unit), FIRST[unit], xts, at)

            def filled_by(last, unit):
                last.then_inc(half_filled[halves(unit)], 1)

            def turn(unit, tiles):
                is_free(pe, unit)
                hf = halves(unit)
                for n, (src, rows) in enumerate(tiles):
                    last = nc.tensor.transpose(by_128[hf][:, n, 0:rows], src, ident[0:rows, 0:rows])
                filled_by(last, unit)

            def turn_tokens(unit, src, first, count):
                turn(unit, [(src[:, t, k * P:(k + 1) * P], P) for k in range(first, first + count) for t in range(TILES)])

            def turn_part(name, q, src, count, tiles):
                def job():
                    pe.wait_ge(xg_ready, count + 1)
                    turn_tokens(f"{name}{q}", src, *tiles)
                return job

            def emptied(*units):
                def job():
                    for unit in units:
                        is_emptied(pe, unit)
                return job

            pe.wait_ge(consts_done, 1)
            for q in range(4):
                turn_part("xT_gmlp", q, xg, q, (4 * q, 4))()
            emptied("xT_gmlp0", "xT_gmlp1", "xT_gmlp2", "xT_gmlp3")()
            with pe.Fori(0, 2) as i:
                for n in range(2):
                    pe.wait_ge(half_free[n], i + NTH[f"gmlp_v{n}"][1])
                    multiply(n, i * (2 * KT) + FIRST[f"gmlp_v{n}"], (xT1,), {})

            def turn_ws():
                pe.wait_ge(loaded["ws"], 16)
                turn("ws", [(ws_raw[:, g, :], P) for g in range(GROUPS)])

            def turn_params():
                pe.wait_ge(loaded["params"], 48)
                turn("params", [(param_rows[:, :], 48)])

            def mix(u):
                def job():
                    unit = f"mix{u}"
                    pe.wait_ge(v_normed, TILES)
                    is_free(pe, unit)
                    hf = halves(unit)
                    for j in range(4):
                        g = 4 * u + j
                        for n in range(TILES):
                            last = mm(ps[hf][:, j, n * GROUP_DIM:(n + 1) * GROUP_DIM], wsT[:, g, :],
                                      gv[:, n, g * GROUP_DIM:(g + 1) * GROUP_DIM], start=True, stop=True)
                    filled_by(last, unit)
                return job

            def turn_y(u):
                def job():
                    pe.wait_ge(z_used, u + 2)
                    turn_tokens(f"yT_gmlp{u}", gu, 8 * u, 8)
                return job

            block_of("gmlp_u0", (xT1,), {3: [turn_ws], 6: [turn_params]})
            block_of("gmlp_u1", (xT1,))
            block_of("gmlp_u2", (xT1,), {4: [mix(0)], 9: [mix(1)]})
            block_of("gmlp_u3", (xT1,), {4: [mix(2)]})
            block_of("gmlp_z0", (xT1,), {4: [mix(3)]})
            block_of("gmlp_z1", (xT1,), {4: [turn_y(0)]})
            block_of("gmlp_z2", (xT1,), {4: [turn_y(1)]})
            emptied("yT_gmlp0", "yT_gmlp1")()
            block_of("gmlp_z3", (xT1,))
            block_of("gmlp_out0", (xT2, xT1), {4: [turn_y(2)], 8: [turn_y(3)], 15: [emptied("yT_gmlp2")],
                                               23: [emptied("yT_gmlp3")]})

            def turn_xg(u, count):
                def job():
                    pe.wait_ge(xg_ready, count)
                    turn_tokens(f"xT_att{u}", xg, 8 * u, 8)
                return job

            def turn_qk(u):
                def job():
                    w, b = divmod(u, 2)
                    is_emptied(pe, ("att_q", "att_k")[w] + str(b))
                    turn_tokens(f"qkT{u}", (q_tok, k_tok)[w][:, b, :, :], 0, 8)
                return job

            def att_z(g):
                unit = f"Z{g}"
                if g == 0:
                    emptied("qkT0", "qkT1", "qkT2", "qkT3")()
                is_free(pe, unit)
                hf = halves(unit)
                for j in range(4):
                    n = 4 * g + j
                    mm(ps[hf][:, j, 0:TOKENS], qkT[:, 1, n, 0:P], qkT[:, 0, n, :], start=True, stop=True)
                    last = mm(ps[hf][:, j, TOKENS:ZW], qkT[:, 1, n, P:TOKENS], qkT[:, 0, n, P:TOKENS],
                              start=True, stop=True)
                filled_by(last, unit)

            def att_l(g):
                unit = f"L{g}"
                pe.wait_ge(sp_done, g + 1)
                is_free(pe, unit)
                hf = halves(unit)
                for j in range(4):
                    s = sp_[:, g % 2, j, :]
                    mm(ps[hf][:, j, 0:TOKENS], onward[:, :], s[:, 0:TOKENS], start=True, stop=False)
                    mm(ps[hf][:, j, P:TOKENS], ones[:, 0:P], s[:, TOKENS:ZW], start=False, stop=True)
                    last = mm(ps[hf][:, j, TOKENS:ZW], onward[:, :], s[:, TOKENS:ZW], start=True, stop=True)
                filled_by(last, unit)

            def att_o(g):
                unit = f"O{g}"
                pe.wait_ge(a_done, g + 1)
                is_emptied(pe, f"att_v{g // 2}")
                is_free(pe, unit)
                hf = halves(unit)
                for j in range(4):
                    a = zs[:, g % 2, j, :]
                    c = (4 * g + j) * DH
                    mm(ps[hf][:, j, 0:DH], a[:, 0:P], av[:, 0, c:c + DH], start=True, stop=True)
                    mm(ps[hf][:, j, DH:2 * DH], a[:, P:TOKENS], av[:, 0, c:c + DH], start=True, stop=False)
                    last = mm(ps[hf][:, j, DH:2 * DH], a[:, TOKENS:ZW], av[:, 1, c:c + DH], start=False, stop=True)
                filled_by(last, unit)

            def turn_ay(u):
                def job():
                    pe.wait_ge(ay_done, u + 1)
                    turn_tokens(f"yT_att{u}", ay[:, u, :, :], 0, 8)
                return job

            block_of("gmlp_out1", (xT2, xT1), {18: [turn_xg(0, 5)]})
            is_emptied(pe, "xT_att0")
            block_of("att_q0", (xT2,), {4: [turn_xg(1, 6)], 7: [emptied("xT_att1")]})
            block_of("att_q1", (xT2,), {4: [turn_qk(0)]})
            block_of("att_k0", (xT2,), {4: [turn_qk(1)]})
            block_of("att_k1", (xT2,), {4: [turn_qk(2)]})
            block_of("att_v0", (xT2,), {4: [turn_qk(3)]})
            block_of("att_v1", (xT2,))
            block_of("att_z0", (xT2,), {0: [lambda: att_z(0)], 2: [lambda: att_z(1)], 5: [lambda: att_l(0)],
                                        8: [lambda: att_o(0)], 10: [lambda: att_l(1)], 12: [lambda: att_z(2)],
                                        15: [lambda: att_o(1)]})
            block_of("att_z1", (xT2,), {2: [lambda: att_l(2)], 4: [lambda: att_z(3)], 7: [lambda: att_o(2)],
                                        9: [lambda: att_l(3)], 12: [lambda: att_o(3)], 14: [turn_ay(0)]})
            is_emptied(pe, "yT_att0")
            block_of("att_out0", (xT1,), {4: [turn_ay(1)], 7: [emptied("yT_att1")]})
            block_of("att_out1", (xT1,))

            def normed_block(unit, name, count, at):
                parts = [turn_part(name, q, h, count + q, tiles) for q, tiles in enumerate(LN_PARTS)]
                there = [emptied(f"{name}{q}") for q in range(len(LN_PARTS))]
                parts[0]()
                there[0]()
                jobs = {0: [parts[1]], 1: [there[1], parts[2]], 3: [there[2]], 4: [parts[3]], 7: [there[3], parts[4]],
                        11: [there[4]]}
                for k, more in at.items():
                    jobs.setdefault(k, []).extend(more)
                block_of(unit, (xT2,), jobs)

            def turn_heads(unit, src, after):
                def job():
                    is_emptied(pe, after)
                    turn_tokens(unit, src, 0, M_HEADS)
                return job

            def gate_products():
                pe.wait_ge(wg_done, 1)
                is_free(pe, "gates")
                hf = halves("gates")
                for t in range(TILES):
                    for k in range(KT):
                        for xp, wp in ((0, 0), (0, 1), (1, 0)):
                            last = mm(ps[hf][:, t, 0:16], xT2[:, xp, k, t * P:(t + 1) * P], wg_split[:, wp, k, :],
                                      start=(k == 0 and xp + wp == 0), stop=(k == KT - 1 and xp == 1))
                filled_by(last, "gates")

            def cumulate():
                pe.wait_ge(logf_done, 1)
                is_free(pe, "cum")
                hf = halves("cum")
                mm(ps[hf][:, 0, 0:M_HEADS], upto[:, :], logf[:, 0, :], start=True, stop=True)
                mm(ps[hf][:, 1, 0:M_HEADS], upto[:, :], logf[:, 1, :], start=True, stop=False)
                filled_by(mm(ps[hf][:, 1, 0:M_HEADS], ones[:, 0:P], logf[:, 0, :], start=False, stop=True), "cum")

            def turn_c():
                pe.wait_ge(cc_done, 1)
                is_free(pe, "cT")
                hf = halves("cT")
                for t in range(TILES):
                    last = nc.tensor.transpose(ps[hf][0:M_HEADS, 0, t * P:(t + 1) * P], cc[:, t, :], ident[:, :])
                filled_by(last, "cT")

            def spread_g():
                pe.wait_ge(G_done, 1)
                is_free(pe, "G_rows")
                hf = halves("G_rows")
                for n in range(M_HEADS):
                    last = mm(flat[hf][:, n * TOKENS:(n + 1) * TOKENS],
                              ident[0:M_HEADS, n:n + 1].to_broadcast([M_HEADS, P]), G[:, :], start=True, stop=True)
                filled_by(last, "G_rows")

            def turn_g():
                is_free(pe, "G_cols")
                hf = halves("G_cols")
                for t in range(TILES):
                    last = nc.tensor.transpose(ps[hf][:, t, 0:M_HEADS], G[:, t * P:(t + 1) * P],
                                               ident[0:M_HEADS, 0:M_HEADS])
                filled_by(last, "G_cols")

            def m_scores(g):
                unit = f"MS{g}"
                emptied("mqT", "mkT")()
                is_free(pe, unit)
                hf = halves(unit)
                for j in range(4):
                    n = 4 * g + j
                    mm(ps[hf][:, j, 0:TOKENS], mqkT[:, 1, n, 0:P], mqkT[:, 0, n, :], start=True, stop=True)
                    last = mm(ps[hf][:, j, TOKENS:ZW], mqkT[:, 1, n, P:TOKENS], mqkT[:, 0, n, P:TOKENS],
                              start=True, stop=True)
                filled_by(last, unit)

            def m_out(g):
                unit = f"MO{g}"
                emptied(f"MS{g}", "mix_v")()
                pe.wait_ge(mv_ones, 1)
                is_free(pe, unit)
                hf = halves(unit)
                for j in range(4):
                    n, a = 4 * g + j, ms[:, g, j, :]
                    E = DH + 1
                    mm(ps[hf][:, j, 0:E], a[:, 0:P], mv[:, 0, n, :], start=True, stop=True)
                    mm(ps[hf][:, j, E:2 * E], a[:, P:TOKENS], mv[:, 0, n, :], start=True, stop=False)
                    last = mm(ps[hf][:, j, E:2 * E], a[:, TOKENS:ZW], mv[:, 1, n, :], start=False, stop=True)
                filled_by(last, unit)

            def turn_ym():
                pe.wait_ge(ym_done, 1)
                turn_tokens("ymT", hm[:, :, :, :].rearrange("p t n d -> p t (n d)"), 0, M_HEADS)

            normed_block("mix_q", "xT_mix", 6, {})
            block_of("mix_k", (xT2,), {4: [turn_heads("mqT", mqk_tok[:, 0, :, :], "mix_q")], 7: [gate_products],
                                       12: [cumulate]})
            block_of("mix_v", (xT2,), {4: [turn_heads("mkT", mqk_tok[:, 1, :, :], "mix_k")], 6: [turn_c], 8: [spread_g],
                                       12: [turn_g]})
            block_of("mix_cC", (xT2,), {4: [lambda: m_scores(0)], 7: [lambda: m_scores(1)], 10: [lambda: m_out(0)],
                                        13: [lambda: m_out(1)]})
            block_of("mix_ch", (xT2,))
            block_of("mix_cB", (xT2,), {4: [turn_heads("zT", cz, "mix_ch")]})
            block_of("mix_o", (xT2,), {4: [turn_heads("cBT", cB, "mix_cB")]})
            pe.wait_ge(yc_lo, 1)
            block_of("mix_out0", (xT1,), {4: [turn_ym], 7: [emptied("ymT")]})
            block_of("mix_out1", (xT1,))

            def turn_keys():
                pe.wait_ge(loaded["keys"], 16)
                turn("keysT", [(keys_raw[:, n, :], P) for n in range(2 * PEER_HEADS)])

            def turn_pq(u):
                def job():
                    is_emptied(pe, f"peer_q{u}")
                    turn_tokens(f"pqT{u}", pq_tok[:, u, :, :], 0, 8)
                return job

            def score(u):
                def job():
                    unit = f"scores{u}"
                    emptied(f"pqT{u}", "keysT")()
                    is_free(pe, unit)
                    hf = halves(unit)
                    for t in range(TILES):
                        for n in range(8):
                            last = mm(by_128[hf][:, 8 * t + n, :], pqT[:, 8 * u + n, t * P:(t + 1) * P],
                                      keysT[:, 8 * u + n, :], start=True, stop=True)
                    filled_by(last, unit)
                return job

            normed_block("peer_q0", "xT_peer", 6 + len(LN_PARTS), {8: [turn_keys]})
            block_of("peer_q1", (xT2,), {2: [turn_pq(0)], 4: [score(0)]})
            turn_pq(1)()
            score(1)()

            def turn_picks(unit, srcs):
                is_free(pe, unit)
                hf = halves(unit)
                for n, src in enumerate(srcs):
                    last = nc.tensor.transpose(ps[hf][:, 3, n * P:(n + 1) * P], src, ident[:, :])
                filled_by(last, unit)

            def scatter(t):
                with pe.Fori(0, P // SCATTER // 2) as i:
                    for s in range(2):
                        m = i * 2 + (t * (P // SCATTER) + s)
                        pe.wait_ge(onehot_done, m + 1)
                        pe.wait_ge(w_stored, m + 1)
                        for n in range(SCATTER):
                            last = mm(by_128[s][:, n, :], onehot_b[:, s, n, :], onehot_a[:, s, n, :], start=True, stop=True)
                        last.then_inc(scattered, 1)

            pe.sem_inc(scattered, 2)
            emptied("peer_q1")()
            for t in range(TILES):
                pe.wait_ge(keys_known, t + 1)
                turn_picks(f"pkT{t}", [pick_keys[:, t, half, :] for half in range(2)])
                pe.wait_ge(wgt_done, t + 1)
                turn_picks(f"wgtT{t}", [wgt[:, t * PICKS:(t + 1) * PICKS]])
                scatter(t)

            def multiply_v(c, s, first=False, last=False):
                def one(t, xp, vp):
                    for n in range(V_BANKS):
                        ins = mm(ps[t][:, n, :], w_x[s][:, xp, 1 - t, 0, :], v_split[s][:, vp, n * BANK:(n + 1) * BANK],
                                 start=first and xp + vp == 0, stop=last and vp == 1)
                    return ins

                pe.wait_ge(v_hi, c + 1)
                pe.wait_ge(w_hi, c + 1)
                for t in range(TILES):
                    one(t, 0, 0)
                pe.wait_ge(w_lo, c + 1)
                for t in range(TILES):
                    one(t, 1, 0)
                pe.wait_ge(v_lo, c + 1)
                for t in range(TILES):
                    ins = one(t, 0, 1)
                ins.then_inc(v_products, 1)

            pe.wait_ge(w_stored, TOKENS // SCATTER + 2)
            emptied("wgtT1")()
            multiply_v(0, 0, first=True)
            multiply_v(1, 1)
            with pe.Fori(1, N_KEYS // 2 - 1) as i:
                for s in range(2):
                    multiply_v(i * 2 + s, s)
            multiply_v(N_KEYS - 2, 0)
            multiply_v(N_KEYS - 1, 1, last=True)

        @block.scalar
        def _(act):
            fn = nc.scalar.activation
            step = step_counter(act, act_step)
            root_count = [0]
            square_count = [0]

            def round_hi(c, k):
                act.wait_ge(raw_landed[k % RAW_SLOTS], c * (16 // RAW_SLOTS) + 16 * (k // RAW_SLOTS + 1))
                if not (isinstance(c, int) and c + k < SPLIT_SLOTS):
                    act.wait_ge(products, c + (k + 1 - SPLIT_SLOTS))
                fn(w_split[:, k % SPLIT_SLOTS, 0, :], w_raw[:, k % RAW_SLOTS, :], ACT.Copy).then_inc(hi_done, 1)

            def through(c, kts=KT, at={}, last=False):
                for k in range(kts):
                    if not (last and k + AHEAD >= kts):
                        round_hi(c, k + AHEAD)
                    for job in at.get(k, ()):
                        job()
                act.wait_ge(products, c + kts)

            def block_of(unit, kts=KT, at={}, last=False):
                through(FIRST[unit], kts, at, last)

            def hi_x(unit, dst, count):
                def job():
                    is_filled(act, unit)
                    fn(dst[:, 0, :, :], by_tok[halves(unit)][:, 0:count, :], ACT.Copy).then_inc(xT_hi, 1)
                return job

            def take(unit, dst, src, func=ACT.Copy, **kw):
                fn(dst, src, func, **kw).then_inc(half_free[halves(unit)], 1)

            def take_scaled(hf, dst, func, scales):
                for t in range(TILES):
                    ins = fn(dst[t], by_tile[hf][:, t, :], func, scale=scales[:, t:t + 1])
                ins.then_inc(half_free[hf], 1)

            def copy_out(unit, dst, func=ACT.Copy):
                def job():
                    is_filled(act, unit)
                    take(unit, dst, flat[halves(unit)], func)
                return job

            def root_next(tiles=slice(0, TILES)):
                root_count[0] += 1
                act.wait_ge(stat, root_count[0])
                fn(root[:, tiles], meansq[:, tiles], ACT.Sqrt).then_inc(rooted, 1)

            def warm_up(func):
                fn(warm[:, :], ident[:, 0:1], func)

            def warm_root():
                warm_up(ACT.Sqrt)

            def sum_squares(src, part, trash):
                for t in range(TILES):
                    if square_count[0]:
                        act.wait_ge(squares, square_count[0])
                    square_count[0] += 1
                    fn(trash, src[:, t, :], ACT.Square, accum_out=sumsq[:, t, part:part + 1]).then_inc(squares, 1)

            for q in range(4):
                round_hi(0, q)
                hi_x(f"xT_gmlp{q}", xT1[:, :, 4 * q:4 * q + 4, :], 4)()
            act.wait_ge(loaded["x0"], 16)
            act.wait_ge(loaded["x1"], 16)
            sum_squares(h[:, :, :], 0, x_trash[:, :])
            root_next()
            act.wait_ge(rstd_ready, 1)
            with act.Fori(0, 2) as i:
                for n in range(2):
                    through(i * (2 * KT) + FIRST[f"gmlp_v{n}"])
                    cut = bass.ds(i * (2 * COLS) + n * COLS, COLS)
                    take_scaled(n, [gv[:, t, cut] for t in range(TILES)], ACT.Gelu_apprx_tanh, rstd)
            for n in range(4):
                block_of(f"gmlp_u{n}", at={14: [root_next]} if n == 0 else {})
                take_scaled(n % 2, [gu[:, t, n * COLS:(n + 1) * COLS] for t in range(TILES)], ACT.Gelu_apprx_tanh, rstd)
            for n in range(4):
                jobs = {}
                if n in (1, 2):
                    jobs = {4: [hi_x(f"yT_gmlp{n - 1}", xT2[:, :, 8 * (n - 1):8 * n, :], 8)]}
                block_of(f"gmlp_z{n}", at=jobs)
                act.wait_ge(z_used, n + 1)
                take_scaled(n % 2, [gz[:, t, :] for t in range(TILES)], ACT.Silu, rstd)
            block_of("gmlp_out0", 2 * KT, {4: [hi_x("yT_gmlp2", xT1[:, :, 0:8, :], 8)],
                                           8: [hi_x("yT_gmlp3", xT1[:, :, 8:16, :], 8)]})

            def att_squares(b):
                def job():
                    is_emptied(act, f"gmlp_out{b}")
                    sum_squares(h[:, :, b * COLS:(b + 1) * COLS], b, q_trash[:, :])
                return job

            block_of("gmlp_out1", 2 * KT, {2: [att_squares(0)], 18: [hi_x("xT_att0", xT2[:, :, 0:8, :], 8)]})
            block_of("att_q0", at={1: [att_squares(1)], 4: [hi_x("xT_att1", xT2[:, :, 8:16, :], 8)], 6: [root_next]})
            act.wait_ge(rstd_ready, 2)
            take_scaled(A, [q_tok[:, 0, t, :] for t in range(TILES)], ACT.Copy, rstd_q)

            def qk_turned(u):
                w, b = divmod(u, 2)
                return copy_out(f"qkT{u}", qkT[:, w, 8 * b:8 * b + 8, :].rearrange("p n t -> p (n t)"))

            block_of("att_q1", at={4: [qk_turned(0)]})
            take_scaled(B, [q_tok[:, 1, t, :] for t in range(TILES)], ACT.Copy, rstd_q)
            for b in range(2):
                block_of(f"att_k{b}", at={4: [qk_turned(1 + b)]})
                take_scaled(b, [k_tok[:, b, t, :] for t in range(TILES)], ACT.Copy, rstd)
            for b in range(2):
                block_of(f"att_v{b}", at={4: [qk_turned(3)]} if b == 0 else {})
                take_scaled(b, [av[:, t, b * COLS:(b + 1) * COLS] for t in range(TILES)], ACT.Copy, rstd)

            def att_copy(g):
                unit = f"Z{g}"
                is_filled(act, unit)
                if g >= 2:
                    is_emptied(act, f"O{g - 2}")
                take(unit, zs[:, g % 2, :, :], ps[halves(unit)][:, :, 0:ZW])

            def att_ln(g):
                act.wait_ge(abs_done, g + 1)
                s = sp_[:, g % 2, :, :]
                step(fn(s, s, ACT.Exp, scale=-1.0))
                fn(s, s, ACT.Ln, bias=1.0).then_inc(ln_done, 1)

            def att_exp(g):
                act.wait_ge(la_done, g + 1)
                z = zs[:, g % 2, :, :]
                fn(z, z, ACT.Exp).then_inc(a_done, 1)

            block_of("att_z0", at={0: [lambda: att_copy(0)], 1: [lambda: att_ln(0)], 2: [lambda: att_copy(1)],
                                   3: [lambda: att_ln(1)], 5: [lambda: att_exp(0)], 10: [lambda: att_exp(1)],
                                   12: [lambda: att_copy(2)], 13: [lambda: att_ln(2)]})
            take_scaled(A, [az[:, 0, t, :] for t in range(TILES)], ACT.Silu, rstd)
            block_of("att_z1", at={2: [lambda: att_exp(2)], 4: [lambda: att_copy(3)], 5: [lambda: att_ln(3)],
                                   9: [lambda: att_exp(3)], 14: [hi_x("yT_att0", xT1[:, :, 0:8, :], 8)]})
            take_scaled(A, [az[:, 1, t, :] for t in range(TILES)], ACT.Silu, rstd)
            block_of("att_out0", at={4: [hi_x("yT_att1", xT1[:, :, 8:16, :], 8)]})

            def mix_squares(b):
                def job():
                    is_emptied(act, f"att_out{b}")
                    sum_squares(h[:, :, b * COLS:(b + 1) * COLS], b, p_trash[:, :])
                return job

            def normed_parts(name):
                return [hi_x(f"{name}{q}", xT2[:, :, k:k + n, :], n) for q, (k, n) in enumerate(LN_PARTS)]

            block_of("att_out1", at={2: [mix_squares(0)], 15: [warm_root]})
            mix_squares(1)()
            root_next()

            def gate_hi():
                act.wait_ge(loaded["wg"], 16)
                fn(wg_split[:, 0, :, :], wg_raw[:, :, :], ACT.Copy).then_inc(wg_hi, 1)

            def gate_log():
                act.wait_ge(gate_abs, 1)
                step(fn(gabs[:, :, :], gabs[:, :, :], ACT.Exp, scale=-1.0))
                fn(gabs[:, :, :], gabs[:, :, :], ACT.Ln, bias=1.0).then_inc(gate_ln, 1)

            def m_weights():
                is_emptied(act, "G_rows")
                fn(mw[:, :, :], mw[:, :, :], ACT.Exp, scale=-1.0).then_inc(mw_done, 1)

            def m_floor():
                is_emptied(act, "G_cols")
                fn(cmin[:, :, :], cmin[:, :, :], ACT.Exp, scale=-1.0).then_inc(m_exp, 1)

            def turned(unit, dst):
                return copy_out(unit, dst.rearrange("p n t -> p (n t)"))

            def head_root():
                act.wait_ge(hm_sq, 1)
                fn(mrs[:, :, :], mrs[:, :, :], ACT.Sqrt).then_inc(hm_root, 1)

            def conv_hi():
                act.wait_ge(yc_done, 1)
                fn(xT1[:, 0, 0:8, :], yc[:, :, :], ACT.Copy).then_inc(yc_hi, 1)

            parts = normed_parts("xT_mix")
            parts[0]()
            block_of("mix_q", at={0: [parts[1]], 1: [parts[2]], 4: [parts[3]], 7: [parts[4]], 8: [gate_hi]})
            take("mix_q", mqk_tok[:, 0, :, :], by_tile[A], scale=DH ** -0.5)
            block_of("mix_k", at={4: [turned("mqT", mqkT[:, 0, :, :])], 9: [gate_log]})
            take("mix_k", mqk_tok[:, 1, :, :], by_tile[B])
            block_of("mix_v", at={4: [turned("mkT", mqkT[:, 1, :, :])], 11: [m_weights], 14: [m_floor]})
            take("mix_v", mv[:, :, :, 0:DH], by_tile[A].rearrange("p t (n d) -> p t n d", d=DH))
            block_of("mix_cC")
            take("mix_cC", cz[:, :, :], by_tile[B])
            block_of("mix_ch", at={11: [head_root]})
            block_of("mix_cB", at={4: [lambda: (is_filled(act, "zT"),
                                                take("zT", zT[:, :, 2:], by_tok[halves("zT")]))]})
            take("mix_cB", cB[:, :, :], by_tile[B])
            block_of("mix_o", at={4: [turned("cBT", cBT[:, :, :])], 7: [conv_hi]})
            take("mix_o", mo[:, :, :], by_tile[A], ACT.Sigmoid)
            block_of("mix_out0", at={4: [hi_x("ymT", xT1[:, :, 8:16, :], 8)]})
            block_of("mix_out1", at={15: [warm_root]})
            root_next()

            parts = normed_parts("xT_peer")
            parts[0]()
            block_of("peer_q0", at={0: [parts[1]], 1: [parts[2]], 4: [parts[3]], 7: [parts[4]], 8: [turned("keysT", keysT[:, :, :])]})
            take("peer_q0", pq_tok[:, 0, :, :], by_tile[A])

            def scores_out(u):
                return copy_out(f"scores{u}", scores[u][:, :, :, :].rearrange("p t n k -> p (t n k)"))

            block_of("peer_q1", at={2: [turned("pqT0", pqT[:, 0:8, :])], 4: [scores_out(0)]}, last=True)
            take("peer_q1", pq_tok[:, 1, :, :], by_tile[B])
            turned("pqT1", pqT[:, 8:16, :])()
            scores_out(1)()
            def gate_exponent(n):
                t, q = divmod(n, TILE_GROUPS)
                act.wait_ge(gate_sub, n + 1)
                cut = gate[:, t, q * GROUP_HEADS:(q + 1) * GROUP_HEADS, :]
                fn(cut, cut, ACT.Exp).then_inc(gate_exp, 1)

            def pick_gelu(t):
                act.wait_ge(idx_ready[1], (t + 1) * PICKS // (2 * GATHER_SLOTS) + 1)
                cut = wgt[:, t * PICKS:(t + 1) * PICKS]
                fn(cut, cut, ACT.Gelu).then_inc(gelu_done, 1)

            def picks_out(unit, dst, count):
                is_filled(act, unit)
                hf = halves(unit)
                take(unit, dst, ps[hf][:, 3, 0:count * P].rearrange("p (k t) -> p k t", t=P))

            def store_w(t, first, count):
                with act.Fori(0, count // 2) as i:
                    for s in range(2):
                        m = i * 2 + (first + s)
                        act.wait_ge(scattered, m + (t * (P // SCATTER) + 3))
                        fn(wT[:, 1 - t, :, bass.ds(m * SCATTER, SCATTER)],
                           by_128[s][:, 0:SCATTER, :].rearrange("p n a -> p a n"), ACT.Copy).then_inc(w_stored, 1)

            act.sem_inc(w_stored, 2)

            def round_w(c, s):
                if not isinstance(c, int):
                    act.wait_ge(v_products, c - 1)
                fn(w_x[s][:, 0, :, :, :], wT[:, :, bass.ds(c, 1), :], ACT.Copy).then_inc(w_hi, 1)

            def round_v(c, s):
                act.wait_ge(v_raw_landed[s], c * 8 + (16 - 8 * s))
                fn(v_split[s][:, 0, :], v_raw[s][:, :], ACT.Copy).then_inc(v_hi, 1)

            for n in range(TILE_GROUPS + 1):
                gate_exponent(n)
            pick_gelu(0)
            picks_out("pkT0", picksT[:, 0:2, 0:P], 2)
            picks_out("wgtT0", picksT[:, 2:3, 0:P], 1)
            share = P // SCATTER // TILE_GROUPS
            for q in range(TILE_GROUPS):
                store_w(0, q * share, share)
                if q + 1 < TILE_GROUPS:
                    gate_exponent(TILE_GROUPS + q + 1)
            picks_out("pkT1", picksT[:, 0:2, P:], 2)
            warm_up(ACT.Gelu)
            pick_gelu(1)
            picks_out("wgtT1", picksT[:, 2:3, P:], 1)
            round_v(0, 0)
            store_w(1, 0, P // SCATTER)
            act.wait_ge(w_stored, TOKENS // SCATTER + 2)
            for s in range(2):
                round_w(s, s)
            round_v(1, 1)
            with act.Fori(1, N_KEYS // 2) as i:
                for s in range(2):
                    round_w(i * 2 + s, s)
                    round_v(i * 2 + s, s)

            warm_root()
            for t in range(TILES):
                root_next(slice(t, t + 1))
                act.wait_ge(shift_ready, t + 1)
                for b in range(2):
                    cut = h[:, t, b * COLS:(b + 1) * COLS]
                    fn(cut, cut, ACT.Identity, bias=shift[:, t:t + 1], scale=rstd[:, t:t + 1]).then_inc(normed, 1)

        @block.vector
        def _(dve):
            v = nc.vector
            step = step_counter(dve, dve_step)
            xt_count = [0]
            root_count = [0]
            rstd_count = [0]

            def split_lo(c, k):
                dve.wait_ge(hi_done, c + (k + 1))
                s = k % SPLIT_SLOTS
                v.tensor_tensor(w_split[:, s, 1, :], w_raw[:, k % RAW_SLOTS, :], w_split[:, s, 0, :].bitcast(F32),
                                ALU.subtract).then_inc(split_done, 1)

            def through(c, kts=KT, at={}, last=False):
                for k in range(kts):
                    if not (last and k + AHEAD >= kts):
                        split_lo(c, k + AHEAD)
                    for job in at.get(k, ()):
                        job()

            def block_of(unit, kts=KT, at={}, last=False):
                through(FIRST[unit], kts, at, last)

            def lo_x(unit, dst, count):
                def job():
                    xt_count[0] += 1
                    dve.wait_ge(xT_hi, xt_count[0])
                    hf = halves(unit)
                    v.tensor_tensor(dst[:, 1, :, :], by_tok[hf][:, 0:count, :], dst[:, 0, :, :].bitcast(F32), ALU.subtract)\
                        .then_inc(half_free[hf], 1)
                return job

            def gained(dst, src, gain, lo, hi):
                return v.tensor_tensor(dst[:, :, lo:hi], src[:, :, lo:hi],
                                       gain[:, lo:hi].unsqueeze(1).to_broadcast([P, TILES, hi - lo]), ALU.mult)

            def mean_square(parts, width, count):
                dve.wait_ge(squares, count)
                total = sumsq[:, :, 0]
                if parts == 2:
                    total = meansq[:, :]
                    step(v.tensor_tensor(total, sumsq[:, :, 0], sumsq[:, :, 1], ALU.add))
                return v.tensor_scalar(meansq[:, :], total, 1.0 / width, RMS_EPS, ALU.mult, ALU.add)

            def inverse_root(dst, tiles=slice(0, TILES)):
                root_count[0] += 1
                dve.wait_ge(rooted, root_count[0])
                return v.reciprocal(dst, root[:, tiles])

            def add_to_h(unit, scale=1.0):
                n, hf = int(unit[-1]), halves(unit)
                dst = h[:, :, n * COLS:(n + 1) * COLS]
                v.scalar_tensor_tensor(out=dst, in0=dst, scalar=scale, in1=by_tile[hf], op0=ALU.mult, op1=ALU.add)\
                    .then_inc(half_free[hf], 1)
                is_emptied(dve, unit)

            def block_stats(src, b):
                for t in range(TILES):
                    for n in (2 * b, 2 * b + 1):
                        ins = v.bn_stats(bn[:, t, n, :], src[:, t, n * BANK:(n + 1) * BANK])
                return ins

            def tile_moments(t):
                return v.bn_aggr(moments[:, t, :], bn[:, t, :, :].rearrange("p n s -> p (n s)"))

            def normalise(src, t, lo, hi):
                return v.tensor_scalar(h[:, t, lo:hi], src[:, t, lo:hi], moments[:, t, 0:1], rstd[:, t:t + 1],
                                       ALU.subtract, ALU.mult)

            def norm_part(src, gain, bias, first, count):
                def job():
                    lo, hi = first * P, (first + count) * P
                    for t in range(TILES):
                        ins = normalise(src, t, lo, hi)
                    step(ins)
                    step(gained(h, h, gain, lo, hi))
                    cut = h[:, :, lo:hi]
                    v.tensor_tensor(cut, cut, bias[:, lo:hi].unsqueeze(1).to_broadcast([P, TILES, hi - lo]), ALU.add)\
                        .then_inc(xg_ready, 1)
                return job

            def magnitude(dst, src):
                return v.scalar_tensor_tensor(out=dst, in0=src, scalar=-1.0, in1=src, op0=ALU.mult, op1=ALU.max)

            for q in range(4):
                if q % 2 == 0:
                    dve.wait_ge(loaded[f"x{q // 2}"], 16)
                    dve.wait_ge(loaded[f"gain{q // 2}"], 16)
                gained(xg, h, row_norm, q * BANK, (q + 1) * BANK).then_inc(xg_ready, 1)
            for q in range(4):
                lo_x(f"xT_gmlp{q}", xT1[:, :, 4 * q:4 * q + 4, :], 4)()
                split_lo(0, q)
            mean_square(1, D, TILES).then_inc(stat, 1)
            inverse_root(rstd[:, :]).then_inc(rstd_ready, 1)
            with dve.Fori(0, 2) as i:
                for n in range(2):
                    through(i * (2 * KT) + FIRST[f"gmlp_v{n}"])

            def causal_ws():
                is_filled(dve, "ws")
                dve.wait_ge(consts_done, 2)
                hf = halves("ws")
                v.tensor_tensor(wsT[:, :, :], by_128[hf], upto[:, :].unsqueeze(1).to_broadcast([P, GROUPS, P]), ALU.mult)\
                    .then_inc(half_free[hf], 1)

            def take_params():
                is_filled(dve, "params")
                hf = halves("params")
                v.tensor_copy(cols[:, :], flat[hf][:, 0:48]).then_inc(half_free[hf], 1)

            def v_square(n):
                def job():
                    t, part = divmod(n, 2)
                    is_emptied(dve, "gmlp_v2")
                    is_emptied(dve, "gmlp_v3")
                    if n:
                        dve.wait_ge(v_squared, n)
                    src = gv[:, t, part * D:(part + 1) * D]
                    v.tensor_tensor_reduce(out=gz[:, :, :].rearrange("p a b -> p (a b)"), in0=src, in1=src, scale=1.0,
                                           scalar=0.0, op0=ALU.mult, op1=ALU.add,
                                           accum_out=sumsq[:, t, part:part + 1]).then_inc(v_squared, 1)
                return job

            def v_stat():
                dve.wait_ge(v_squared, 4)
                step(v.tensor_tensor(meansq[:, :], sumsq[:, :, 0], sumsq[:, :, 1], ALU.add))
                v.tensor_scalar(meansq[:, :], meansq[:, :], 1.0 / GMLP_W, RMS_EPS, ALU.mult, ALU.add).then_inc(stat, 1)

            def v_norm(t):
                def job():
                    if t == 0:
                        inverse_root(rstd_v[:, :]).then_inc(z_used, 1)
                        dve.wait_ge(z_used, 1)
                        dve.wait_ge(loaded["row_v"], 16)
                    v.scalar_tensor_tensor(out=gv[:, t, :], in0=gv[:, t, :], scalar=rstd_v[:, t:t + 1], in1=row_v[:, :],
                                           op0=ALU.mult, op1=ALU.mult).then_inc(v_normed, 1)
                return job

            def mixed(u):
                def job():
                    unit = f"mix{u}"
                    is_filled(dve, unit)
                    is_emptied(dve, f"gmlp_u{u}")
                    hf = halves(unit)
                    for j in range(4):
                        g = 4 * u + j
                        for n in range(TILES):
                            dst = gu[:, n, g * GROUP_DIM:(g + 1) * GROUP_DIM]
                            ins = v.scalar_tensor_tensor(out=dst, in0=ps[hf][:, j, n * GROUP_DIM:(n + 1) * GROUP_DIM],
                                                         scalar=cols[:, g:g + 1], in1=dst, op0=ALU.add, op1=ALU.mult)
                    ins.then_inc(half_free[hf], 1)
                return job

            def times_z(n):
                def job():
                    is_emptied(dve, f"gmlp_z{n}")
                    is_emptied(dve, f"mix{n}")
                    dst = gu[:, :, n * COLS:(n + 1) * COLS]
                    v.tensor_tensor(dst, dst, gz[:, :, :], ALU.mult).then_inc(z_used, 1)
                return job

            block_of("gmlp_u0", at={3: [causal_ws], 6: [take_params], 7: [v_square(0)], 9: [v_square(1)],
                                    11: [v_square(2)], 13: [v_square(3), v_stat]})
            block_of("gmlp_u1", at={1: [v_norm(0)], 5: [v_norm(1)]})
            block_of("gmlp_u2", at={4: [mixed(0)], 9: [mixed(1)]})
            block_of("gmlp_u3", at={4: [mixed(2)]})
            block_of("gmlp_z0", at={4: [mixed(3)]})
            block_of("gmlp_z1", at={0: [times_z(0)], 4: [lo_x("yT_gmlp0", xT2[:, :, 0:8, :], 8)]})
            block_of("gmlp_z2", at={0: [times_z(1)], 4: [lo_x("yT_gmlp1", xT2[:, :, 8:16, :], 8)]})
            block_of("gmlp_z3", at={0: [times_z(2)]})
            block_of("gmlp_out0", 2 * KT, {0: [times_z(3)], 4: [lo_x("yT_gmlp2", xT1[:, :, 0:8, :], 8)],
                                           8: [lo_x("yT_gmlp3", xT1[:, :, 8:16, :], 8)]})

            def att_gain(b):
                def job():
                    unit = f"gmlp_out{b}"
                    dve.wait_ge(products, FIRST[unit] + 2 * KT)
                    add_to_h(unit)
                    dve.wait_ge(loaded["row_norm1"], 16)
                    gained(xg, h, row_norm, b * COLS, (b + 1) * COLS).then_inc(xg_ready, 1)
                return job

            def att_rstd():
                step(inverse_root(rstd[:, :]))
                v.tensor_scalar(rstd_q[:, :], rstd[:, :], DH ** -0.5, None, ALU.mult).then_inc(rstd_ready, 1)

            att_gain(0)()
            block_of("gmlp_out1", 2 * KT, {18: [lo_x("xT_att0", xT2[:, :, 0:8, :], 8)]})
            att_gain(1)()
            block_of("att_q0", at={4: [lo_x("xT_att1", xT2[:, :, 8:16, :], 8),
                                       lambda: mean_square(2, D, 3 * TILES).then_inc(stat, 1)],
                                   7: [att_rstd]})
            for unit in ("att_q1", "att_k0", "att_k1", "att_v0", "att_v1"):
                block_of(unit)
            diag = lambda m: m.rearrange("p j (k t) -> p j k t", t=P)[:, :, 0:3:2, :]
            over = lambda m, n: m.unsqueeze(1).unsqueeze(1).to_broadcast([P, n, 2, P])

            def att_abs(g):
                is_emptied(dve, f"Z{g}")
                magnitude(sp_[:, g % 2, :, :], zs[:, g % 2, :, :]).then_inc(abs_done, 1)

            def att_sp(g):
                dve.wait_ge(ln_done, g + 1)
                s = sp_[:, g % 2, :, :]
                step(v.scalar_tensor_tensor(out=s, in0=zs[:, g % 2, :, :], scalar=0.0, in1=s, op0=ALU.max, op1=ALU.add))
                v.tensor_tensor(diag(s), diag(s), over(before[:, :], 4), ALU.mult).then_inc(sp_done, 1)

            def att_la(g):
                unit = f"L{g}"
                is_filled(dve, unit)
                z = zs[:, g % 2, :, :]
                v.tensor_tensor(z, z, ps[halves(unit)][:, :, 0:ZW], ALU.subtract).then_inc(half_free[halves(unit)], 1)
                is_emptied(dve, unit)
                v.tensor_tensor(diag(z), diag(z), over(barred[:, :], 4), ALU.add).then_inc(la_done, 1)

            def att_out(g):
                unit = f"O{g}"
                is_filled(dve, unit)
                hf = halves(unit)
                src = ps[hf][:, :, 0:2 * DH].rearrange("p j (t d) -> p j t d", d=DH)
                b, c = g // 2, (g % 2) * 4 * DH
                dst = ao[:, b, :, c:c + 4 * DH].rearrange("p t (j d) -> p j t d", d=DH)
                v.tensor_copy(dst, src).then_inc(half_free[hf], 1)

            def att_gate(b):
                def job():
                    for unit in (f"O{2 * b}", f"O{2 * b + 1}", f"att_z{b}"):
                        is_emptied(dve, unit)
                    v.tensor_tensor(ay[:, b, :, :], ao[:, b, :, :], az[:, b, :, :], ALU.mult).then_inc(ay_done, 1)
                return job

            block_of("att_z0", at={0: [lambda: att_abs(0)], 1: [lambda: att_sp(0)], 2: [lambda: att_abs(1)],
                                   3: [lambda: att_sp(1)], 5: [lambda: att_la(0)], 8: [lambda: att_out(0)],
                                   10: [lambda: att_la(1)], 12: [lambda: att_abs(2)], 13: [lambda: att_sp(2)],
                                   15: [lambda: att_out(1)]})
            block_of("att_z1", at={2: [lambda: att_la(2)], 4: [lambda: att_abs(3)], 5: [lambda: att_sp(3)],
                                   7: [lambda: att_out(2)], 8: [att_gate(0)], 9: [lambda: att_la(3)],
                                   12: [lambda: att_out(3)], 14: [lo_x("yT_att0", xT1[:, :, 0:8, :], 8)]})
            block_of("att_out0", at={0: [att_gate(1)], 4: [lo_x("yT_att1", xT1[:, :, 8:16, :], 8)]})

            def mix_gain(b):
                unit = f"att_out{b}"
                dve.wait_ge(products, FIRST[unit] + KT)
                add_to_h(unit)
                dve.wait_ge(loaded["rows_mix"], 48)
                step(gained(p_, h, row_a, b * COLS, (b + 1) * COLS))
                return block_stats(p_, b)

            mix_gain(0)
            block_of("att_out1")
            step(mix_gain(1))
            for t in range(TILES):
                tile_moments(t)
            step(mean_square(2, D, 5 * TILES))
            v.scalar_tensor_tensor(out=meansq[:, :], in0=meansq[:, :], scalar=LN_EPS, in1=moments[:, :, 1], op0=ALU.mult,
                                   op1=ALU.add).then_inc(stat, 1)
            step(inverse_root(rstd[:, :]))

            def gate_lo():
                dve.wait_ge(wg_hi, 1)
                v.tensor_tensor(wg_split[:, 1, :, :], wg_raw[:, :, :], wg_split[:, 0, :, :].bitcast(F32), ALU.subtract)\
                    .then_inc(wg_done, 1)

            def gate_values():
                is_filled(dve, "gates")
                hf = halves("gates")
                dve.wait_ge(loaded["gate"], 16)
                v.tensor_tensor(gates[:, :, :], ps[hf][:, 0:2, 0:16],
                                row_gate[:, :].unsqueeze(1).to_broadcast([P, TILES, 16]), ALU.add)\
                    .then_inc(half_free[hf], 1)
                is_emptied(dve, "gates")
                magnitude(gabs[:, :, :], gates[:, :, M_HEADS:]).then_inc(gate_abs, 1)

            def gate_logs():
                dve.wait_ge(gate_ln, 1)
                v.scalar_tensor_tensor(out=logf[:, :, :], in0=gates[:, :, M_HEADS:], scalar=0.0, in1=gabs[:, :, :],
                                       op0=ALU.min, op1=ALU.subtract).then_inc(logf_done, 1)

            def cumulated():
                is_filled(dve, "cum")
                hf = halves("cum")
                v.tensor_copy(Bc[:, :, :], ps[hf][:, 0:2, 0:M_HEADS]).then_inc(half_free[hf], 1)
                is_emptied(dve, "cum")
                v.tensor_tensor(cc[:, :, :], gates[:, :, 0:M_HEADS], Bc[:, :, :], ALU.subtract).then_inc(cc_done, 1)

            def running_max():
                is_filled(dve, "cT")
                hf = halves("cT")
                v.tensor_copy(c_rows[:, :], ps[hf][0:M_HEADS, 0, 0:TOKENS]).then_inc(half_free[hf], 1)
                is_emptied(dve, "cT")
                v.tensor_tensor_scan(G[:, :], ones[0:M_HEADS, :], c_rows[:, :], 0.0, ALU.mult, ALU.max).then_inc(G_done, 1)

            def m_arguments():
                is_filled(dve, "G_rows")
                hf = halves("G_rows")
                for n in range(M_HEADS):
                    for t, (lo, hi) in enumerate(((0, TOKENS), (TOKENS, ZW))):
                        src = flat[hf][:, n * TOKENS + t * P:(n + 1) * TOKENS]
                        ins = v.tensor_scalar(mw[:, n, lo:hi], src, cc[:, t, n:n + 1], 0.0, ALU.subtract, ALU.max)
                ins.then_inc(half_free[hf], 1)

            def m_mask():
                dve.wait_ge(mw_done, 1)
                v.tensor_tensor(diag(mw[:, :, :]), diag(mw[:, :, :]), over(upto[:, :], M_HEADS), ALU.mult)\
                    .then_inc(mw_masked, 1)

            def m_totals():
                is_filled(dve, "G_cols")
                hf = halves("G_cols")
                v.tensor_tensor(cmin[:, :, :], ps[hf][:, 0:2, 0:M_HEADS], Bc[:, :, :], ALU.add).then_inc(half_free[hf], 1)

            def m_weigh(g):
                def job():
                    unit = f"MS{g}"
                    is_filled(dve, unit)
                    dve.wait_ge(mw_masked, 1)
                    hf = halves(unit)
                    v.tensor_tensor(ms[:, g, :, :], ps[hf][:, :, 0:ZW], mw[:, 4 * g:4 * g + 4, :], ALU.mult)\
                        .then_inc(half_free[hf], 1)
                return job

            def m_divide(g):
                def job():
                    unit = f"MO{g}"
                    is_filled(dve, unit)
                    dve.wait_ge(m_exp, 1)
                    hf = halves(unit)
                    o = ps[hf][:, :, 0:2 * (DH + 1)].rearrange("p j (t e) -> p j t e", e=DH + 1)
                    den = mden[:, :, :]
                    step(v.tensor_copy(den, o[:, :, :, DH]))
                    step(magnitude(den, den))
                    step(v.tensor_tensor(den, den, cmin[:, :, 4 * g:4 * g + 4].rearrange("p t j -> p j t"), ALU.max))
                    step(v.reciprocal(den, den))
                    v.tensor_tensor(hm[:, :, 4 * g:4 * g + 4, :].rearrange("p t j d -> p j t d"), o[:, :, :, 0:DH],
                                    den.unsqueeze(3).to_broadcast([P, 4, TILES, DH]), ALU.mult).then_inc(half_free[hf], 1)
                    is_emptied(dve, unit)
                return job

            wide = lambda m: m.unsqueeze(3).to_broadcast([P, TILES, M_HEADS, DH])
            hm4 = hm[:, :, :, :]
            hm3 = hm4.rearrange("p t n d -> p t (n d)")

            def head_sum():
                step(v.tensor_reduce(mmu[:, :, :], hm4, AX_X, ALU.add))
                step(v.tensor_scalar(mmu[:, :, :], mmu[:, :, :], 1.0 / DH, None, ALU.mult))

            def head_centre():
                step(v.tensor_tensor(hm4, hm4, wide(mmu[:, :, :]), ALU.subtract))

            def head_square():
                step(v.tensor_tensor(hsq[:, :, :, :], hm4, hm4, ALU.mult))

            def head_variance():
                step(v.tensor_reduce(mrs[:, :, :], hsq[:, :, :, :], AX_X, ALU.add))
                v.tensor_scalar(mrs[:, :, :], mrs[:, :, :], 1.0 / DH, LN_EPS, ALU.mult, ALU.add).then_inc(hm_sq, 1)

            def head_scale():
                dve.wait_ge(hm_root, 1)
                step(v.reciprocal(mrs[:, :, :], mrs[:, :, :]))
                step(v.tensor_tensor(hm4, hm4, wide(mrs[:, :, :]), ALU.mult))

            def head_gain():
                dve.wait_ge(loaded["mh"], 16)
                step(v.tensor_tensor(hm3, hm3, row_mh[:, :].unsqueeze(1).to_broadcast([P, TILES, D_HALF]), ALU.mult))

            def conv_tap(j):
                def job():
                    if j == CONV_K - 1:
                        is_emptied(dve, "zT")
                        dve.wait_ge(zT_pad, 1)
                    for f in range(M_HEADS):
                        w = cols[:, 16 + 8 * j + f:17 + 8 * j + f]
                        src = zT[:, f, j:j + TOKENS]
                        if j == CONV_K - 1:
                            ins = v.tensor_scalar(yc[:, f, :], src, w, cols[:, 40 + f:41 + f], ALU.mult, ALU.add)
                        else:
                            ins = v.scalar_tensor_tensor(out=yc[:, f, :], in0=src, scalar=w, in1=yc[:, f, :],
                                                         op0=ALU.mult, op1=ALU.add)
                    step(ins)
                return job

            def conv_gate():
                is_emptied(dve, "cBT")
                v.tensor_tensor(yc[:, :, :], yc[:, :, :], cBT[:, :, :], ALU.mult).then_inc(yc_done, 1)

            def conv_lo():
                dve.wait_ge(yc_hi, 1)
                v.tensor_tensor(xT1[:, 1, 0:8, :], yc[:, :, :], xT1[:, 0, 0:8, :].bitcast(F32), ALU.subtract)\
                    .then_inc(yc_lo, 1)

            def m_gate():
                is_emptied(dve, "mix_o")
                v.tensor_tensor(hm3, hm3, mo[:, :, :], ALU.mult).then_inc(ym_done, 1)

            def zero_pad():
                v.memset(zT[:, :, 0:2], 0.0).then_inc(zT_pad, 1)

            def normed_parts(name, src, gain, bias):
                return ([norm_part(src, gain, bias, *tiles) for tiles in LN_PARTS],
                        [lo_x(f"{name}{q}", xT2[:, :, k:k + n, :], n) for q, (k, n) in enumerate(LN_PARTS)])

            norm, lo_of = normed_parts("xT_mix", p_, row_b, row_c)
            for job in (norm[0], norm[1], lo_of[0], norm[2], lo_of[1], norm[3]):
                job()
            block_of("mix_q", at={1: [lo_of[2]], 2: [norm[4]], 4: [lo_of[3]], 7: [lo_of[4]], 8: [gate_lo]})
            block_of("mix_k", at={7: [gate_values], 10: [gate_logs], 12: [cumulated]})
            v.memset(mv[:, :, :, DH:DH + 1], 1.0).then_inc(mv_ones, 1)
            block_of("mix_v", at={6: [running_max], 8: [m_arguments], 12: [m_mask, m_totals]})
            block_of("mix_cC", at={4: [m_weigh(0)], 7: [m_weigh(1), zero_pad], 10: [m_divide(0)], 13: [m_divide(1)]})
            block_of("mix_ch", at={1: [head_sum], 4: [head_centre], 6: [head_square], 8: [head_variance],
                                   11: [head_scale], 13: [head_gain]})
            is_emptied(dve, "mix_cC")
            dve.wait_ge(products, FIRST["mix_ch"] + KT)
            v.tensor_tensor(cz[:, :, :], by_tile[A], cz[:, :, :], ALU.mult).then_inc(half_free[A], 1)
            block_of("mix_cB", at={7: [conv_tap(2)], 10: [conv_tap(1)], 13: [conv_tap(0)]})
            block_of("mix_o", at={5: [conv_gate], 7: [conv_lo]})
            block_of("mix_out0", at={0: [m_gate], 4: [lo_x("ymT", xT1[:, :, 8:16, :], 8)]})

            def mix_add(b):
                unit = f"mix_out{b}"
                dve.wait_ge(products, FIRST[unit] + KT)
                add_to_h(unit, ALPHA)
                return block_stats(h, b)

            def deviation():
                v.tensor_scalar(meansq[:, :], moments[:, :, 1], LN_EPS, None, ALU.add).then_inc(stat, 1)
                step(inverse_root(rstd[:, :]))

            mix_add(0)
            block_of("mix_out1")
            step(mix_add(1))
            for t in range(TILES):
                ins = tile_moments(t)
            step(ins)
            deviation()
            dve.wait_ge(loaded["rows_ln1"], 32)
            norm, lo_of = normed_parts("xT_peer", h, row_a, row_b)
            for job in (norm[0], norm[1], lo_of[0], norm[2], lo_of[1], norm[3]):
                job()
            block_of("peer_q0", at={1: [lo_of[2]], 2: [norm[4]], 4: [lo_of[3]], 7: [lo_of[4]]})

            def best16(values, rest, top, where, groups):
                def first_eight():
                    for n in range(groups):
                        ins = v.max(top[:, n, 0:8], values[:, n, :])
                    step(ins)
                    for n in range(groups):
                        v.max_index(where[:, n, 0:8], top[:, n, 0:8], values[:, n, :])
                        ins = v.match_replace(rest[:, n, :], top[:, n, 0:8], values[:, n, :], LOWEST)
                    step(ins)

                def next_eight():
                    for n in range(groups):
                        ins = v.max(top[:, n, 8:16], rest[:, n, :])
                    step(ins)
                    for n in range(groups):
                        ins = v.max_index(where[:, n, 8:16], top[:, n, 8:16], rest[:, n, :])
                    step(ins)
                return [first_eight, next_eight]

            square = [P, GROUP_HEADS, TOPK, TOPK]
            onehot4 = onehot[:, :, :].rearrange("p (h k) a -> p h k a", k=TOPK)
            sv4 = sv[:, :, :].rearrange("p (h s) k -> p h s k", s=2)
            sif4 = sif[:, :, :].rearrange("p (h s) k -> p h s k", s=2)

            def choosing(n):
                t, q = divmod(n, TILE_GROUPS)
                u, part = divmod(q * 2 * GROUP_HEADS, PEER_HEADS)

                def scores_there():
                    is_emptied(dve, f"scores{u}")

                def sums():
                    step(v.tensor_copy(sif[:, :, :], si[:, :, :]))
                    step(v.tensor_tensor(cand[:, :, :].rearrange("p h (a b) -> p h a b", b=TOPK),
                                         sv4[:, :, 0, :].unsqueeze(3).to_broadcast(square),
                                         sv4[:, :, 1, :].unsqueeze(2).to_broadcast(square), ALU.add))

                def exponents():
                    v.tensor_tensor(gate[:, t, q * GROUP_HEADS:(q + 1) * GROUP_HEADS, :], tops[:, :, :],
                                    tops[:, :, 0:1].to_broadcast([P, GROUP_HEADS, TOPK]), ALU.subtract).then_inc(gate_sub, 1)

                a, b = (pick_keys[:, t, half, q * GROUP_PICKS:(q + 1) * GROUP_PICKS] for half in range(2))

                def look_up(half, key, op, x):
                    def job():
                        step(v.tensor_scalar(topa[:, :, :], topj[:, :, :], x, None, op))
                        step(v.tensor_copy(topaf[:, :, :], topa[:, :, :]))
                        step(v.tensor_tensor(onehot4, topaf[:, :, :].unsqueeze(3).to_broadcast(square),
                                             iota16[:, :].unsqueeze(1).unsqueeze(1).to_broadcast(square), ALU.is_equal))
                        step(v.tensor_tensor(onehot4, onehot4, sif4[:, :, half, :].unsqueeze(2).to_broadcast(square),
                                             ALU.mult))
                        step(v.tensor_reduce(key, onehot[:, :, :], AX_X, ALU.add))
                    return job

                def experts():
                    step(v.scalar_tensor_tensor(out=eid[:, n * GROUP_PICKS:(n + 1) * GROUP_PICKS], in0=a,
                                                scalar=float(N_KEYS), in1=b, op0=ALU.mult, op1=ALU.add))

                values = scores[u][:, t, part:part + 2 * GROUP_HEADS, :]
                return ([scores_there] + best16(values, left, sv, si, 2 * GROUP_HEADS) + [sums]
                        + best16(cand, cand_left, tops, topj, GROUP_HEADS)
                        + [exponents, look_up(0, a, ALU.logical_shift_right, 4), look_up(1, b, ALU.bitwise_and, TOPK - 1),
                           experts])

            def choose(n):
                for part in choosing(n):
                    part()

            def finish_gate(n):
                t, q = divmod(n, TILE_GROUPS)
                dve.wait_ge(gate_exp, n + 1)
                cut = gate[:, t, q * GROUP_HEADS:(q + 1) * GROUP_HEADS, :]
                step(v.tensor_reduce(gsum[:, :], cut, AX_X, ALU.add))
                step(v.reciprocal(gsum[:, :], gsum[:, :]))
                step(v.tensor_tensor(cut, cut, gsum[:, :].unsqueeze(2).to_broadcast([P, GROUP_HEADS, TOPK]), ALU.mult))

            def stage(b, first):
                v.tensor_copy(idx[:, b, :], eid[:, bass.ds(first, GATHER_SLOTS)]).then_inc(idx_ready[b], 1)

            BODY = 2 * GATHER_SLOTS

            def gathered(i, m, s):
                dve.wait_ge(row_landed[s], i * (16 * 2) + 16 * (m // GATHER_SLOTS + 1))

            def one_hots(s, m, token):
                dve.wait_ge(scattered, m + 1)
                v.tensor_tensor(onehot_b[:, s, :, :], iota_keys[:, :].unsqueeze(1).to_broadcast([P, SCATTER, N_KEYS]),
                                picksT[:, 1, bass.ds(token, SCATTER)].unsqueeze(2).to_broadcast([P, SCATTER, N_KEYS]),
                                ALU.is_equal)
                for n in range(SCATTER):
                    ins = v.tensor_scalar(onehot_a[:, s, n, :], iota_keys[:, :], picksT[:, 0, bass.ds(token + n, 1)],
                                          picksT[:, 2, bass.ds(token + n, 1)], ALU.is_equal, ALU.mult)
                ins.then_inc(onehot_done, 1)

            def dot_rows(n, batches=0):
                t, q = divmod(n, TILE_GROUPS)
                first = n * GROUP_PICKS
                per = batches // (GROUP_PICKS // BODY)
                with dve.Fori(0, GROUP_PICKS // BODY) as i:
                    for b in range(2):
                        for s in range(GATHER_SLOTS):
                            gathered(i, first + b * GATHER_SLOTS, s)
                            v.tensor_tensor_reduce(out=ring[:, s, :], in0=ring[:, s, :], in1=h[:, t, :], scale=1.0,
                                                   scalar=0.0, op0=ALU.mult, op1=ALU.add,
                                                   accum_out=dots[:, b, s:s + 1]).then_inc(rows_used, 1)
                            done = b * GATHER_SLOTS + s + 1
                            if done * per % BODY == BODY // 2:
                                m = q * batches + done * per // BODY
                                one_hots(m % 2, i * per + m, i * (per * SCATTER) + m * SCATTER)
                        dve.wait_ge(rows_used, i * BODY + (first + (b + 2) * GATHER_SLOTS))
                        v.tensor_copy(wgt[:, bass.ds(i * BODY + (first + b * GATHER_SLOTS), GATHER_SLOTS)], dots[:, b, :])
                        stage(b, i * BODY + (first + (b + 2) * GATHER_SLOTS))

            def weights(t):
                dve.wait_ge(gelu_done, t + 1)
                w = wgt[:, t * PICKS:(t + 1) * PICKS]
                v.tensor_tensor(w, w, gate[:, t, :, :].rearrange("p h k -> p (h k)"), ALU.mult).then_inc(wgt_done, 1)
                dve.wait_ge(wgt_done, t + 1)
                step(v.tensor_scalar(h[:, t, V_DENSE:], h[:, t, V_DENSE:], ALPHA, None, ALU.mult))
                is_emptied(dve, f"wgtT{t}")

            dve.sem_inc(rows_used, GATHER_SLOTS)
            dve.sem_inc(v_used, V_SLOTS)

            def first_indices():
                for b in range(2):
                    stage(b, b * GATHER_SLOTS)

            def keys_of(t):
                v.memset(v_odd[:, :], 0.0).then_inc(keys_known, 1)
                dve.wait_ge(keys_known, t + 1)

            first = choosing(0)
            block_of("peer_q1", at={5: first[0:2], 6: first[2:3], 7: first[3:4], 8: first[4:5], 9: first[5:7],
                                    10: first[7:8], 11: first[8:] + [first_indices]}, last=True)
            ALL = TILES * PICKS
            GROUPS_IN_ALL = TILES * TILE_GROUPS
            for n in range(GROUPS_IN_ALL):
                if n + 1 < GROUPS_IN_ALL:
                    choose(n + 1)
                if n + 2 == TILE_GROUPS:
                    keys_of(0)
                if n + 2 == GROUPS_IN_ALL:
                    step(v.tensor_scalar(eid[:, ALL:2 * ALL], eid[:, 0:ALL], float(V_PARTS), V_PARTS - 1.0, ALU.mult,
                                         ALU.add))
                    step(v.memset(eid[:, 2 * ALL:], 0))
                    keys_of(1)
                finish_gate(n)
                if n == TILE_GROUPS:
                    weights(0)
                    dve.wait_ge(consts_done, 3)
                dot_rows(n, 0 if n < TILE_GROUPS else P // SCATTER // TILE_GROUPS)
            weights(1)

            def weigh(t, i, m):
                dve.wait_ge(v_landed[m % V_SLOTS], i * (16 * BODY // V_SLOTS) + 16 * (m // V_SLOTS + 1))
                dve.wait_ge(v_used, i * BODY + (m - 1 + V_SLOTS))
                acc = v_odd[:, :] if m % 2 else h[:, t, V_DENSE:]
                v.scalar_tensor_tensor(out=acc, in0=v_rows[m % V_SLOTS][:, :], scalar=wgt[:, bass.ds(i * BODY + m, 1)],
                                       in1=acc, op0=ALU.mult, op1=ALU.add).then_inc(v_used, 1)
                if (m + 1) % GATHER_SLOTS == 0:
                    stage(m // GATHER_SLOTS % 2, i * BODY + (ALL + m + 1 + GATHER_SLOTS))

            def fold(t):
                dve.wait_ge(v_used, (t + 1) * PICKS + V_SLOTS)
                step(v.tensor_tensor(h[:, t, V_DENSE:], h[:, t, V_DENSE:], v_odd[:, :], ALU.add))

            def lo_v(c, s):
                dve.wait_ge(w_hi, c + 1)
                v.tensor_tensor(w_x[s][:, 1, :, :, :], wT[:, :, bass.ds(c, 1), :], w_x[s][:, 0, :, :, :].bitcast(F32),
                                ALU.subtract).then_inc(w_lo, 1)
                dve.wait_ge(v_hi, c + 1)
                v.tensor_tensor(v_split[s][:, 1, :], v_raw[s][:, :], v_split[s][:, 0, :].bitcast(F32), ALU.subtract)\
                    .then_inc(v_lo, 1)

            with dve.Fori(0, P // SCATTER // 2) as i:
                for s in range(2):
                    one_hots(s, i * 2 + (P // SCATTER + s), i * (2 * SCATTER) + (P + s * SCATTER))

            def stream_v(t):
                with dve.Fori(0, PICKS // BODY) as i:
                    for n in range(BODY // 2):
                        lo_v(i * (BODY // 2) + (t * (N_KEYS // TILES) + n), n % 2)
                        weigh(t, i, t * PICKS + 2 * n)
                        weigh(t, i, t * PICKS + 2 * n + 1)

            stream_v(0)
            fold(0)
            step(v.memset(v_odd[:, :], 0.0))
            stream_v(1)
            fold(1)

            for t in range(TILES):
                v.bn_stats(bn[:, t, V_BANKS, :], h[:, t, V_DENSE:])
            dve.wait_ge(v_products, N_KEYS)
            for t in range(TILES):
                dst = h[:, t, 0:V_DENSE]
                step(v.scalar_tensor_tensor(out=dst, in0=dst, scalar=ALPHA, in1=flat[t][:, 0:V_DENSE], op0=ALU.mult,
                                            op1=ALU.add))
                for n in range(V_BANKS):
                    ins = v.bn_stats(bn[:, t, n, :], h[:, t, n * BANK:(n + 1) * BANK])
                step(ins)
                step(tile_moments(t))
                v.tensor_scalar(meansq[:, t:t + 1], moments[:, t, 1:2], LN_EPS, None, ALU.add).then_inc(stat, 1)
                step(inverse_root(rstd[:, t:t + 1], slice(t, t + 1)))
                v.scalar_tensor_tensor(out=shift[:, t:t + 1], in0=moments[:, t, 0:1], scalar=-1.0, in1=rstd[:, t:t + 1],
                                       op0=ALU.mult, op1=ALU.mult).then_inc(shift_ready, 1)
            for n in range(2 * TILES):
                t, b = divmod(n, 2)
                cut = h[:, t, b * COLS:(b + 1) * COLS]
                dve.wait_ge(loaded["rows_ln2"], 32)
                dve.wait_ge(normed, n + 1)
                step(v.tensor_tensor(cut, cut, row_g2[:, b * COLS:(b + 1) * COLS], ALU.mult))
                v.tensor_tensor(cut, cut, row_b2[:, b * COLS:(b + 1) * COLS], ALU.add).then_inc(out_ready, 1)


_INS = ["x", "norm_g", "a_w_in", "a_v_norm_g", "a_w_s", "a_b_s", "a_w_out", "b_w_in", "b_w_out", "final_g", "ln_in_g_2",
        "ln_in_b_2", "w_in_2", "b_gate_2", "conv_w_2", "conv_b_2", "mh_norm_g_2", "w_out_2", "ln1_g_2", "ln1_b_2",
        "peer_wq_2", "peer_keys_2", "peer_u_2", "peer_v_2", "ln2_g_2", "ln2_b_2"]


def kernel(**inputs):
    import numpy as np
    import concourse.bacc as bacc
    from concourse.bass_utils import run_bass_kernel_spmd

    nc = bacc.Bacc("TRN2", target_bir_lowering=False, num_devices=1)
    arrays, args = {}, []
    for name in _INS:
        a = np.ascontiguousarray(inputs[name])
        arrays["in_" + name] = a
        args.append(nc.dram_tensor("in_" + name, a.shape, F32, kind="ExternalInput").ap())
    out = nc.dram_tensor("out_h", (1, TOKENS, D), F32, kind="ExternalOutput").ap()
    build(nc, *args, out)
    r = run_bass_kernel_spmd(nc, [arrays], core_ids=[0])
    return r.results[0]["out_h"]
```
